# Optimizing a Trainium2 kernel written in Bass

```python
import math
import jax, jax.numpy as jnp
from jax import lax
import numpy as np

D_MODEL = 1024
BATCH = 1
SEQ = 256
DEPTH = 1

MIX_WIDTH = D_MODEL
SGU_GROUPS = 4
SGU_CH = D_MODEL // 8
SGU_WIDTH = SGU_GROUPS * SGU_CH
CHUNK = 128
DIFF_HEADS = 4
DIFF_QK_DIM = D_MODEL // 16
DIFF_V_DIM = 2 * DIFF_QK_DIM
DIFF_QK_WIDTH = DIFF_HEADS * 2 * DIFF_QK_DIM
DIFF_WIDTH = DIFF_HEADS * DIFF_V_DIM
Q_BLOCK = 128
IN_WIDTH = 2 * SGU_WIDTH + 2 * DIFF_QK_WIDTH + DIFF_WIDTH
MEM_LEN = 256
MEM_HEADS = 4
MEM_HEAD_DIM = D_MODEL // MEM_HEADS
MEM_WIDTH = MEM_HEADS * MEM_HEAD_DIM
N_GROUPS = 4
EXPERTS_PER_GROUP = 8
N_EXPERTS = N_GROUPS * EXPERTS_PER_GROUP
TOP_K = 2
D_EXPERT = D_MODEL // 2
EXPERT_BLOCK = 128
RMS_EPS = 1e-6
LN_EPS = 1e-5


def rms_norm(x, g, eps=RMS_EPS):
    xf = x.astype(jnp.float32)
    y = xf * lax.rsqrt(jnp.mean(xf * xf, axis=-1, keepdims=True) + eps)
    return (y * g.astype(jnp.float32)).astype(x.dtype)

def layer_norm(x, g, b, eps=LN_EPS):
    xf = x.astype(jnp.float32)
    mu = jnp.mean(xf, axis=-1, keepdims=True)
    var = jnp.mean(jnp.square(xf - mu), axis=-1, keepdims=True)
    y = (xf - mu) * lax.rsqrt(var + eps)
    return (y * g.astype(jnp.float32) + b.astype(jnp.float32)).astype(x.dtype)

def chunked_sgu(u, v, ln_g, ln_b, w_s, b_s):
    Bn, Sn, G, C = v.shape
    vn = layer_norm(v, ln_g, ln_b)
    vc = vn.reshape(Bn, Sn // CHUNK, CHUNK, G, C)
    ws = jnp.tril(w_s).astype(vc.dtype)
    sp = jnp.einsum('gts,bnsgc->bntgc', ws, vc) + b_s.T.astype(vc.dtype)[:, :, None]
    return u * sp.reshape(Bn, Sn, G, C)

def diff_attention(q, k, v, lam):
    Bn, H, _, Sn, Dq = q.shape
    n_qb = Sn // Q_BLOCK
    slopes = 2.0 ** (-8.0 * jnp.arange(1, H + 1, dtype=jnp.float32) / H)
    q_blocks = jnp.moveaxis(q.reshape(Bn, H, 2, n_qb, Q_BLOCK, Dq), 3, 0)
    kpos = jnp.arange(Sn, dtype=jnp.int32)

    def attend(args):
        qb, i = args
        s = jnp.einsum('bhiqd,bhikd->bhiqk', qb, k).astype(jnp.float32)
        qpos = i * Q_BLOCK + jnp.arange(Q_BLOCK, dtype=jnp.int32)
        dist = (qpos[:, None] - kpos[None, :]).astype(jnp.float32)
        s = s - (slopes[:, None, None] * dist)[None, :, None]
        s = jnp.where(dist >= 0, s, -jnp.inf)
        p = jax.nn.softmax(s, axis=-1)
        a = p[:, :, 0] - lam * p[:, :, 1]
        return jnp.einsum('bhqk,bhkd->bqhd', a.astype(v.dtype), v)

    o = lax.map(attend, (q_blocks, jnp.arange(n_qb, dtype=jnp.int32)))
    return jnp.moveaxis(o, 0, 1).reshape(Bn, Sn, H, v.shape[-1])

def memory_attention(hq, mem_n, w_q, w_kv, w_o):
    Bn, Sn, _ = hq.shape
    Mn = mem_n.shape[1]
    q = (hq @ w_q).reshape(Bn, Sn, MEM_HEADS, MEM_HEAD_DIM) * (MEM_HEAD_DIM ** -0.5)
    kv = (mem_n @ w_kv).reshape(Bn, Mn, 2, MEM_HEADS, MEM_HEAD_DIM)
    k, v = kv[:, :, 0], kv[:, :, 1]
    s = jnp.einsum('bqhd,bkhd->bhqk', q, k).astype(jnp.float32)
    p = jax.nn.softmax(s, axis=-1)
    o = jnp.einsum('bhqk,bkhd->bqhd', p.astype(v.dtype), v).reshape(Bn, Sn, MEM_WIDTH)
    return o @ w_o

def hierarchical_moe(h, w_rg, b_rg, w_re, b_re, w_gate, w_up, w_down):
    Bn, Sn, D = h.shape
    t = h.reshape(-1, D)
    N = t.shape[0]
    pg = jax.nn.softmax((t @ w_rg + b_rg).astype(jnp.float32), axis=-1)
    gate_g, gidx = lax.top_k(pg, 1)
    el = (t @ w_re + b_re).astype(jnp.float32).reshape(N, N_GROUPS, EXPERTS_PER_GROUP)
    el = el[jnp.arange(N), gidx[:, 0]]
    pe = jax.nn.softmax(el, axis=-1)
    pe_top, eloc = lax.top_k(pe, TOP_K)
    wts = gate_g * pe_top / jnp.sum(pe_top, axis=-1, keepdims=True)
    eid = (gidx * EXPERTS_PER_GROUP + eloc).reshape(-1)
    A = N * TOP_K
    tok = jnp.repeat(jnp.arange(N, dtype=jnp.int32), TOP_K)
    order = jnp.argsort(eid)
    e_sorted = eid[order]
    counts = jnp.bincount(eid, length=N_EXPERTS)
    starts = jnp.cumsum(counts) - counts
    padded = (counts + EXPERT_BLOCK - 1) // EXPERT_BLOCK * EXPERT_BLOCK
    pend = jnp.cumsum(padded)
    pstarts = pend - padded
    pos_sorted = (pstarts[e_sorted] + jnp.arange(A, dtype=jnp.int32) - starts[e_sorted]).astype(jnp.int32)
    P = -(-A // EXPERT_BLOCK) * EXPERT_BLOCK + N_EXPERTS * EXPERT_BLOCK
    n_blocks = P // EXPERT_BLOCK
    row_tok = jnp.zeros((P,), jnp.int32).at[pos_sorted].set(tok[order])
    block_expert = jnp.clip(jnp.searchsorted(pend, jnp.arange(n_blocks, dtype=jnp.int32) * EXPERT_BLOCK,
                                             side='right'), 0, N_EXPERTS - 1).astype(jnp.int32)
    x_rows = t[row_tok].reshape(n_blocks, EXPERT_BLOCK, D)

    def expert_rows(args):
        xb, e = args
        g = xb @ w_gate[e]
        u = xb @ w_up[e]
        return (jax.nn.silu(g) * u) @ w_down[e]

    y_rows = lax.map(expert_rows, (x_rows, block_expert)).reshape(P, D)
    pos = jnp.zeros((A,), jnp.int32).at[order].set(pos_sorted)
    y = y_rows[pos].reshape(N, TOP_K, D)
    out = jnp.einsum('nk,nkd->nd', wts.astype(y.dtype), y)
    return out.reshape(Bn, Sn, D)

def first_inputs(seed: int = 0) -> dict:
    key = jax.random.key(seed)
    ks = jax.random.split(key, 32)
    L, D = DEPTH, D_MODEL
    f32 = jnp.float32

    def nrm(k, shape, scale):
        return jax.random.normal(k, shape, f32) * scale

    def gain(k, shape):
        return 1.0 + 0.05 * jax.random.normal(k, shape, f32)

    return {
        "x": jax.random.normal(ks[0], (BATCH, SEQ, D), f32),
        "mem": jax.random.normal(ks[1], (BATCH, MEM_LEN, D), f32),
        "norm_mix": gain(ks[2], (L, D)),
        "w_in": nrm(ks[3], (L, D, IN_WIDTH), D ** -0.5),
        "sgu_ln_g": gain(ks[4], (L, SGU_GROUPS, SGU_CH)),
        "sgu_ln_b": nrm(ks[5], (L, SGU_GROUPS, SGU_CH), 0.02),
        "sgu_w": nrm(ks[6], (L, SGU_GROUPS, CHUNK, CHUNK), CHUNK ** -0.5),
        "sgu_b": gain(ks[7], (L, SGU_GROUPS, CHUNK)),
        "lambda_q1": nrm(ks[8], (L, DIFF_QK_DIM), 0.1),
        "lambda_k1": nrm(ks[9], (L, DIFF_QK_DIM), 0.1),
        "lambda_q2": nrm(ks[10], (L, DIFF_QK_DIM), 0.1),
        "lambda_k2": nrm(ks[11], (L, DIFF_QK_DIM), 0.1),
        "diff_subln": gain(ks[12], (L, DIFF_V_DIM)),
        "w_out": nrm(ks[13], (L, MIX_WIDTH, D), MIX_WIDTH ** -0.5),
        "norm_xq": gain(ks[14], (L, D)),
        "norm_mem": gain(ks[15], (L, D)),
        "w_q_mem": nrm(ks[16], (L, D, MEM_WIDTH), D ** -0.5),
        "w_kv_mem": nrm(ks[17], (L, D, 2 * MEM_WIDTH), D ** -0.5),
        "w_o_mem": nrm(ks[18], (L, MEM_WIDTH, D), MEM_WIDTH ** -0.5),
        "norm_ffn": gain(ks[19], (L, D)),
        "w_router_group": nrm(ks[20], (L, D, N_GROUPS), D ** -0.5),
        "b_router_group": nrm(ks[21], (L, N_GROUPS), 0.01),
        "w_router_expert": nrm(ks[22], (L, D, N_EXPERTS), D ** -0.5),
        "b_router_expert": nrm(ks[23], (L, N_EXPERTS), 0.01),
        "w_gate": nrm(ks[24], (L, N_EXPERTS, D, D_EXPERT), D ** -0.5),
        "w_up": nrm(ks[25], (L, N_EXPERTS, D, D_EXPERT), D ** -0.5),
        "w_down": nrm(ks[26], (L, N_EXPERTS, D_EXPERT, D), D_EXPERT ** -0.5),
        "norm_final": gain(ks[27], (D,)),
    }

def first_block(x, mem, norm_mix, w_in, sgu_ln_g, sgu_ln_b, sgu_w, sgu_b, lambda_q1, lambda_k1, lambda_q2,
              lambda_k2, diff_subln, w_out, norm_xq, norm_mem, w_q_mem, w_kv_mem, w_o_mem, norm_ffn,
              w_router_group, b_router_group, w_router_expert, b_router_expert, w_gate, w_up, w_down,
              norm_final):
    Bn, Sn, _ = x.shape
    cuts = [SGU_WIDTH, 2 * SGU_WIDTH, 2 * SGU_WIDTH + DIFF_QK_WIDTH, 2 * SGU_WIDTH + 2 * DIFF_QK_WIDTH]
    for l in range(DEPTH):
        lambda_init = 0.8 - 0.6 * math.exp(-0.3 * l)
        h = rms_norm(x, norm_mix[l])
        z = h @ w_in[l]
        zu, zv, zq, zk, zval = jnp.split(z, cuts, axis=-1)
        u = jax.nn.gelu(zu, approximate=False).reshape(Bn, Sn, SGU_GROUPS, SGU_CH)
        v = jax.nn.gelu(zv, approximate=False).reshape(Bn, Sn, SGU_GROUPS, SGU_CH)
        a_out = chunked_sgu(u, v, sgu_ln_g[l], sgu_ln_b[l], sgu_w[l], sgu_b[l]).reshape(Bn, Sn, SGU_WIDTH)
        q = zq.reshape(Bn, Sn, DIFF_HEADS, 2, DIFF_QK_DIM).transpose(0, 2, 3, 1, 4) * (DIFF_QK_DIM ** -0.5)
        k = zk.reshape(Bn, Sn, DIFF_HEADS, 2, DIFF_QK_DIM).transpose(0, 2, 3, 1, 4)
        vv = zval.reshape(Bn, Sn, DIFF_HEADS, DIFF_V_DIM).transpose(0, 2, 1, 3)
        lam = (jnp.exp(jnp.sum(lambda_q1[l].astype(jnp.float32) * lambda_k1[l].astype(jnp.float32)))
               - jnp.exp(jnp.sum(lambda_q2[l].astype(jnp.float32) * lambda_k2[l].astype(jnp.float32)))
               + lambda_init)
        o = diff_attention(q, k, vv, lam)
        o = rms_norm(o, diff_subln[l]) * (1.0 - lambda_init)
        mixed = jnp.concatenate([a_out, o.reshape(Bn, Sn, DIFF_WIDTH)], axis=-1) @ w_out[l]
        x = x + mixed
        x = x + memory_attention(rms_norm(x, norm_xq[l]), rms_norm(mem, norm_mem[l]),
                                 w_q_mem[l], w_kv_mem[l], w_o_mem[l])
        x = x + hierarchical_moe(rms_norm(x, norm_ffn[l]), w_router_group[l], b_router_group[l],
                                 w_router_expert[l], b_router_expert[l], w_gate[l], w_up[l], w_down[l])
    return rms_norm(x, norm_final)


N_MIXERS = 2
ATT_HEADS = 8
ATT_HEAD_DIM = D_MODEL // ATT_HEADS
MOBA_BLOCK = 256
MOBA_TOPK = 3
MOBA_QUERY_CHUNK = 32
MLSTM_HEADS = 8
MLSTM_DV = D_MODEL // MLSTM_HEADS
MLSTM_DQK = MLSTM_DV // 2
MLSTM_CHUNK = 64
GATE_SOFTCAP = 15.0
D_FF = 4 * D_MODEL
N_ATTN_LAYERS = (DEPTH + N_MIXERS - 1) // N_MIXERS
N_MLSTM_LAYERS = DEPTH // N_MIXERS


def rms_norm_2(x, gain):
    xf = x.astype(jnp.float32)
    y = xf * lax.rsqrt(jnp.mean(xf * xf, axis=-1, keepdims=True) + RMS_EPS)
    return (y * gain.astype(jnp.float32)).astype(x.dtype)

def alibi_slopes(n_heads):
    return jnp.exp2(-8.0 * jnp.arange(1, n_heads + 1, dtype=jnp.float32) / n_heads)

def soft_cap(z):
    return GATE_SOFTCAP * jnp.tanh(z / GATE_SOFTCAP)

def moba_attention(x, w_qkv, w_o):
    bsz, seq, _ = x.shape
    H, dh, blk, qlen = ATT_HEADS, ATT_HEAD_DIM, MOBA_BLOCK, MOBA_QUERY_CHUNK
    f32 = jnp.float32
    q, k, v = jnp.split(x @ w_qkv, 3, axis=-1)

    def to_heads(t):
        return t.reshape(bsz, seq, H, dh).transpose(0, 2, 1, 3)

    q = to_heads(q) * (dh ** -0.5)
    k = to_heads(k)
    v = to_heads(v)
    n_blk = -(-seq // blk)
    pad = n_blk * blk - seq
    k_blk = jnp.pad(k, ((0, 0), (0, 0), (0, pad), (0, 0))).reshape(bsz, H, n_blk, blk, dh)
    v_blk = jnp.pad(v, ((0, 0), (0, 0), (0, pad), (0, 0))).reshape(bsz, H, n_blk, blk, dh)

    k_mean = jnp.mean(k_blk.astype(f32), axis=3)
    gate = jnp.einsum('bhsd,bhnd->bhsn', q.astype(f32), k_mean)
    n_past = jnp.arange(seq) // blk
    is_past = jnp.arange(n_blk)[None, :] < n_past[:, None]
    gate = jnp.where(is_past, gate, -jnp.inf)
    top = min(MOBA_TOPK, n_blk)
    _, sel = lax.top_k(gate, top)
    sel = sel.astype(jnp.int32)

    n_chunk = seq // qlen
    q_c = jnp.moveaxis(q.reshape(bsz, H, n_chunk, qlen, dh), 2, 0)
    sel_c = jnp.moveaxis(sel.reshape(bsz, H, n_chunk, qlen, top), 2, 0)
    slopes = alibi_slopes(H)
    b_idx = jnp.arange(bsz)[:, None, None, None]
    h_idx = jnp.arange(H)[None, :, None, None]
    offs = jnp.arange(blk)

    def attend_chunk(args):
        c, q_blk, sel_blk = args
        t = c * qlen + jnp.arange(qlen)
        own = (c * qlen) // blk
        k_own = lax.dynamic_index_in_dim(k_blk, own, axis=2, keepdims=False)
        v_own = lax.dynamic_index_in_dim(v_blk, own, axis=2, keepdims=False)
        dist_own = (t[:, None] - (own * blk + offs)[None, :]).astype(f32)
        s_own = jnp.einsum('bhqd,bhkd->bhqk', q_blk, k_own).astype(f32) - slopes[:, None, None] * dist_own
        s_own = jnp.where(dist_own >= 0, s_own, -jnp.inf)
        k_sel = k_blk[b_idx, h_idx, sel_blk]
        v_sel = v_blk[b_idx, h_idx, sel_blk]
        dist_sel = (t[:, None, None] - (sel_blk[..., None] * blk + offs)).astype(f32)
        s_sel = jnp.einsum('bhqd,bhqjkd->bhqjk', q_blk, k_sel).astype(f32) - slopes[:, None, None, None] * dist_sel
        slot_ok = jnp.arange(top)[None, :] < (t // blk)[:, None]
        s_sel = jnp.where(slot_ok[:, :, None], s_sel, -jnp.inf)
        scores = jnp.concatenate([s_own, s_sel.reshape(bsz, H, qlen, top * blk)], axis=-1)
        p = jax.nn.softmax(scores, axis=-1).astype(v_blk.dtype)
        p_own = p[..., :blk]
        p_sel = p[..., blk:].reshape(bsz, H, qlen, top, blk)
        return (jnp.einsum('bhqk,bhkd->bhqd', p_own, v_own)
                + jnp.einsum('bhqjk,bhqjkd->bhqd', p_sel, v_sel))

    o = lax.map(attend_chunk, (jnp.arange(n_chunk), q_c, sel_c))
    o = o.transpose(1, 0, 3, 2, 4).reshape(bsz, seq, H * dh)
    return o @ w_o

def mlstm_chunkwise(q, k, v, log_i, log_f):
    bsz, H, seq, dqk = q.shape
    dv = v.shape[-1]
    L = MLSTM_CHUNK
    n_chunk = seq // L

    def chunks(t):
        return jnp.moveaxis(t.reshape(bsz, H, n_chunk, L, *t.shape[3:]), 2, 0)

    causal = jnp.tril(jnp.ones((L, L), dtype=bool))

    def step(carry, inp):
        C, n, m = carry
        qc, kc, vc, ic, fc = inp
        b = jnp.cumsum(fc, axis=-1)
        log_d = jnp.where(causal, b[..., :, None] - b[..., None, :] + ic[..., None, :], -jnp.inf)
        log_inter = b + m[..., None]
        m_t = jnp.maximum(log_inter, jnp.max(log_d, axis=-1))
        d = jnp.exp(log_d - m_t[..., None])
        w_inter = jnp.exp(log_inter - m_t)
        s = jnp.einsum('bhtd,bhsd->bhts', qc, kc) * d
        num = (w_inter[..., None] * jnp.einsum('bhtd,bhdv->bhtv', qc, C)
               + jnp.einsum('bhts,bhsv->bhtv', s, vc))
        den = w_inter * jnp.einsum('bhtd,bhd->bht', qc, n) + jnp.sum(s, axis=-1)
        h = num / jnp.maximum(jnp.abs(den), jnp.exp(-m_t))[..., None]
        b_end = b[..., -1]
        log_w = b_end[..., None] - b + ic
        m_new = jnp.maximum(b_end + m, jnp.max(log_w, axis=-1))
        decay = jnp.exp(b_end + m - m_new)
        w = jnp.exp(log_w - m_new[..., None])
        C = decay[..., None, None] * C + jnp.einsum('bhs,bhsd,bhsv->bhdv', w, kc, vc)
        n = decay[..., None] * n + jnp.einsum('bhs,bhsd->bhd', w, kc)
        return (C, n, m_new), h

    f32 = jnp.float32
    init = (jnp.zeros((bsz, H, dqk, dv), f32), jnp.zeros((bsz, H, dqk), f32), jnp.zeros((bsz, H), f32))
    _, h = lax.scan(step, init, (chunks(q), chunks(k), chunks(v), chunks(log_i), chunks(log_f)))
    return jnp.moveaxis(h, 0, 2).reshape(bsz, H, seq, dv)

def mlstm_mixer(x, w_in, b_gates, norm_h, w_out):
    bsz, seq, _ = x.shape
    H, dqk, dv = MLSTM_HEADS, MLSTM_DQK, MLSTM_DV
    f32 = jnp.float32
    proj = x @ w_in
    q, k, v, o_pre, gate_pre = jnp.split(
        proj, [H * dqk, 2 * H * dqk, 2 * H * dqk + H * dv, 2 * H * dqk + 2 * H * dv], axis=-1)

    def to_heads(t, dim):
        return t.reshape(bsz, seq, H, dim).transpose(0, 2, 1, 3).astype(f32)

    q = to_heads(q, dqk)
    k = to_heads(k, dqk) * (dqk ** -0.5)
    v = to_heads(v, dv)
    gates = soft_cap(gate_pre.astype(f32) + b_gates.astype(f32)).transpose(0, 2, 1)
    log_i = gates[:, :H]
    log_f = jax.nn.log_sigmoid(gates[:, H:])
    h = mlstm_chunkwise(q, k, v, log_i, log_f)
    h = h * lax.rsqrt(jnp.mean(h * h, axis=-1, keepdims=True) + RMS_EPS)
    h = h.transpose(0, 2, 1, 3).reshape(bsz, seq, H * dv) * norm_h.astype(f32)
    y = (jax.nn.sigmoid(o_pre.astype(f32)) * h).astype(x.dtype)
    return y @ w_out

def squared_relu_mlp(x, w_up, w_down):
    return jnp.square(jax.nn.relu(x @ w_up)) @ w_down

def second_inputs(seed: int = 0) -> dict:
    key = jax.random.key(seed)
    ks = jax.random.split(key, 16)
    f32 = jnp.float32

    def dense(k, shape):
        return jax.random.normal(k, shape, f32) * shape[-2] ** -0.5

    def gain(k, shape):
        return 1.0 + 0.05 * jax.random.normal(k, shape, f32)

    H = MLSTM_HEADS
    mlstm_in = 2 * H * MLSTM_DQK + 2 * H * MLSTM_DV + 2 * H
    i_bias = 0.1 * jax.random.normal(ks[13], (N_MLSTM_LAYERS, H), f32)
    f_bias = 3.0 + 0.5 * jax.random.normal(ks[14], (N_MLSTM_LAYERS, H), f32)
    return {
        "x": jax.random.normal(ks[0], (BATCH, SEQ, D_MODEL), f32),
        "norm_mix_pre": gain(ks[1], (DEPTH, D_MODEL)),
        "norm_mix_post": gain(ks[2], (DEPTH, D_MODEL)),
        "norm_ffn_pre": gain(ks[3], (DEPTH, D_MODEL)),
        "norm_ffn_post": gain(ks[4], (DEPTH, D_MODEL)),
        "w_up": dense(ks[5], (DEPTH, D_MODEL, D_FF)),
        "w_down": dense(ks[6], (DEPTH, D_FF, D_MODEL)),
        "attn_w_qkv": dense(ks[7], (N_ATTN_LAYERS, D_MODEL, 3 * ATT_HEADS * ATT_HEAD_DIM)),
        "attn_w_o": dense(ks[8], (N_ATTN_LAYERS, ATT_HEADS * ATT_HEAD_DIM, D_MODEL)),
        "mlstm_w_in": dense(ks[9], (N_MLSTM_LAYERS, D_MODEL, mlstm_in)),
        "mlstm_b_gates": jnp.concatenate([i_bias, f_bias], axis=-1),
        "mlstm_norm_h": gain(ks[10], (N_MLSTM_LAYERS, H * MLSTM_DV)),
        "mlstm_w_out": dense(ks[11], (N_MLSTM_LAYERS, H * MLSTM_DV, D_MODEL)),
    }

def second_block(x, norm_mix_pre, norm_mix_post, norm_ffn_pre, norm_ffn_post, w_up, w_down,
              attn_w_qkv, attn_w_o, mlstm_w_in, mlstm_b_gates, mlstm_norm_h, mlstm_w_out):
    h = x
    for layer in range(DEPTH):
        j = layer // N_MIXERS
        u = rms_norm_2(h, norm_mix_pre[layer])
        if layer % N_MIXERS == 0:
            u = moba_attention(u, attn_w_qkv[j], attn_w_o[j])
        else:
            u = mlstm_mixer(u, mlstm_w_in[j], mlstm_b_gates[j], mlstm_norm_h[j], mlstm_w_out[j])
        h = h + rms_norm_2(u, norm_mix_post[layer])
        u = squared_relu_mlp(rms_norm_2(h, norm_ffn_pre[layer]), w_up[layer], w_down[layer])
        h = h + rms_norm_2(u, norm_ffn_post[layer])
    return h


def setup_inputs(seed=0):
    out = dict(first_inputs(seed))
    for name, value in second_inputs(seed + 1).items():
        if name != "x":
            out[name + "_2"] = value
    return out


def reference(
    x, mem, norm_mix, w_in, sgu_ln_g, sgu_ln_b, sgu_w, sgu_b, lambda_q1, lambda_k1, lambda_q2,
    lambda_k2, diff_subln, w_out, norm_xq, norm_mem, w_q_mem, w_kv_mem, w_o_mem, norm_ffn,
    w_router_group, b_router_group, w_router_expert, b_router_expert, w_gate, w_up, w_down,
    norm_final, norm_mix_pre_2, norm_mix_post_2, norm_ffn_pre_2, norm_ffn_post_2, w_up_2,
    w_down_2, attn_w_qkv_2, attn_w_o_2, mlstm_w_in_2, mlstm_b_gates_2, mlstm_norm_h_2,
    mlstm_w_out_2,
):
    x = first_block(
        x, mem, norm_mix, w_in, sgu_ln_g, sgu_ln_b, sgu_w, sgu_b, lambda_q1, lambda_k1,
        lambda_q2, lambda_k2, diff_subln, w_out, norm_xq, norm_mem, w_q_mem, w_kv_mem, w_o_mem,
        norm_ffn, w_router_group, b_router_group, w_router_expert, b_router_expert, w_gate,
        w_up, w_down, norm_final,
    )
    return second_block(
        x, norm_mix_pre_2, norm_mix_post_2, norm_ffn_pre_2, norm_ffn_post_2, w_up_2, w_down_2,
        attn_w_qkv_2, attn_w_o_2, mlstm_w_in_2, mlstm_b_gates_2, mlstm_norm_h_2, mlstm_w_out_2,
    )


_drawn_inputs = setup_inputs


def setup_inputs(seed=0):
    import zlib

    import numpy as np

    out = dict(_drawn_inputs(seed))
    spreads = {}
    factors = {'sgu_ln_b': 3.914,
     'lambda_k1': 4.558,
     'lambda_q2': 4.616,
     'norm_xq': 2.844,
     'norm_mem': 3.618,
     'b_router_group': 50.016,
     'b_router_expert': 30.916,
     'norm_ffn': 3.055}
    for name, (base, spread) in spreads.items():
        noise = np.random.default_rng([zlib.crc32(name.encode()), seed]).standard_normal(out[name].shape)
        drawn = base * np.exp(spread * noise) if base else spread * noise
        out[name] = __import__('jax').numpy.asarray(drawn.astype(out[name].dtype))
    for name, factor in factors.items():
        out[name] = (out[name] * factor).astype(out[name].dtype)
    return out
```

```python
import math

import concourse.bass as bass
from concourse import mybir

F32 = mybir.dt.float32
I32 = mybir.dt.int32
ALU = mybir.AluOpType
ACT = mybir.ActivationFunctionType
AX = mybir.AxisListType.X

P = 128
PIECE = 4096
RING = 9
SLOTS = 64
NEG = -1.0e30
RMS_EPS = 1e-6
LN_EPS = 1e-5


class Steps:

    def __init__(self, nc, name):
        self.sem = nc.alloc_semaphore(name)
        self.count = 0

    def __call__(self, instruction):
        self.count += 1
        instruction.then_inc(self.sem, 1)
        return (self.sem, self.count)


class Handoffs:

    AHEAD = 3

    def __init__(self, nc, prefix):
        names = ("built", "gathered", "rows", "turned", "xT", "routeT", "gate_up", "silu", "hidden",
                 "hidden_turned", "hiddenT", "down", "y", "scattered")
        self.sems = {name: nc.alloc_semaphore(prefix + name) for name in names}
        for name in names:
            nc.gpsimd.sem_inc(self.sems[name], self.AHEAD)

    def wait(self, engine, name, experts):
        engine.wait_ge(self.sems[name], experts + self.AHEAD)

    def passed(self, name, instruction):
        instruction.then_inc(self.sems[name], 1)


def build_program(nc, a, out):
    _, S, D = a["x"].shape
    NH = S // P
    KC = D // P
    M = a["mem"].shape[1]
    GROUPS, CHUNK = a["sgu_b"].shape[1:]
    SGU = GROUPS * P
    DQK = a["lambda_q1"].shape[1]
    DH = 4
    MH = 4
    MHD = D // MH
    NG = a["w_router_group"].shape[2]
    NE = a["w_router_expert"].shape[2]
    EPG = NE // NG
    DE = a["w_gate"].shape[3]
    H2 = 8
    DFF = a["w_up_2"].shape[2]
    LAMBDA_INIT = 0.8 - 0.6 * math.exp(-0.3 * 0)
    assert (S, D, M, CHUNK, DE, KC, NH) == (256, 1024, 256, 128, 512, 8, 2)
    HALF = KC // 2
    JT = P // SLOTS
    assert JT in (2, 4)

    PE, DVE, SC, POOL, SP = nc.tensor, nc.vector, nc.scalar, nc.gpsimd, nc.sync
    pe, dve, act, pool = Steps(nc, "pe_steps"), Steps(nc, "dve_steps"), Steps(nc, "act_steps"), Steps(nc, "pool_steps")
    waited = {}

    def wait(engine, *steps):
        for s in steps:
            if s is None:
                continue
            sem, value = s
            key = (id(engine), id(sem))
            if waited.get(key, 0) < value:
                engine.wait_ge(sem, value)
                waited[key] = value

    ring = nc.alloc_sbuf_tensor("ring", [P, RING * PIECE], F32)
    arena = [nc.alloc_sbuf_tensor(f"arena{i}", [P, 2048], F32) for i in range(7)]
    bc = nc.alloc_sbuf_tensor("gain_rows", [P, 1024], F32)
    ident = nc.alloc_sbuf_tensor("ident", [P, P], F32)
    ones = nc.alloc_sbuf_tensor("ones", [P, P], F32)
    alibi = nc.alloc_sbuf_tensor("alibi", [P, S], F32)
    iota = nc.alloc_sbuf_tensor("iota", [P, P], F32)
    gains = nc.alloc_sbuf_tensor("gains", [P, 6, KC], F32)
    small = nc.alloc_sbuf_tensor("small", [P, 128], F32)
    pos = nc.alloc_sbuf_tensor("pos", [P, NH, NE + 1], F32)
    wts = nc.alloc_sbuf_tensor("wts", [P, NH, NE + 1], F32)
    spill_flag = nc.alloc_sbuf_tensor("spill_flag", [1, 1], I32)
    banks = [nc.alloc_psum_tensor(f"bank{i}", [P, 512], F32) for i in range(8)]
    bank_free = [None] * 8

    def tok(t):
        return t[:, :].rearrange("p (h n) -> p h n", h=NH)

    def chunks(t):
        return t[:, :].rearrange("p (c t) -> p c t", t=S)

    X, XN, XT = tok(arena[0]), tok(arena[1]), chunks(arena[2])

    slot_sem = [nc.alloc_semaphore(f"slot{i}") for i in range(RING)]
    released = []

    def slot(p):
        s = p % RING
        return ring[:, s * PIECE:(s + 1) * PIECE]

    def landed(p):
        return (slot_sem[p % RING], 16 * (p // RING + 1))

    def cols(w, lo, n=512):
        return w.rearrange("(p c) n -> p c n", c=KC)[:, :, lo:lo + n]

    def natural(w, lo, n=512):
        return w.rearrange("(c p) n -> p c n", p=P)[:, :, lo:lo + n]

    w_in, w_out = a["w_in"][0], a["w_out"][0]
    w_kv, w_q, w_om = a["w_kv_mem"][0], a["w_q_mem"][0], a["w_o_mem"][0]
    Z_V, Z_U, Z_Q, Z_K, Z_VAL = range(5)
    first = [cols(w_in, SGU), cols(w_in, 0), cols(w_in, 2 * SGU), cols(w_in, 2 * SGU + 512), cols(w_in, 2 * SGU + 1024),
             natural(w_out, 0), natural(w_out, 512),
             cols(w_kv, 0), cols(w_kv, 512), cols(w_kv, 1024), cols(w_kv, 1536),
             cols(w_q, 0), cols(w_q, 512), natural(w_om, 0), natural(w_om, 512)]
    P_OUT, P_KV, P_QM, P_OM = 5, 7, 11, 13
    NFIRST = len(first)
    w_qkv, w_o2, w_up2, w_down2 = a["attn_w_qkv_2"][0], a["attn_w_o_2"][0], a["w_up_2"][0], a["w_down_2"][0]
    second = ([cols(w_qkv, 512 * i) for i in range(6)] + [natural(w_o2, 0), natural(w_o2, 512)]
              + [cols(w_up2, 512 * i) for i in range(DFF // 512)]
              + [w_down2.rearrange("(c p) n -> p c n", p=P)[:, 4 * i:4 * i + 4, :] for i in range(DFF // 512)])
    P_SECOND = NFIRST + 3 * NE
    P_QKV, P_O2, P_UP, P_DOWN = P_SECOND, P_SECOND + 6, P_SECOND + 8, P_SECOND + 8 + DFF // 512

    def load_piece(p, src):
        n = src.shape[2]
        SP.dma_start(slot(p).rearrange("p (c n) -> p c n", n=n), src).then_inc(slot_sem[p % RING], 16)

    def W8(p):
        return slot(p).rearrange("p (c n) -> p c n", c=KC)

    loads = {}

    def load(name, dst, src, engine=SC):
        if name not in loads:
            loads[name] = [nc.alloc_semaphore("load_" + name), 0]
        loads[name][1] += 16
        engine.dma_start(dst, src).then_inc(loads[name][0], 16)
        return (loads[name][0], loads[name][1])

    x_in = load("x", X, a["x"][0].rearrange("(h p) d -> p h d", p=P))
    G_MIX, G_XQ, G_MEM, G_FFN, G_PRE2, G_FFN2 = range(6)
    for i, name in enumerate(("norm_mix", "norm_xq", "norm_mem", "norm_ffn", "norm_mix_pre_2", "norm_ffn_pre_2")):
        gains_in = load("gains", gains[:, i, :], a[name][0].rearrange("(p c) -> p c", c=KC))
    for p in range(RING):
        load_piece(p, first[p])
    vv = arena[5][:, 0:1024].rearrange("p (h n) -> p h n", h=NH)
    sgu_raw = arena[6][:, 0:512].rearrange("p (g s) -> p g s", g=GROUPS)
    sgu_wT = arena[5][:, 1024:1536].rearrange("p (g t) -> p g t", g=GROUPS)
    sgu_in = load("sgu", sgu_raw, a["sgu_w"][0].rearrange("g t s -> t g s"))
    sgu_in = load("sgu", bc[:, 0:512], a["sgu_ln_g"].rearrange("l g c -> l (g c)").partition_broadcast(P)
                  .rearrange("q l n -> q (l n)"))
    sgu_in = load("sgu", bc[:, 512:1024], a["sgu_ln_b"].rearrange("l g c -> l (g c)").partition_broadcast(P)
                  .rearrange("q l n -> q (l n)"))
    sgu_bias = arena[6][0:1, 512:1024]
    sgu_in = load("sgu", sgu_bias, a["sgu_b"].rearrange("l g c -> l (g c)"))
    lam_rows = arena[6][:, 1024:1024 + 4 * DQK].rearrange("p (i n) -> p i n", i=4)
    for i, name in enumerate(("lambda_q1", "lambda_k1", "lambda_q2", "lambda_k2")):
        lam_in = load("lambda", lam_rows[:, i, :], a[name].partition_broadcast(P).rearrange("q l n -> q (l n)"))
    subln = small[:, 0:1]
    lam_in = load("lambda", subln, a["diff_subln"].rearrange("l (p o) -> p (l o)", o=1))

    minus_half = small[:, 8:16]
    pool_const = pool(POOL.memset(ident[:, :], 0.0))
    pool(POOL.memset(ones[:, :], 1.0))
    pool(POOL.memset(minus_half, -0.5))
    wait(POOL, pool_const)
    ident_ready = pool(POOL.affine_select(out=ident[:, :], in_=ident[:, :], compare_op=ALU.not_equal, fill=1.0,
                                          base=0, pattern=[[-1, P]], channel_multiplier=1))
    al0 = pool(POOL.iota(alibi[:, :], pattern=[[1, S]], base=-P, channel_multiplier=-1,
                         allow_small_or_imprecise_dtypes=True))
    wait(POOL, al0)
    alibi_ready = pool(POOL.affine_select(out=alibi[:, :], in_=alibi[:, :], compare_op=ALU.is_ge, fill=NEG,
                                          base=P, pattern=[[-1, S]], channel_multiplier=1))
    iota_ready = pool(POOL.iota(iota[:, :].rearrange("p (j s) -> p j s", j=JT), pattern=[[0, JT], [1, SLOTS]], base=0,
                                channel_multiplier=0, allow_small_or_imprecise_dtypes=True))

    turn = [0]

    def next_bank(limit=8):
        b = turn[0] % limit
        turn[0] += 1
        wait(PE, bank_free[b])
        return b

    def rms_scale(src, n, squares, col, *ready):
        sums = small[:, col:col + NH]
        wait(SC, *ready)
        wait(DVE, *ready)
        q0 = act(SC.activation(squares[:, 0, :], src[:, 0, :], ACT.Square, accum_out=sums[:, 0:1]))
        q1 = dve(DVE.tensor_tensor_reduce(squares[:, 1, :], src[:, 1, :], src[:, 1, :], 1.0, 0.0, ALU.mult,
                                          ALU.add, sums[:, 1:2]))
        return rsqrt(sums, n, RMS_EPS, q0, q1)

    def rsqrt(sums, n, eps, *ready):
        wait(DVE, *ready)
        v = dve(DVE.tensor_scalar(sums, sums, 1.0 / n, eps, ALU.mult, ALU.add))
        wait(POOL, v)
        return pool(POOL.tensor_tensor(sums, sums, minus_half[:, 0:sums.shape[1]], ALU.pow))

    def scale_halves(dst, src, col, *ready):
        wait(DVE, *ready)
        wait(SC, *ready)
        s0 = dve(DVE.tensor_scalar(dst[:, 0, :], src[:, 0, :], small[:, col:col + 1], None, ALU.mult))
        s1 = act(SC.activation(dst[:, 1, :], src[:, 1, :], ACT.Copy, scale=small[:, col + 1:col + 2]))
        return s0, s1

    def transpose_gained(dst, src, gain, free, *ready):
        s = src.rearrange("t h (p c) -> t h c p", c=KC)
        wait(PE, ident_ready, *ready)
        done = []
        for c2 in range(KC // 2):
            b = next_bank()
            for c in range(2):
                for h in range(NH):
                    o = c * S + h * P
                    last = PE.transpose(banks[b][:, o:o + P], s[:, h, 2 * c2 + c, :], ident[:, :])
            t = pe(last)
            for c in range(2):
                k = 2 * c2 + c
                if c2 % 2:
                    wait(SC, t, gains_in, *free)
                    e = act(SC.activation(dst[:, k, :], banks[b][:, c * S:(c + 1) * S], ACT.Copy,
                                          scale=gains[:, gain, k:k + 1]))
                else:
                    wait(DVE, t, gains_in, *free)
                    e = dve(DVE.tensor_scalar(dst[:, k, :], banks[b][:, c * S:(c + 1) * S],
                                              gains[:, gain, k:k + 1], None, ALU.mult))
            done.append(e)
            bank_free[b] = e
        return done

    def token_major(lhs, p, h, *ready):
        wait(PE, landed(p), *ready)
        b = next_bank()
        w = W8(p)
        for k in range(KC):
            last = PE.matmul(banks[b][:, :], lhs[:, k, h * P:(h + 1) * P], w[:, k, :], start=k == 0, stop=k == KC - 1)
        return b, pe(last)

    def transposed(rhs, p, pair, *ready):
        wait(PE, landed(p), *ready)
        b = next_bank()
        w = W8(p)
        for n in range(2):
            o = (2 * pair + n) * P
            for k in range(KC):
                last = PE.matmul(banks[b][:, n * S:(n + 1) * S], w[:, k, o:o + P], rhs[:, k, :],
                                 start=k == 0, stop=k == KC - 1)
        return b, pe(last)

    def evacuate(dst, b, step, *free, scale=1.0, func=None, on_act=True):
        if on_act:
            wait(SC, step, *free)
            bank_free[b] = act(SC.activation(dst, banks[b][:, :], func or ACT.Copy, scale=scale))
        else:
            wait(DVE, step, *free)
            bank_free[b] = dve(DVE.tensor_scalar(dst, banks[b][:, :], scale, None, ALU.mult))
        return bank_free[b]

    def add_residual(b, step, h, lo):
        wait(DVE, step)
        xs = X[:, h, lo:lo + 512]
        bank_free[b] = dve(DVE.tensor_tensor(xs, banks[b][:, :], xs, ALU.add))
        return bank_free[b]

    def release(step):
        released.append(step)
        p = len(released) - 1 + RING
        if p < NFIRST:
            wait(SP, step)
            load_piece(p, first[p])

    r = rms_scale(X, D, XN, 16, x_in)
    scaled = scale_halves(XN, X, 16, r)
    xT = transpose_gained(XT, XN, G_MIX, (), *scaled)

    wait(PE, sgu_in)
    b = next_bank()
    for g in range(GROUPS):
        last = PE.transpose(banks[b][:, g * P:(g + 1) * P], sgu_raw[:, g, :], ident[:, :])
    sgu_copied = evacuate(sgu_wT.rearrange("p g t -> p (g t)"), b, pe(last))
    wait(POOL, sgu_copied)
    sgu_masked = pool(POOL.affine_select(out=sgu_wT, in_=sgu_wT, compare_op=ALU.is_ge, fill=0.0, base=0,
                                         pattern=[[0, GROUPS], [1, P]], channel_multiplier=-1))

    uT = arena[3][:, 0:1024].rearrange("p (g t) -> p g t", t=S)
    v = arena[3][:, 1024:2048].rearrange("p (h n) -> p h n", h=NH)
    qT = arena[4][:, 0:1024].rearrange("p (g t) -> p g t", t=S)
    kT = arena[4][:, 1024:2048].rearrange("p (g t) -> p g t", t=S)
    v_done = []
    for h in range(NH):
        b, s = token_major(XT, Z_V, h, *xT)
        v_done.append(evacuate(v[:, h, :], b, s, func=ACT.Gelu))
    release(s)
    for pair in range(2):
        b, s = transposed(XT, Z_U, pair)
        u_done = evacuate(uT[:, 2 * pair:2 * pair + 2, :].rearrange("p g t -> p (g t)"), b, s, func=ACT.Gelu)
    release(s)

    vg = v.rearrange("p h (g c) -> p (h g) c", g=GROUPS)
    sq = XN.rearrange("p h (g c) -> p (h g) c", c=P)[:, 0:NH * GROUPS, :]
    mean = small[:, 24:32]
    var = small[:, 32:40]
    G8 = NH * GROUPS

    def each(s):
        return s.unsqueeze(2).to_broadcast([P, G8, P])

    def per_half(row):
        return row.unsqueeze(1).to_broadcast([P, NH, SGU])

    wait(DVE, *v_done)
    n1 = dve(DVE.tensor_reduce(mean, vg, AX, ALU.add))
    wait(DVE, n1)
    n2 = dve(DVE.tensor_scalar(mean, mean, 1.0 / P, None, ALU.mult))
    wait(DVE, n2)
    n3 = dve(DVE.tensor_tensor(vg, vg, each(mean), ALU.subtract))
    wait(DVE, n3, *xT)
    n4 = dve(DVE.tensor_tensor(sq, vg, vg, ALU.mult))
    wait(DVE, n4)
    n5 = dve(DVE.tensor_reduce(var, sq, AX, ALU.add))
    n6 = rsqrt(var, P, LN_EPS, n5)
    wait(DVE, n6, sgu_in)
    n7 = dve(DVE.tensor_tensor(vg, vg, each(var), ALU.mult))
    wait(DVE, n7)
    n8 = dve(DVE.tensor_tensor(v, v, per_half(bc[:, 0:512]), ALU.mult))
    wait(DVE, n8)
    vn_done = dve(DVE.tensor_tensor(v, v, per_half(bc[:, 512:1024]), ALU.add))

    for piece, dst, scale in ((Z_Q, qT, float(DQK) ** -0.5), (Z_K, kT, 1.0)):
        for pair in range(2):
            b, s = transposed(XT, piece, pair)
            qk_done = evacuate(dst[:, 2 * pair:2 * pair + 2, :].rearrange("p g t -> p (g t)"), b, s, scale=scale)
        release(s)
    for h in range(NH):
        b, s = token_major(XT, Z_VAL, h)
        vv_done = evacuate(vv[:, h, :], b, s)
    release(s)

    mixed_sgu = []
    sp_banks = []
    wait(PE, vn_done, sgu_masked, sgu_in, u_done)
    for n in range(NH):
        b = next_bank()
        for g in range(GROUPS):
            o = banks[b][:, g * P:(g + 1) * P]
            PE.matmul(o, v[:, n, g * P:(g + 1) * P], sgu_wT[:, g, :], start=True, stop=False)
            last = PE.matmul(o, ones[0:1, :], sgu_bias[0:1, g * P:(g + 1) * P], start=False, stop=True)
        sp_banks.append((b, pe(last)))

    lam = small[:, 40:44]
    lam_tmp = arena[6][:, 1024 + 4 * DQK:1024 + 6 * DQK].rearrange("p (i n) -> p i n", i=2)
    wait(DVE, lam_in)
    l1 = dve(DVE.tensor_tensor(lam_tmp, lam_rows[:, 0::2, :], lam_rows[:, 1::2, :], ALU.mult))
    wait(DVE, l1)
    l2 = dve(DVE.tensor_reduce(lam[:, 0:2], lam_tmp, AX, ALU.add))
    wait(SC, l2)
    l3 = act(SC.activation(lam[:, 2:4], lam[:, 0:2], ACT.Exp))
    wait(DVE, l3)
    l4 = dve(DVE.tensor_tensor(lam[:, 0:1], lam[:, 3:4], lam[:, 2:3], ALU.subtract))
    wait(DVE, l4)
    neg_lam_ready = dve(DVE.tensor_scalar(lam[:, 0:1], lam[:, 0:1], -LAMBDA_INIT, None, ALU.add))
    neg_lam = lam[:, 0:1]
    subln_ready = dve(DVE.tensor_scalar(small[:, 1:2], subln, 1.0 - LAMBDA_INIT, None, ALU.mult))

    mixedT = chunks(arena[6])
    for n, (b, s) in enumerate(sp_banks):
        wait(DVE, s, u_done, neg_lam_ready, sp_banks[-1][1])
        bank_free[b] = dve(DVE.tensor_tensor(mixedT[:, 0:4, n * P:(n + 1) * P],
                                             banks[b][:, :].rearrange("p (g t) -> p g t", g=GROUPS),
                                             uT[:, :, n * P:(n + 1) * P], ALU.mult))
        mixed_sgu.append(bank_free[b])

    memX = tok(arena[3])
    wait(SC, *mixed_sgu)
    mem_in = load("mem", memX, a["mem"][0].rearrange("(h p) d -> p h d", p=P))

    slopes = [2.0 ** (-8.0 * (i + 1) / DH) for i in range(DH)]
    XNf = arena[1]
    SCR = 2
    sc_read = [None] * SCR
    aT_read = [None] * SCR
    o_bank = []
    scratch_free = (n5,)
    unit = 0
    o_sb = XNf[:, 1536:2048].rearrange("p (h n) -> p h n", n=P)
    for qb in range(NH):
        nk = (qb + 1) * P
        a0 = S - nk
        ob = None
        o_steps = []
        for h in range(DH):
            u = unit % SCR
            unit += 1
            sc = XNf[:, u * 512:(u + 1) * 512].rearrange("p (i k) -> p i k", i=2)[:, :, 0:nk]
            aT = XNf[:, 1024 + u * 256:1024 + (u + 1) * 256].rearrange("p (k q) -> p k q", q=P)
            st = small[:, 48 + 8 * u:56 + 8 * u]
            wait(PE, qk_done)
            b2 = [next_bank(7) for _ in range(2)]
            for i in range(2):
                rows = slice(i * DQK, (i + 1) * DQK)
                last = PE.matmul(banks[b2[i]][:, 0:nk], qT[rows, h, qb * P:(qb + 1) * P], kT[rows, h, 0:nk],
                                 start=True, stop=True)
            s_step = pe(last)
            wait(DVE, s_step, alibi_ready, sc_read[u], *scratch_free)
            for i in range(2):
                t1 = dve(DVE.scalar_tensor_tensor(out=sc[:, i, :], in0=alibi[:, a0:S], scalar=slopes[h],
                                                  in1=banks[b2[i]][:, 0:nk], op0=ALU.mult, op1=ALU.add))
                bank_free[b2[i]] = t1
            wait(DVE, t1)
            t2 = dve(DVE.tensor_reduce(st[:, 0:2], sc, AX, ALU.max))
            wait(DVE, t2)
            t3 = dve(DVE.tensor_scalar(st[:, 2:4], st[:, 0:2], -1.0, None, ALU.mult))
            wait(SC, t3)
            for i in range(2):
                t4 = act(SC.activation(sc[:, i, :], sc[:, i, :], ACT.Exp, bias=st[:, 2 + i:3 + i],
                                       accum_out=st[:, 4 + i:5 + i]))
            wait(DVE, t4)
            t5 = dve(DVE.reciprocal(st[:, 6:8], st[:, 4:6]))
            wait(DVE, t5, neg_lam_ready)
            t6 = dve(DVE.tensor_tensor(st[:, 7:8], st[:, 7:8], neg_lam, ALU.mult))
            wait(DVE, t6)
            t7 = dve(DVE.tensor_scalar(sc[:, 1, :], sc[:, 1, :], st[:, 7:8], None, ALU.mult))
            wait(DVE, t7)
            t8 = dve(DVE.scalar_tensor_tensor(out=sc[:, 0, :], in0=sc[:, 0, :], scalar=st[:, 6:7], in1=sc[:, 1, :],
                                              op0=ALU.mult, op1=ALU.add))
            wait(PE, t8)
            b = next_bank(7)
            for kb in range(qb + 1):
                last = PE.transpose(banks[b][:, kb * P:(kb + 1) * P], sc[:, 0, kb * P:(kb + 1) * P], ident[:, :])
            t9 = pe(last)
            sc_read[u] = t9
            wait(SC, t9, aT_read[u])
            t10 = act(SC.activation(aT[:, 0:qb + 1, :].rearrange("p k q -> p (k q)"), banks[b][:, 0:nk], ACT.Copy))
            bank_free[b] = t10
            wait(PE, t10, vv_done)
            if ob is None:
                wait(PE, bank_free[7])
                ob = 7
            for kb in range(qb + 1):
                last = PE.matmul(banks[ob][:, h * P:(h + 1) * P], aT[:, kb, :], vv[:, kb, h * P:(h + 1) * P],
                                 start=kb == 0, stop=kb == qb)
            aT_read[u] = pe(last)
        o_free = scratch_free if qb == 0 else (o_turned,)
        wait(SC, aT_read[u], *o_free)
        w1 = act(SC.activation(o_sb.rearrange("p h n -> p (h n)"), banks[7][:, :], ACT.Copy))
        bank_free[7] = w1
        osq = arena[5][:, 1536:2048].rearrange("p (h n) -> p h n", n=P)
        ost = small[:, 64:68]
        wait(DVE, w1)
        w2 = dve(DVE.tensor_tensor(osq, o_sb, o_sb, ALU.mult))
        wait(DVE, w2)
        w3 = dve(DVE.tensor_reduce(ost, osq, AX, ALU.add))
        w4 = rsqrt(ost, P, RMS_EPS, w3)
        wait(DVE, w4)
        w5 = dve(DVE.tensor_tensor(o_sb, o_sb, ost.unsqueeze(2).to_broadcast([P, DH, P]), ALU.mult))
        wait(PE, w5)
        b = next_bank(7)
        for h in range(DH):
            last = PE.transpose(banks[b][:, h * P:(h + 1) * P], o_sb[:, h, :], ident[:, :])
        o_turned = pe(last)
        wait(SC, o_turned, subln_ready, sp_banks[-1][1], neg_lam_ready)
        mixed_diff = act(SC.activation(mixedT[:, 4:8, qb * P:(qb + 1) * P],
                                       banks[b][:, :].rearrange("p (h t) -> p h t", t=P), ACT.Copy,
                                       scale=small[:, 1:2]))
        bank_free[b] = mixed_diff

    memT = chunks(arena[4])
    r = rms_scale(memX, D, XN, 68, mem_in, o_turned, aT_read[0], aT_read[1], sc_read[0], sc_read[1])
    scaled = scale_halves(memX, memX, 68, r)
    memT_done = transpose_gained(memT, memX, G_MEM, (sc_read[0], sc_read[1]), *scaled)

    wait(PE, mixed_diff, *mixed_sgu)
    x1 = []
    for half in range(2):
        for h in range(NH):
            b, s = token_major(mixedT, P_OUT + half, h)
            x1.append(add_residual(b, s, h, 512 * half))
        release(s)
    mixed_read = s

    kmT = chunks(arena[5])
    vm = tok(arena[3])
    for j in range(2):
        for pair in range(2):
            b, s = transposed(memT, P_KV + j, pair, *memT_done)
            c = 4 * j + 2 * pair
            km_done = evacuate(kmT[:, c:c + 2, :].rearrange("p c t -> p (c t)"), b, s, aT_read[0], aT_read[1], w3)
        release(s)
    for j in range(2):
        for h in range(NH):
            b, s = token_major(memT, P_KV + 2 + j, h)
            vm_done = evacuate(vm[:, h, 512 * j:512 * (j + 1)], b, s)
        release(s)
    memT_read = s

    r = rms_scale(X, D, XN, 16, *x1)
    scaled = scale_halves(XN, X, 16, r)
    xT = transpose_gained(XT, XN, G_XQ, (), *scaled)
    qmT = chunks(arena[6])
    for j in range(2):
        for pair in range(2):
            b, s = transposed(XT, P_QM + j, pair, *xT)
            c = 4 * j + 2 * pair
            qm_done = evacuate(qmT[:, c:c + 2, :].rearrange("p c t -> p (c t)"), b, s, mixed_read)
        release(s)
    xn_read = s

    omT = chunks(arena[4])
    sc_read, pT_read = [None, None], [None, None]
    MSCALE = float(MHD) ** -0.5
    for h in range(MH):
        u = h % 2
        sc = XNf[:, u * 512:(u + 1) * 512].rearrange("p (q k) -> p q k", q=NH)
        pT = XNf[:, 1024 + u * 512:1536 + u * 512].rearrange("p (k q) -> p k q", q=S)
        st = small[:, 48 + 8 * u:56 + 8 * u]
        wait(PE, qm_done, km_done)
        b = next_bank()
        for qb in range(NH):
            for c in range(2):
                last = PE.matmul(banks[b][:, qb * M:(qb + 1) * M], qmT[:, 2 * h + c, qb * P:(qb + 1) * P],
                                 kmT[:, 2 * h + c, :], start=c == 0, stop=c == 1)
        s_step = pe(last)
        s_ps = banks[b][:, :].rearrange("p (q k) -> p q k", q=NH)
        wait(DVE, s_step)
        t2 = dve(DVE.tensor_reduce(st[:, 0:2], s_ps, AX, ALU.max))
        wait(DVE, t2)
        t3 = dve(DVE.tensor_scalar(st[:, 2:4], st[:, 0:2], -MSCALE, None, ALU.mult))
        wait(SC, t3, sc_read[u], xn_read)
        for qb in range(NH):
            t4 = act(SC.activation(sc[:, qb, :], s_ps[:, qb, :], ACT.Exp, bias=st[:, 2 + qb:3 + qb], scale=MSCALE,
                                   accum_out=st[:, 4 + qb:5 + qb]))
        bank_free[b] = t4
        wait(DVE, t4)
        t5 = dve(DVE.reciprocal(st[:, 6:8], st[:, 4:6]))
        wait(DVE, t5)
        t6 = dve(DVE.tensor_tensor(sc, sc, st[:, 6:8].unsqueeze(2).to_broadcast([P, NH, M]), ALU.mult))
        wait(PE, t6)
        b = next_bank()
        for kb in range(M // P):
            for qb in range(NH):
                o = kb * S + qb * P
                last = PE.transpose(banks[b][:, o:o + P], sc[:, qb, kb * P:(kb + 1) * P], ident[:, :])
        sc_read[u] = pe(last)
        wait(SC, pT_read[u])
        t7 = evacuate(pT.rearrange("p k q -> p (k q)"), b, sc_read[u])
        wait(PE, t7, vm_done)
        b = next_bank()
        for c in range(2):
            for kb in range(M // P):
                o = h * MHD + c * P
                last = PE.matmul(banks[b][:, c * S:(c + 1) * S], vm[:, kb, o:o + P], pT[:, kb, :],
                                 start=kb == 0, stop=kb == M // P - 1)
        pT_read[u] = pe(last)
        om_done = evacuate(omT[:, 2 * h:2 * h + 2, :].rearrange("p c t -> p (c t)"), b, pT_read[u], memT_read,
                           on_act=False)
    x2 = []
    for half in range(2):
        for h in range(NH):
            b, s = token_major(omT, P_OM + half, h, om_done)
            x2.append(add_residual(b, s, h, 512 * half))
        release(s)
    om_read = s

    NR = NG + NE
    wr = arena[3][:, 0:KC * NR].rearrange("p (c n) -> p c n", c=KC)
    rb = arena[3][:, 320:320 + NR]
    wait(SC, pT_read[0], pT_read[1])
    load("router", wr[:, :, 0:NG], a["w_router_group"][0].rearrange("(p c) n -> p c n", c=KC))
    load("router", wr[:, :, NG:NR], a["w_router_expert"][0].rearrange("(p c) n -> p c n", c=KC))
    load("router", rb[:, 0:NG], a["b_router_group"].partition_broadcast(P).rearrange("q l n -> q (l n)"))
    router_in = load("router", rb[:, NG:NR], a["b_router_expert"].partition_broadcast(P).rearrange("q l n -> q (l n)"))
    wait(POOL, pT_read[0], pT_read[1])
    tri = arena[3][:, 384:512]
    tri0 = pool(POOL.memset(tri, 1.0))
    wait(POOL, tri0)
    tri_ready = pool(POOL.affine_select(out=tri, in_=tri, compare_op=ALU.is_gt, fill=0.0, base=0, pattern=[[1, P]],
                                        channel_multiplier=-1))
    rank = arena[3][:, 512:544]
    rank_ready = pool(POOL.iota(rank, pattern=[[-1, NE]], base=NE, channel_multiplier=0,
                                allow_small_or_imprecise_dtypes=True))

    r = rms_scale(X, D, XN, 16, *x2, sc_read[0], sc_read[1])
    scaled = scale_halves(XN, X, 16, r)
    xT = transpose_gained(XT, XN, G_FFN, (), *scaled)
    wait(PE, router_in, *xT)
    b = next_bank()
    for h in range(NH):
        for k in range(KC):
            last = PE.matmul(banks[b][:, h * 64:h * 64 + NR], XT[:, k, h * P:(h + 1) * P], wr[:, k, :],
                             start=k == 0, stop=k == KC - 1)
    s = pe(last)
    R = arena[3]

    def tile3(at, n):
        return R[:, at:at + NH * n].rearrange("p (h n) -> p h n", h=NH)

    logits = tile3(560, NR)
    top, gate_g = tile3(640, 1), tile3(642, 1)
    eg, hot_g, pick = tile3(656, NG), tile3(664, NG), tile3(672, NG)
    el = tile3(688, EPG)
    tmp = tile3(704, NE)
    m1, m2, e2, den = tile3(768, 1), tile3(770, 1), tile3(772, 1), tile3(774, 1)
    hot1, hot2, el2 = tile3(784, EPG), tile3(800, EPG), tile3(816, EPG)
    wsel, asel = tile3(832, EPG), tile3(848, EPG)
    assigned, weight = tile3(864, NE), tile3(928, NE)

    def V(ins, *ready):
        s = dve(ins)
        wait(DVE, s)
        return s

    def wide(ap, n):
        return ap.to_broadcast([P, NH, n])

    wait(DVE, s, router_in, rank_ready)
    V(DVE.tensor_tensor(logits, banks[b][:, 0:128].rearrange("p (h n) -> p h n", h=NH)[:, :, 0:NR],
                        rb.unsqueeze(1).to_broadcast([P, NH, NR]), ALU.add))
    bank_free[b] = (dve.sem, dve.count)

    def first_max(hot, top_, src, n):
        V(DVE.tensor_reduce(top_, src, AX, ALU.max))
        V(DVE.tensor_tensor(hot, src, wide(top_, n), ALU.is_equal))
        V(DVE.tensor_tensor(hot, hot, rank[:, 0:n].unsqueeze(1).to_broadcast([P, NH, n]), ALU.mult))
        V(DVE.tensor_reduce(den, hot, AX, ALU.max))
        V(DVE.tensor_tensor(hot, hot, wide(den, n), ALU.is_equal))

    lg = logits[:, :, 0:NG]
    first_max(hot_g, top, lg, NG)
    g1 = V(DVE.tensor_tensor(eg, lg, wide(top, NG), ALU.subtract))
    wait(SC, g1)
    g2 = act(SC.activation(eg, eg, ACT.Exp))
    wait(DVE, g2)
    V(DVE.tensor_reduce(gate_g, eg, AX, ALU.add))
    V(DVE.reciprocal(gate_g, gate_g))
    for h in range(NH):
        V(DVE.tensor_tensor(tmp[:, h, :].rearrange("p (g e) -> p g e", g=NG),
                            logits[:, h, NG:NR].rearrange("p (g e) -> p g e", g=NG),
                            hot_g[:, h, :].unsqueeze(2).to_broadcast([P, NG, EPG]), ALU.mult))
        V(DVE.tensor_reduce(el[:, h, :], tmp[:, h, :].rearrange("p (g e) -> p e g", g=NG), AX, ALU.add))
    first_max(hot1, m1, el, EPG)
    V(DVE.scalar_tensor_tensor(out=el2, in0=hot1, scalar=-3.0e38, in1=el, op0=ALU.mult, op1=ALU.add))
    first_max(hot2, m2, el2, EPG)
    g3 = V(DVE.tensor_tensor(e2, m2, m1, ALU.subtract))
    wait(SC, g3)
    g4 = act(SC.activation(e2, e2, ACT.Exp))
    wait(DVE, g4)
    V(DVE.tensor_scalar(den, e2, 1.0, None, ALU.add))
    V(DVE.reciprocal(den, den))
    V(DVE.tensor_tensor(den, den, gate_g, ALU.mult))
    V(DVE.tensor_tensor(e2, e2, den, ALU.mult))
    V(DVE.tensor_tensor(wsel, hot1, wide(den, EPG), ALU.mult))
    V(DVE.tensor_tensor(el2, hot2, wide(e2, EPG), ALU.mult))
    V(DVE.tensor_tensor(wsel, wsel, el2, ALU.add))
    V(DVE.tensor_tensor(asel, hot1, hot2, ALU.add))
    for h in range(NH):
        for dst, sel in ((assigned, asel), (weight, wsel)):
            V(DVE.tensor_tensor(dst[:, h, :].rearrange("p (g e) -> p g e", g=NG),
                                sel[:, h, :].unsqueeze(1).to_broadcast([P, NG, EPG]),
                                hot_g[:, h, :].unsqueeze(2).to_broadcast([P, NG, EPG]), ALU.mult))
    V(DVE.memset(pos[:, :, NE:NE + 1], -1.0))
    V(DVE.memset(wts[:, :, NE:NE + 1], 0.0))
    weights_ready = V(DVE.tensor_copy(wts[:, :, 0:NE], weight))
    wait(PE, weights_ready, tri_ready)
    b = next_bank()
    PE.matmul(banks[b][:, 0:NE], tri, assigned[:, 0, :], start=True, stop=True)
    PE.matmul(banks[b][:, NE:2 * NE], tri, assigned[:, 1, :], start=True, stop=False)
    PE.matmul(banks[b][:, NE:2 * NE], ones[:, :], assigned[:, 0, :], start=False, stop=True)
    PE.matmul(banks[b][:, 2 * NE:3 * NE], ones[:, :], assigned[:, 0, :], start=True, stop=False)
    s = pe(PE.matmul(banks[b][:, 2 * NE:3 * NE], ones[:, :], assigned[:, 1, :], start=False, stop=True))
    wait(DVE, s)
    place = pos[:, :, 0:NE]
    V(DVE.tensor_scalar(place, banks[b][:, 0:2 * NE].rearrange("p (h n) -> p h n", h=NH), 1.0, None, ALU.add))
    V(DVE.tensor_tensor(place, place, assigned, ALU.mult))
    V(DVE.tensor_scalar(place, place, -1.0, None, ALU.add))
    V(DVE.tensor_reduce(den[:, 0, :], banks[b][:, 2 * NE:3 * NE], AX, ALU.max))
    routed = V(DVE.tensor_scalar(spill_flag[:, :], den[0:1, 0, :], float(SLOTS), None, ALU.is_gt))
    bank_free[b] = routed

    ACC = banks[0:4]
    GATH, GU, DN, MISC = banks[4:8]
    NGU = 2 * DE // JT
    NY = D // JT
    E3 = arena[3]
    ROWS = arena[4][:, 0:512]
    XTE = arena[4][:, 512:1024]
    SILU = arena[4][:, 1024:1024 + DE // JT]
    HID = arena[4][:, 1280:1280 + DE // JT]
    HT = arena[4][:, 1536:2048]
    YS = arena[5][:, 0:NY]
    ONEHOT = arena[5][:, 512:512 + 3 * NH * SLOTS].rearrange("p (j h s) -> p j h s", j=3, h=NH)
    ROUTE = arena[5][:, 1024:1024 + 3 * NH * P].rearrange("p (j h s) -> p j h s", j=3, h=NH)
    ROUTET = arena[6][:, 0:3 * NH * P].rearrange("p (j h t) -> p j h t", j=3, h=NH)
    SP_IOTA = arena[6][:, 1024:1024 + P]
    hn = XN.rearrange("t h (p c) -> t h c p", c=KC)
    gain_ffn = gains[:, G_FFN, :]
    HCH = DE // JT // P
    CPT = KC // JT

    wait(DVE, om_read)
    wait(SC, om_read)
    for b in range(8):
        wait(PE, bank_free[b])
    wait(PE, *x2)
    for h in range(NH):
        for j in range(2):
            last = PE.matmul(ACC[2 * h + j][:, :], ident[:, :], X[:, h, 512 * j:512 * (j + 1)], start=True, stop=True,
                             skip_group_check=True)
    residual_in = pe(last)
    wait(DVE, iota_ready)

    def build(q, e, j, places, turned):
        q.wait(DVE, "turned", turned)
        for h in range(NH):
            DVE.tensor_scalar(ONEHOT[:, j, h, :], places[:, 0:SLOTS], pos[:, h, bass.ds(e, 1)], None, ALU.is_equal)
        for h in range(NH):
            last = DVE.tensor_scalar(ROUTE[:, j, h, :], places[:, :], pos[:, h, bass.ds(e, 1)], wts[:, h, bass.ds(e, 1)],
                                     ALU.is_equal, ALU.mult)
        q.passed("built", last)

    def gather(q, n, j):
        q.wait(PE, "built", n + 1)
        q.wait(PE, "xT", n)
        for h in range(NH):
            for t in range(JT):
                last = PE.matmul(GATH[t * SLOTS:(t + 1) * SLOTS, 0:CPT * P], ONEHOT[:, j, h, :],
                                 hn[:, h, t * CPT:(t + 1) * CPT, :], start=h == 0, stop=h == NH - 1,
                                 tile_position=(0, t * SLOTS), skip_group_check=True)
        q.passed("gathered", last)

    def rows_out(q, n):
        q.wait(SC, "gathered", n + 1)
        q.wait(SC, "turned", n)
        q.passed("rows", SC.activation(ROWS[:, 0:CPT * P], GATH[:, 0:CPT * P], ACT.Copy))

    def turn_rows(q, n, j, hidden_read):
        q.wait(PE, "rows", n + 1)
        for c in range(CPT):
            PE.transpose(GATH[:, c * P:(c + 1) * P], ROWS[:, c * P:(c + 1) * P], ident[:, :])
        q.wait(PE, "routeT", n)
        q.wait(PE, "hiddenT", hidden_read)
        for h in range(NH):
            last = PE.transpose(MISC[:, h * P:(h + 1) * P], ROUTE[:, j, h, :], ident[:, :])
        q.passed("turned", last)

    def xT_out(q, n):
        q.wait(DVE, "turned", n + 1)
        for c in range(CPT):
            g = gain_ffn[:, c::CPT].unsqueeze(2).to_broadcast([P, JT, SLOTS])
            last = DVE.tensor_tensor(XTE[:, c * P:(c + 1) * P].rearrange("p (t s) -> p t s", t=JT),
                                     GATH[:, c * P:(c + 1) * P].rearrange("p (t s) -> p t s", t=JT), g, ALU.mult)
        q.passed("xT", last)

    def routeT_out(q, n, j, scattered):
        q.wait(SC, "turned", n + 1)
        q.wait(SC, "scattered", scattered)
        q.passed("routeT", SC.activation(ROUTET[:, j, :, :].rearrange("p h t -> p (h t)"), MISC[:, 0:NH * P],
                                         ACT.Copy))

    def gate_up(q, n, w):
        q.wait(PE, "xT", n + 1)
        q.wait(PE, "hidden", n)
        wgu = ring[:, w * PIECE:(w + 2) * PIECE].rearrange("p (m c n) -> p m c n", m=2, c=KC)
        for k in range(KC):
            o = (k % CPT) * P + (k // CPT) * SLOTS
            for t in range(JT):
                last = PE.matmul(GU[t * SLOTS:(t + 1) * SLOTS, 0:NGU], XTE[:, o:o + SLOTS],
                                 wgu[:, :, k, t * (DE // JT):(t + 1) * (DE // JT)], start=k == 0, stop=k == KC - 1,
                                 tile_position=(0, t * SLOTS), skip_group_check=True)
        q.passed("gate_up", last)

    def silu_out(q, n):
        q.wait(SC, "gate_up", n + 1)
        q.wait(SC, "hidden", n)
        q.passed("silu", SC.activation(SILU, GU[:, 0:DE // JT], ACT.Silu))

    def hidden_out(q, n):
        q.wait(DVE, "silu", n + 1)
        q.wait(DVE, "hidden_turned", n)
        q.passed("hidden", DVE.tensor_tensor(HID, GU[:, DE // JT:NGU], SILU, ALU.mult))

    def turn_hidden(q, n, route_read):
        q.wait(PE, "hidden", n + 1)
        q.wait(PE, "hiddenT", n)
        q.wait(PE, "routeT", route_read)
        for i in range(HCH):
            last = PE.transpose(MISC[:, 256 + i * P:256 + (i + 1) * P], HID[:, i * P:(i + 1) * P], ident[:, :])
        q.passed("hidden_turned", last)

    def hiddenT_out(q, n):
        q.wait(SC, "hidden_turned", n + 1)
        q.wait(SC, "down", n)
        q.passed("hiddenT", SC.activation(HT[:, 0:HCH * P], MISC[:, 256:256 + HCH * P], ACT.Copy))

    def down(q, n, w):
        q.wait(PE, "hiddenT", n + 1)
        q.wait(PE, "y", n)
        wd = ring[:, (w + 2) * PIECE:(w + 3) * PIECE].rearrange("p (c n) -> p c n", n=D)
        K4 = DE // P
        for k in range(K4):
            o = (k % HCH) * P + (k // HCH) * SLOTS
            for t in range(JT):
                last = PE.matmul(DN[t * SLOTS:(t + 1) * SLOTS, 0:NY], HT[:, o:o + SLOTS],
                                 wd[:, k, t * NY:(t + 1) * NY], start=k == 0, stop=k == K4 - 1,
                                 tile_position=(0, t * SLOTS), skip_group_check=True)
        q.passed("down", last)

    def y_out(q, n):
        q.wait(DVE, "down", n + 1)
        q.wait(DVE, "scattered", n)
        q.passed("y", DVE.tensor_copy(YS, DN[:, 0:NY]))

    def scatter(q, n, j, halves, signal=True):
        q.wait(PE, "y", n + 1)
        q.wait(PE, "routeT", n + 1)
        for h in halves:
            for t in range(JT):
                o = (t * NY) % 512
                last = PE.matmul(ACC[2 * h + t * NY // 512][:, o:o + NY],
                                 ROUTET[t * SLOTS:(t + 1) * SLOTS, j, h, :], YS[t * SLOTS:(t + 1) * SLOTS, :],
                                 start=False, stop=True, tile_position=(t * SLOTS, 0), skip_group_check=True)
        if signal:
            q.passed("scattered", last)

    w_gate = a["w_gate"][0].rearrange("e (p c) n -> e p (c n)", c=KC)
    w_up = a["w_up"][0].rearrange("e (p c) n -> e p (c n)", c=KC)
    w_down = a["w_down"][0].rearrange("e (c p) n -> e p c n", p=P)

    def expert_loads(e, w, sems):
        for i, src in enumerate((w_gate, w_up)):
            SP.dma_start(ring[:, (w + i) * PIECE:(w + i + 1) * PIECE],
                         src[bass.ds(e, 1), :, :].rearrange("o p n -> (o p) n")).then_inc(sems[i], 16)
        SP.dma_start(ring[:, (w + 2) * PIECE:(w + 3) * PIECE].rearrange("p (c n) -> p c n", n=D),
                     w_down[bass.ds(e, 1), :, :, :].rearrange("o p c n -> (o p) c n")).then_inc(sems[2], 16)

    def weights_of(n0, i, part):
        p = NFIRST + 3 * n0 + part
        return slot_sem[p % RING], 16 * (p // RING + 1) + 16 * i

    q = Handoffs(nc, "moe_")

    def step(n, n0, i, route_next=True, scatter_prev=True, build_next=True):
        w = (NFIRST + 3 * n0) % RING
        j = n0 % 3
        if build_next:
            build(q, n + 2, (j + 2) % 3, iota, n)
        if route_next:
            gather(q, n + 1, (j + 1) % 3)
            rows_out(q, n + 1)
        for part in (0, 1):
            PE.wait_ge(*weights_of(n0, i, part))
        gate_up(q, n, w)
        silu_out(q, n)
        hidden_out(q, n)
        if route_next:
            turn_rows(q, n + 1, (j + 1) % 3, n)
            xT_out(q, n + 1)
            routeT_out(q, n + 1, (j + 1) % 3, n - 1)
        if scatter_prev:
            scatter(q, n - 1, (j + 2) % 3, (0,), signal=False)
        turn_hidden(q, n, n + 2 if route_next else n + 1)
        hiddenT_out(q, n)
        if scatter_prev:
            scatter(q, n - 1, (j + 2) % 3, (1,))
        PE.wait_ge(*weights_of(n0, i, 2))
        down(q, n, w)
        y_out(q, n)

    def expert_stream(n, n0, *read):
        w = (NFIRST + 3 * n0) % RING
        if read:
            wait(SP, *read)
        else:
            q.wait(SP, "gate_up", n - 2)
            q.wait(SP, "down", n - 2)
        expert_loads(n, w, [slot_sem[w], slot_sem[w + 1], slot_sem[w + 2]])

    expert_stream(0, 0, *released[NFIRST - RING:NFIRST - RING + 3])
    expert_stream(1, 1, *released[NFIRST - RING + 3:NFIRST - RING + 6])
    wait(SP, *released[NFIRST - RING + 6:NFIRST - RING + 9])

    build(q, 0, 0, iota, 0)
    build(q, 1, 1, iota, 0)
    gather(q, 0, 0)
    rows_out(q, 0)
    turn_rows(q, 0, 0, 0)
    xT_out(q, 0)
    routeT_out(q, 0, 0, 0)
    step(0, 0, 0, scatter_prev=False)
    ROUNDS = (NE - 2) // 3
    assert NE == 2 + 3 * ROUNDS
    with nc.Fori(0, ROUNDS) as i:
        for j in range(3):
            expert_stream(i * 3 + (2 + j), 2 + j)
            step(i * 3 + (1 + j), 1 + j, i)
    step(NE - 1, NE - 1, 0, route_next=False, build_next=False)
    scatter(q, NE - 1, (NE - 1) % 3, (0, 1))

    engines = (PE, DVE, SC, POOL, SP)
    for engine in engines:
        wait(engine, routed)
    spill = nc.values_load(spill_flag[0:1, 0:1], min_val=0, max_val=1)
    sq = Handoffs(nc, "spill_")
    spill_sem = [nc.alloc_semaphore(f"spill_weights{i}") for i in range(3)]
    spill_iota_sem = nc.alloc_semaphore("spill_iota")
    SPILL_W = 3
    passes = S // SLOTS - 1
    with nc.If(spill > 0):
        for engine in engines:
            q.wait(engine, "scattered", NE)
        for m in range(passes):
            if m:
                sq.wait(DVE, "built", m * NE)
            DVE.tensor_scalar(SP_IOTA, iota[:, :], float(SLOTS * (m + 1)), None, ALU.add).then_inc(spill_iota_sem, 1)
            DVE.wait_ge(spill_iota_sem, m + 1)
            with nc.Fori(0, NE) as e:
                n = e + m * NE
                sq.wait(SP, "down", n)
                expert_loads(e, SPILL_W, spill_sem)
                build(sq, e, 0, SP_IOTA, n)
                gather(sq, n, 0)
                rows_out(sq, n)
                turn_rows(sq, n, 0, n)
                xT_out(sq, n)
                routeT_out(sq, n, 0, n)
                for i in (0, 1):
                    PE.wait_ge(spill_sem[i], (n + 1) * 16)
                gate_up(sq, n, SPILL_W)
                silu_out(sq, n)
                hidden_out(sq, n)
                turn_hidden(sq, n, n + 1)
                hiddenT_out(sq, n)
                PE.wait_ge(spill_sem[2], (n + 1) * 16)
                down(sq, n, SPILL_W)
                y_out(sq, n)
                scatter(sq, n, 0, (0, 1))
        for engine in engines:
            sq.wait(engine, "scattered", passes * NE)

    released2 = []

    def release2(step=None):
        released2.append(step)
        k = len(released2) - 1 + RING
        if k < len(second):
            wait(SP, step)
            load_piece(P_SECOND + k, second[k])

    for k in range(RING):
        if k % 3 == 0:
            q.wait(SP, "gate_up", NE - 2 + k // 3)
            q.wait(SP, "down", NE - 2 + k // 3)
        load_piece(P_SECOND + k, second[k])

    def gain_row(name, src, *free):
        wait(SC, *free)
        return load(name, bc[:, :], src.partition_broadcast(P).rearrange("q l n -> q (l n)"))

    final_in = gain_row("norm_final", a["norm_final"].rearrange("(l n) -> l n", l=1), vn_done)
    q.wait(DVE, "scattered", NE)
    q.wait(SC, "scattered", NE)

    def drain(bank_of, *ready):
        done = []
        for h in range(NH):
            for j in range(2):
                b = bank_of(h, j)
                e = SC if j else DVE
                wait(e, *ready)
                o = XN[:, h, 512 * j:512 * (j + 1)]
                bank_free[b] = act(SC.activation(o, banks[b][:, :], ACT.Copy)) if j else dve(DVE.tensor_copy(o, banks[b][:, :]))
                done.append(bank_free[b])
        return done

    def rms_rows(squares, gain_in, *ready):
        r = rms_scale(XN, D, squares, 16, *ready)
        scaled = scale_halves(XN, XN, 16, r)
        wait(DVE, gain_in, *scaled)
        return [dve(DVE.tensor_tensor(XN[:, h, :], XN[:, h, :], bc[:, :], ALU.mult)) for h in range(NH)]

    drained = drain(lambda h, j: 2 * h + j)
    for b in range(4, 8):
        bank_free[b] = drained[-2]
    normed = rms_rows(tok(arena[2]), final_in, *drained)
    wait(DVE, *normed)
    x_ready = dve(DVE.tensor_copy(X, XN))
    mix_post_in = gain_row("mix_post", a["norm_mix_post_2"], x_ready)

    r = rms_scale(X, D, tok(arena[2]), 16, x_ready)
    scaled = scale_halves(XN, X, 16, r)
    xT = transpose_gained(XT, XN, G_PRE2, (r,), *scaled)

    q2T, k2T, v2, o2T = chunks(arena[3]), chunks(arena[4]), tok(arena[5]), chunks(arena[6])
    DH2 = D // H2
    piece = P_QKV
    for dst, scale in ((q2T, float(DH2) ** -0.5), (k2T, 1.0)):
        for j in range(2):
            for pair in range(2):
                b, s = transposed(XT, piece, pair, *xT)
                c = 4 * j + 2 * pair
                qk_done = evacuate(dst[:, c:c + 2, :].rearrange("p c t -> p (c t)"), b, s, x_ready, scale=scale)
            release2(s)
            piece += 1
    for j in range(2):
        for h in range(NH):
            b, s = token_major(XT, piece, h)
            v_done = evacuate(v2[:, h, 512 * j:512 * (j + 1)], b, s)
        release2(s)
        piece += 1

    slopes2 = [2.0 ** (-8.0 * (i + 1) / H2) for i in range(H2)]
    sc_read, pT_read = [None, None], [None, None]
    for h in range(H2):
        u = h % 2
        sc = XNf[:, u * 512:(u + 1) * 512].rearrange("p (q k) -> p q k", q=NH)
        pT = XNf[:, 1024 + u * 512:1536 + u * 512].rearrange("p (k q) -> p k q", q=S)
        st = small[:, 48 + 8 * u:56 + 8 * u]
        wait(PE, qk_done)
        b = next_bank()
        s_ps = banks[b][:, :].rearrange("p (q k) -> p q k", q=NH)
        for qb in range(NH):
            nk = (qb + 1) * P
            last = PE.matmul(s_ps[:, qb, 0:nk], q2T[:, h, qb * P:(qb + 1) * P], k2T[:, h, 0:nk], start=True, stop=True)
        s_step = pe(last)
        wait(DVE, s_step, sc_read[u], *xT)
        for qb in range(NH):
            nk = (qb + 1) * P
            t1 = dve(DVE.scalar_tensor_tensor(out=sc[:, qb, 0:nk], in0=alibi[:, S - nk:S], scalar=slopes2[h],
                                              in1=s_ps[:, qb, 0:nk], op0=ALU.mult, op1=ALU.add))
        bank_free[b] = t1
        wait(DVE, t1)
        for qb in range(NH):
            t2 = dve(DVE.tensor_reduce(st[:, qb:qb + 1], sc[:, qb, 0:(qb + 1) * P], AX, ALU.max))
        wait(DVE, t2)
        t3 = dve(DVE.tensor_scalar(st[:, 2:4], st[:, 0:2], -1.0, None, ALU.mult))
        wait(SC, t3)
        for qb in range(NH):
            nk = (qb + 1) * P
            t4 = act(SC.activation(sc[:, qb, 0:nk], sc[:, qb, 0:nk], ACT.Exp, bias=st[:, 2 + qb:3 + qb],
                                   accum_out=st[:, 4 + qb:5 + qb]))
        wait(DVE, t4)
        t5 = dve(DVE.reciprocal(st[:, 6:8], st[:, 4:6]))
        wait(DVE, t5)
        for qb in range(NH):
            nk = (qb + 1) * P
            t6 = dve(DVE.tensor_scalar(sc[:, qb, 0:nk], sc[:, qb, 0:nk], st[:, 6 + qb:7 + qb], None, ALU.mult))
        wait(PE, t6)
        b = next_bank()
        PE.transpose(banks[b][:, 0:P], sc[:, 0, 0:P], ident[:, :])
        PE.transpose(banks[b][:, P:2 * P], sc[:, 1, 0:P], ident[:, :])
        sc_read[u] = pe(PE.transpose(banks[b][:, 2 * P:3 * P], sc[:, 1, P:2 * P], ident[:, :]))
        wait(SC, sc_read[u], pT_read[u])
        pTf = pT.rearrange("p k q -> p (k q)")
        t7 = act(SC.activation(pTf[:, 0:3 * P], banks[b][:, 0:3 * P], ACT.Copy))
        bank_free[b] = t7
        wait(PE, t7, v_done)
        b = next_bank()
        hd = slice(h * DH2, (h + 1) * DH2)
        PE.matmul(banks[b][:, 0:S], v2[:, 0, hd], pTf[:, 0:S], start=True, stop=False)
        pT_read[u] = pe(PE.matmul(banks[b][:, P:S], v2[:, 1, hd], pTf[:, S:S + P], start=False, stop=True))
        wait(DVE, pT_read[u])
        o_done = dve(DVE.tensor_copy(o2T[:, h, :], banks[b][:, 0:S]))
        bank_free[b] = o_done

    def post_norm(bank_of, steps, gain_in):
        drained = drain(bank_of, *steps)
        normed = rms_rows(tok(arena[2]), gain_in, *drained)
        done = []
        for h in range(NH):
            wait(DVE, normed[h])
            done.append(dve(DVE.tensor_tensor(X[:, h, :], X[:, h, :], XN[:, h, :], ALU.add)))
        return done

    used, steps = {}, []
    for j in range(2):
        for h in range(NH):
            b, s = token_major(o2T, P_O2 + j, h, o_done)
            used[h, j] = b
            steps.append(s)
        release2(s)
    x_ready = post_norm(lambda h, j: used[h, j], steps, mix_post_in)
    ffn_post_in = gain_row("ffn_post", a["norm_ffn_post_2"], *x_ready)

    r = rms_scale(X, D, XN, 16, *x_ready)
    scaled = scale_halves(XN, X, 16, r)
    xT = transpose_gained(XT, XN, G_FFN2, (), *scaled)

    def hidden2(f, n=1):
        return arena[3 + f // 8][:, (f % 8) * S:(f % 8 + n) * S]

    for j in range(DFF // 512):
        for pair in range(2):
            b, s = transposed(XT, P_UP + j, pair, *xT)
            f = 4 * j + 2 * pair
            wait(SC, steps[-1])
            t = evacuate(hidden2(f, 2), b, s, func=ACT.Relu)
            wait(DVE, t)
            squared = dve(DVE.tensor_tensor(hidden2(f, 2), hidden2(f, 2), hidden2(f, 2), ALU.mult))
        release2(s)
    out_banks = [next_bank() for _ in range(4)]
    wait(PE, squared)
    NDOWN = DFF // 512
    for j in range(NDOWN):
        wait(PE, landed(P_DOWN + j))
        w = slot(P_DOWN + j).rearrange("p (c n) -> p c n", n=D)
        for h in range(NH):
            for half in range(2):
                for k in range(4):
                    last = PE.matmul(banks[out_banks[2 * h + half]][:, :], hidden2(4 * j + k)[:, h * P:(h + 1) * P],
                                     w[:, k, 512 * half:512 * (half + 1)], start=j == 0 and k == 0,
                                     stop=j == NDOWN - 1 and k == 3, skip_group_check=True)
        s = pe(last)
        release2(s)
    x_ready = post_norm(lambda h, j: out_banks[2 * h + j], [s], ffn_post_in)
    stored = nc.alloc_semaphore("stored")
    for h in range(NH):
        wait(SP, x_ready[h])
        SP.dma_start(out[0].rearrange("(h p) d -> p h d", p=P)[:, h, :], X[:, h, :]).then_inc(stored, 16)
    SP.wait_ge(stored, 16 * NH)


INPUTS = ("x", "mem", "norm_mix", "w_in", "sgu_ln_g", "sgu_ln_b", "sgu_w", "sgu_b", "lambda_q1", "lambda_k1",
          "lambda_q2", "lambda_k2", "diff_subln", "w_out", "norm_xq", "norm_mem", "w_q_mem", "w_kv_mem", "w_o_mem",
          "norm_ffn", "w_router_group", "b_router_group", "w_router_expert", "b_router_expert", "w_gate", "w_up",
          "w_down", "norm_final", "norm_mix_pre_2", "norm_mix_post_2", "norm_ffn_pre_2", "norm_ffn_post_2", "w_up_2",
          "w_down_2", "attn_w_qkv_2", "attn_w_o_2")


def kernel(**inputs):
    import numpy as np
    import concourse.bacc as bacc
    from concourse.bass_utils import run_bass_kernel_spmd

    nc = bacc.Bacc("TRN2", target_bir_lowering=False, num_devices=1)
    arrays, aps = {}, {}
    for name in INPUTS:
        arrays["in_" + name] = np.ascontiguousarray(inputs[name])
        aps[name] = nc.dram_tensor("in_" + name, arrays["in_" + name].shape, F32, kind="ExternalInput").ap()
    out = nc.dram_tensor("out_0", arrays["in_x"].shape, F32, kind="ExternalOutput").ap()
    build_program(nc, aps, out)
    return run_bass_kernel_spmd(nc, [arrays], core_ids=[0]).results[0]["out_0"]
```

```python
import math

import concourse.bass as bass
from concourse import mybir

F32 = mybir.dt.float32
I32 = mybir.dt.int32
ALU = mybir.AluOpType
ACT = mybir.ActivationFunctionType
AX = mybir.AxisListType.X

P = 128
PIECE = 4096
RING = 9
SLOTS = 64
NEG = -1.0e30
RMS_EPS = 1e-6
LN_EPS = 1e-5


class Steps:

    def __init__(self, nc, name):
        self.sem = nc.alloc_semaphore(name)
        self.count = 0

    def __call__(self, instruction):
        self.count += 1
        instruction.then_inc(self.sem, 1)
        return (self.sem, self.count)


class Handoffs:

    AHEAD = 3

    def __init__(self, nc, prefix):
        names = ("built", "gathered", "rows", "turned", "xT", "routeT", "gate_up", "silu", "hidden",
                 "hidden_turned", "hiddenT", "down", "y", "scattered")
        self.sems = {name: nc.alloc_semaphore(prefix + name) for name in names}
        for name in names:
            nc.gpsimd.sem_inc(self.sems[name], self.AHEAD)

    def wait(self, engine, name, experts):
        engine.wait_ge(self.sems[name], experts + self.AHEAD)

    def passed(self, name, instruction):
        instruction.then_inc(self.sems[name], 1)


def build_program(nc, a, out):
    _, S, D = a["x"].shape
    NH = S // P
    KC = D // P
    M = a["mem"].shape[1]
    GROUPS, CHUNK = a["sgu_b"].shape[1:]
    SGU = GROUPS * P
    DQK = a["lambda_q1"].shape[1]
    DH = 4
    MH = 4
    MHD = D // MH
    NG = a["w_router_group"].shape[2]
    NE = a["w_router_expert"].shape[2]
    EPG = NE // NG
    DE = a["w_gate"].shape[3]
    H2 = 8
    DFF = a["w_up_2"].shape[2]
    LAMBDA_INIT = 0.8 - 0.6 * math.exp(-0.3 * 0)
    assert (S, D, M, CHUNK, DE, KC, NH) == (256, 1024, 256, 128, 512, 8, 2)
    HALF = KC // 2
    JT = P // SLOTS
    assert JT in (2, 4)

    PE, DVE, SC, POOL, SP = nc.tensor, nc.vector, nc.scalar, nc.gpsimd, nc.sync
    pe, dve, act, pool = Steps(nc, "pe_steps"), Steps(nc, "dve_steps"), Steps(nc, "act_steps"), Steps(nc, "pool_steps")
    waited = {}

    def wait(engine, *steps):
        for s in steps:
            if s is None:
                continue
            sem, value = s
            key = (id(engine), id(sem))
            if waited.get(key, 0) < value:
                engine.wait_ge(sem, value)
                waited[key] = value

    ring = nc.alloc_sbuf_tensor("ring", [P, RING * PIECE], F32)
    arena = [nc.alloc_sbuf_tensor(f"arena{i}", [P, 2048], F32) for i in range(7)]
    bc = nc.alloc_sbuf_tensor("gain_rows", [P, 1024], F32)
    ident = nc.alloc_sbuf_tensor("ident", [P, P], F32)
    ones = nc.alloc_sbuf_tensor("ones", [P, P], F32)
    alibi = nc.alloc_sbuf_tensor("alibi", [P, S], F32)
    iota = nc.alloc_sbuf_tensor("iota", [P, P], F32)
    gains = nc.alloc_sbuf_tensor("gains", [P, 6, KC], F32)
    small = nc.alloc_sbuf_tensor("small", [P, 128], F32)
    pos = nc.alloc_sbuf_tensor("pos", [P, NH, NE + 1], F32)
    wts = nc.alloc_sbuf_tensor("wts", [P, NH, NE + 1], F32)
    spill_flag = nc.alloc_sbuf_tensor("spill_flag", [1, 1], I32)
    banks = [nc.alloc_psum_tensor(f"bank{i}", [P, 512], F32) for i in range(8)]
    bank_free = [None] * 8

    def tok(t):
        return t[:, :].rearrange("p (h n) -> p h n", h=NH)

    def chunks(t):
        return t[:, :].rearrange("p (c t) -> p c t", t=S)

    X, XN, XT = tok(arena[0]), tok(arena[1]), chunks(arena[2])

    slot_sem = [nc.alloc_semaphore(f"slot{i}") for i in range(RING)]
    released = []

    def slot(p):
        s = p % RING
        return ring[:, s * PIECE:(s + 1) * PIECE]

    def landed(p):
        return (slot_sem[p % RING], 16 * (p // RING + 1))

    def cols(w, lo, n=512):
        return w.rearrange("(p c) n -> p c n", c=KC)[:, :, lo:lo + n]

    def natural(w, lo, n=512):
        return w.rearrange("(c p) n -> p c n", p=P)[:, :, lo:lo + n]

    w_in, w_out = a["w_in"][0], a["w_out"][0]
    w_kv, w_q, w_om = a["w_kv_mem"][0], a["w_q_mem"][0], a["w_o_mem"][0]
    Z_Q, Z_K, Z_VAL, Z_V, Z_U = range(5)
    first = [cols(w_in, 2 * SGU), cols(w_in, 2 * SGU + 512), cols(w_in, 2 * SGU + 1024), cols(w_in, SGU), cols(w_in, 0),
             natural(w_out, 0), natural(w_out, 512),
             cols(w_kv, 0), cols(w_kv, 512), cols(w_q, 0), cols(w_q, 512), cols(w_kv, 1024), cols(w_kv, 1536),
             natural(w_om, 0), natural(w_om, 512)]
    P_OUT, P_KM, P_QM, P_VM, P_OM = 5, 7, 9, 11, 13
    NFIRST = len(first)
    w_qkv, w_o2, w_up2, w_down2 = a["attn_w_qkv_2"][0], a["attn_w_o_2"][0], a["w_up_2"][0], a["w_down_2"][0]
    second = ([cols(w_qkv, 512 * i) for i in range(6)] + [natural(w_o2, 0), natural(w_o2, 512)]
              + [cols(w_up2, 512 * i) for i in range(DFF // 512)]
              + [w_down2.rearrange("(c p) n -> p c n", p=P)[:, 4 * i:4 * i + 4, :] for i in range(DFF // 512)])
    P_SECOND = NFIRST + 3 * NE
    P_QKV, P_O2, P_UP, P_DOWN = P_SECOND, P_SECOND + 6, P_SECOND + 8, P_SECOND + 8 + DFF // 512

    def load_piece(p, src):
        n = src.shape[2]
        SP.dma_start(slot(p).rearrange("p (c n) -> p c n", n=n), src).then_inc(slot_sem[p % RING], 16)

    def W8(p):
        return slot(p).rearrange("p (c n) -> p c n", c=KC)

    loads = {}

    def load(name, dst, src, engine=SC):
        if name not in loads:
            loads[name] = [nc.alloc_semaphore("load_" + name), 0]
        loads[name][1] += 16
        engine.dma_start(dst, src).then_inc(loads[name][0], 16)
        return (loads[name][0], loads[name][1])

    x_in = [load(f"x{h}", X[:, h, :], a["x"][0, h * P:(h + 1) * P, :], SP) for h in range(NH)]
    G_MIX, G_XQ, G_MEM, G_FFN, G_PRE2, G_FFN2 = range(6)
    for i, name in enumerate(("norm_mix", "norm_xq", "norm_mem", "norm_ffn", "norm_mix_pre_2", "norm_ffn_pre_2")):
        gains_in = load("gains", gains[:, i, :], a[name][0].rearrange("(p c) -> p c", c=KC))
    for p in range(4):
        load_piece(p, first[p])
    vv = arena[5][:, 0:1024].rearrange("p (h n) -> p h n", h=NH)
    sgu_raw = arena[6][:, 0:512].rearrange("p (g s) -> p g s", g=GROUPS)
    sgu_wT = arena[5][:, 1024:1536].rearrange("p (g t) -> p g t", g=GROUPS)
    sgu_bias = arena[6][0:1, 512:1024]
    lam_rows = arena[6][:, 1024:1024 + 4 * DQK].rearrange("p (i n) -> p i n", i=4)
    subln = small[:, 0:1]
    load("sgu", sgu_raw, a["sgu_w"][0].rearrange("g t s -> t g s"), SP)
    for half, name in enumerate(("sgu_ln_g", "sgu_ln_b")):
        load("sgu", bc[:, 512 * half:512 * (half + 1)], a[name].rearrange("l g c -> l (g c)").partition_broadcast(P)
             .rearrange("q l n -> q (l n)"), SP)
    sgu_in = load("sgu", sgu_bias, a["sgu_b"].rearrange("l g c -> l (g c)"), SP)
    for i, name in enumerate(("lambda_q1", "lambda_k1", "lambda_q2", "lambda_k2")):
        load("lambda", lam_rows[:, i, :], a[name].partition_broadcast(P).rearrange("q l n -> q (l n)"), SP)
    lam_in = load("lambda", subln, a["diff_subln"].rearrange("l (p o) -> p (l o)", o=1), SP)
    for p in range(4, RING):
        load_piece(p, first[p])

    minus_half = small[:, 8:16]
    pool_const = pool(POOL.memset(ident[:, :], 0.0))
    pool(POOL.memset(ones[:, :], 1.0))
    pool(POOL.memset(minus_half, -0.5))
    wait(POOL, pool_const)
    ident_ready = pool(POOL.affine_select(out=ident[:, :], in_=ident[:, :], compare_op=ALU.not_equal, fill=1.0,
                                          base=0, pattern=[[-1, P]], channel_multiplier=1))
    al0 = pool(POOL.iota(alibi[:, :], pattern=[[1, S]], base=-P, channel_multiplier=-1,
                         allow_small_or_imprecise_dtypes=True))
    wait(POOL, al0)
    alibi_ready = pool(POOL.affine_select(out=alibi[:, :], in_=alibi[:, :], compare_op=ALU.is_ge, fill=NEG,
                                          base=P, pattern=[[-1, S]], channel_multiplier=1))
    iota_ready = pool(POOL.iota(iota[:, :].rearrange("p (j s) -> p j s", j=JT), pattern=[[0, JT], [1, SLOTS]], base=0,
                                channel_multiplier=0, allow_small_or_imprecise_dtypes=True))

    turn = [0]

    rotating = [8]

    def next_bank():
        b = turn[0] % rotating[0]
        turn[0] += 1
        wait(PE, bank_free[b])
        return b

    def rsqrt(v, *ready):
        wait(POOL, *ready)
        return pool(POOL.tensor_tensor(v, v, minus_half[:, 0:v.shape[1]], ALU.pow))

    def inverse_rms(parts, squares, stat, *ready):
        in_psum = len(ready) and ready[0] == "psum"
        ready = ready[1:] if in_psum else ready
        wait(SC, *ready)
        q0 = act(SC.activation(squares[:, 0:512], parts[0], ACT.Square, accum_out=stat[:, 0:1]))
        if in_psum:
            q1 = act(SC.activation(squares[:, 512:1024], parts[1], ACT.Square, accum_out=stat[:, 1:2]))
            wait(DVE, q0, q1)
            v = dve(DVE.tensor_tensor(stat[:, 0:1], stat[:, 0:1], stat[:, 1:2], ALU.add))
            wait(DVE, v)
            v = dve(DVE.tensor_scalar(stat[:, 0:1], stat[:, 0:1], 1.0 / D, RMS_EPS, ALU.mult, ALU.add))
        else:
            wait(DVE, *ready)
            q1 = dve(DVE.tensor_tensor_reduce(squares[:, 512:1024], parts[1], parts[1], 1.0, D * RMS_EPS, ALU.mult,
                                              ALU.add, stat[:, 1:2]))
            wait(DVE, q0, q1)
            v = dve(DVE.tensor_scalar(stat[:, 0:1], stat[:, 0:1], stat[:, 1:2], 1.0 / D, ALU.add, ALU.mult))
        return rsqrt(stat[:, 0:1], v)

    def normalise(dst, src, col, ready):
        done = []
        for h in range(NH):
            stat = small[:, col + 2 * h:col + 2 * h + 2]
            parts = [src[:, h, 0:512], src[:, h, 512:1024]]
            sqr = dst[:, h, :] if dst is not src else XN[:, h, :]
            r = inverse_rms(parts, sqr, stat, *ready[h])
            wait(DVE, r)
            wait(SC, r)
            done.append([dve(DVE.tensor_scalar(dst[:, h, 0:512], parts[0], stat[:, 0:1], None, ALU.mult)),
                         act(SC.activation(dst[:, h, 512:1024], parts[1], ACT.Copy, scale=stat[:, 0:1]))])
        return done

    def transpose_gained(dst, src, gain, free, ready):
        s = src.rearrange("t h (p c) -> t h c p", c=KC)
        wait(PE, ident_ready)
        done = []
        for h in range(NH):
            wait(PE, *ready[h])
            steps = []
            for c4 in range(2):
                b = next_bank()
                for c in range(4):
                    last = PE.transpose(banks[b][:, c * P:(c + 1) * P], s[:, h, 4 * c4 + c, :], ident[:, :])
                t = pe(last)
                if c4:
                    wait(SC, t, gains_in, *free)
                    for c in range(4):
                        k = 4 * c4 + c
                        e = act(SC.activation(dst[:, k, h * P:(h + 1) * P], banks[b][:, c * P:(c + 1) * P], ACT.Copy,
                                              scale=gains[:, gain, k:k + 1]))
                else:
                    wait(DVE, t, gains_in, *free)
                    e = dve(DVE.tensor_tensor(dst[:, 0:4, h * P:(h + 1) * P],
                                              banks[b][:, :].rearrange("p (c t) -> p c t", c=4),
                                              gains[:, gain, 0:4].unsqueeze(2).to_broadcast([P, 4, P]), ALU.mult))
                steps.append(e)
                bank_free[b] = e
            done.append(steps)
        return done

    def both(steps):
        return [t for half in steps for t in half]

    def token_major(lhs, p, h, *ready):
        wait(PE, landed(p), *ready)
        b = next_bank()
        w = W8(p)
        for k in range(KC):
            last = PE.matmul(banks[b][:, :], lhs[:, k, h * P:(h + 1) * P], w[:, k, :], start=k == 0, stop=k == KC - 1)
        return b, pe(last)

    def transposed(rhs, p, pair, *ready):
        wait(PE, landed(p), *ready)
        b = next_bank()
        w = W8(p)
        for n in range(2):
            o = (2 * pair + n) * P
            for k in range(KC):
                last = PE.matmul(banks[b][:, n * S:(n + 1) * S], w[:, k, o:o + P], rhs[:, k, :],
                                 start=k == 0, stop=k == KC - 1)
        return b, pe(last)

    def evacuate(dst, b, step, *free, scale=1.0, func=None, on_act=True):
        if on_act:
            wait(SC, step, *free)
            bank_free[b] = act(SC.activation(dst, banks[b][:, :], func or ACT.Copy, scale=scale))
        else:
            wait(DVE, step, *free)
            bank_free[b] = dve(DVE.tensor_scalar(dst, banks[b][:, :], scale, None, ALU.mult))
        return bank_free[b]

    def release(step):
        released.append(step)
        p = len(released) - 1 + RING
        if p < NFIRST:
            wait(SP, step)
            load_piece(p, first[p])

    def attention(units, scores, soften, turn, apply, fillers):
        fillers = list(fillers)
        for u in range(units + 3):
            if u < units:
                scores(u)
                soften(u)
            if fillers:
                fillers.pop(0)()
            if 0 <= u - 2 < units:
                turn(u - 2)
            if 0 <= u - 3 < units:
                apply(u - 3)
        for f in fillers:
            f()

    NSETS = 4
    set_free = [None] * NSETS

    def scratch(u):
        i = u % NSETS
        return arena[1][:, 512 * i:512 * (i + 1)]

    def stats(u):
        i = u % NSETS
        return small[:, 48 + 8 * i:56 + 8 * i]

    scaled = normalise(XN, X, 16, [(t,) for t in x_in])
    xT = both(transpose_gained(XT, XN, G_MIX, (), scaled))

    uT = arena[3][:, 0:1024].rearrange("p (g t) -> p g t", t=S)
    v = arena[3][:, 1024:2048].rearrange("p (h n) -> p h n", h=NH)
    qT = arena[4][:, 0:1024].rearrange("p (g t) -> p g t", t=S)
    kT = arena[4][:, 1024:2048].rearrange("p (g t) -> p g t", t=S)
    for piece, dst, scale in ((Z_Q, qT, float(DQK) ** -0.5), (Z_K, kT, 1.0)):
        for pair in range(2):
            b, s = transposed(XT, piece, pair, *xT)
            qk_done = evacuate(dst[:, 2 * pair:2 * pair + 2, :].rearrange("p g t -> p (g t)"), b, s, scale=scale)
        release(s)

    lam = small[:, 40:44]
    lam_tmp = arena[6][:, 1024 + 4 * DQK:1024 + 6 * DQK].rearrange("p (i n) -> p i n", i=2)
    wait(DVE, lam_in)
    l1 = dve(DVE.tensor_tensor(lam_tmp, lam_rows[:, 0::2, :], lam_rows[:, 1::2, :], ALU.mult))
    wait(DVE, l1)
    l2 = dve(DVE.tensor_reduce(lam[:, 0:2], lam_tmp, AX, ALU.add))
    wait(SC, l2)
    l3 = act(SC.activation(lam[:, 2:4], lam[:, 0:2], ACT.Exp))
    wait(DVE, l3)
    l4 = dve(DVE.tensor_tensor(lam[:, 0:1], lam[:, 3:4], lam[:, 2:3], ALU.subtract))
    wait(DVE, l4)
    neg_lam_ready = dve(DVE.tensor_scalar(lam[:, 0:1], lam[:, 0:1], -LAMBDA_INIT, None, ALU.add))
    neg_lam = lam[:, 0:1]
    subln_ready = dve(DVE.tensor_scalar(small[:, 1:2], subln, 1.0 - LAMBDA_INIT, None, ALU.mult))

    done = {}

    def fill_values(h):
        b, s = token_major(XT, Z_VAL, h)
        done["values"] = evacuate(vv[:, h, :], b, s, on_act=False)
        if h == NH - 1:
            release(s)

    def fill_v(h):
        b, s = token_major(XT, Z_V, h)
        done["v", h] = evacuate(v[:, h, :], b, s, func=ACT.Gelu)
        if h == NH - 1:
            release(s)

    def fill_u(pair):
        b, s = transposed(XT, Z_U, pair)
        done["u"] = evacuate(uT[:, 2 * pair:2 * pair + 2, :].rearrange("p g t -> p (g t)"), b, s, func=ACT.Gelu)
        if pair:
            release(s)

    def fill_sgu_weights():
        wait(PE, sgu_in)
        b = next_bank()
        for g in range(GROUPS):
            last = PE.transpose(banks[b][:, g * P:(g + 1) * P], sgu_raw[:, g, :], ident[:, :])
        copied = evacuate(sgu_wT.rearrange("p g t -> p (g t)"), b, pe(last))
        wait(POOL, copied)
        done["sgu_w"] = pool(POOL.affine_select(out=sgu_wT, in_=sgu_wT, compare_op=ALU.is_ge, fill=0.0, base=0,
                                                pattern=[[0, GROUPS], [1, P]], channel_multiplier=-1))
        done["sgu_raw_read"] = copied

    slopes = [2.0 ** (-8.0 * (i + 1) / DH) for i in range(DH)]
    XNf = arena[1]
    xn_turned = xT
    score_step, soft_step, turn_step = {}, {}, {}
    o_sb = arena[5][:, 1536:2048].rearrange("p (h n) -> p h n", n=P)
    o_turned = [None]
    mixedT = chunks(arena[6])
    score_banks = {}

    def diff_scores(u):
        qb, h = divmod(u, DH)
        nk = (qb + 1) * P
        wait(PE, qk_done)
        score_banks[u] = [next_bank() for _ in range(2)]
        for i in range(2):
            rows = slice(i * DQK, (i + 1) * DQK)
            last = PE.matmul(banks[score_banks[u][i]][:, 0:nk], qT[rows, h, qb * P:(qb + 1) * P], kT[rows, h, 0:nk],
                             start=True, stop=True)
        score_step[u] = pe(last)

    def diff_soften(u):
        qb, h = divmod(u, DH)
        nk = (qb + 1) * P
        sc = scratch(u).rearrange("p (i k) -> p i k", i=2)[:, :, 0:nk]
        st = stats(u)
        wait(DVE, score_step[u], alibi_ready, set_free[u % NSETS], *xn_turned)
        for i in range(2):
            b = score_banks[u][i]
            t = bank_free[b] = dve(DVE.scalar_tensor_tensor(out=sc[:, i, :], in0=alibi[:, S - nk:S], scalar=slopes[h],
                                                            in1=banks[b][:, 0:nk], op0=ALU.mult, op1=ALU.add))
        wait(DVE, t)
        t = dve(DVE.tensor_reduce(st[:, 0:2], sc, AX, ALU.max))
        wait(DVE, t)
        t = dve(DVE.tensor_scalar(st[:, 2:4], st[:, 0:2], -1.0, None, ALU.mult))
        wait(SC, t)
        for i in range(2):
            t = act(SC.activation(sc[:, i, :], sc[:, i, :], ACT.Exp, bias=st[:, 2 + i:3 + i],
                                  accum_out=st[:, 4 + i:5 + i]))
        wait(DVE, t)
        t = dve(DVE.reciprocal(st[:, 6:8], st[:, 4:6]))
        wait(DVE, t, neg_lam_ready)
        t = dve(DVE.tensor_scalar(sc[:, 1, :], sc[:, 1, :], st[:, 7:8], neg_lam, ALU.mult, ALU.mult))
        wait(DVE, t)
        soft_step[u] = dve(DVE.scalar_tensor_tensor(out=sc[:, 0, :], in0=sc[:, 0, :], scalar=st[:, 6:7],
                                                    in1=sc[:, 1, :], op0=ALU.mult, op1=ALU.add))

    def diff_turn(u):
        qb, h = divmod(u, DH)
        wait(PE, soft_step[u])
        b = next_bank()
        for kb in range(qb + 1):
            last = PE.transpose(banks[b][:, kb * P:(kb + 1) * P], scratch(u)[:, kb * P:(kb + 1) * P], ident[:, :])
        t = pe(last)
        wait(SC, t)
        bank_free[b] = turn_step[u] = act(SC.activation(scratch(u)[:, 256:256 + (qb + 1) * P],
                                                        banks[b][:, 0:(qb + 1) * P], ACT.Copy))

    def diff_apply(u):
        qb, h = divmod(u, DH)
        aT = scratch(u)[:, 256:512].rearrange("p (k q) -> p k q", q=P)
        wait(PE, turn_step[u], done["values"])
        if h == 0:
            wait(PE, bank_free[7])
        for kb in range(qb + 1):
            last = PE.matmul(banks[7][:, h * P:(h + 1) * P], aT[:, kb, :], vv[:, kb, h * P:(h + 1) * P],
                             start=kb == 0, stop=kb == qb)
        set_free[u % NSETS] = pe(last)
        if h < DH - 1:
            return
        wait(SC, set_free[u % NSETS], o_turned[0])
        w1 = act(SC.activation(o_sb.rearrange("p h n -> p (h n)"), banks[7][:, :], ACT.Copy))
        osq = banks[7][:, :].rearrange("p (h n) -> p h n", n=P)
        ost = small[:, 80:84]
        wait(DVE, w1)
        w2 = dve(DVE.tensor_tensor(osq, o_sb, o_sb, ALU.mult))
        wait(DVE, w2)
        w3 = dve(DVE.tensor_reduce(ost, osq, AX, ALU.add))
        bank_free[7] = w3
        wait(DVE, w3)
        w3 = dve(DVE.tensor_scalar(ost, ost, 1.0 / P, RMS_EPS, ALU.mult, ALU.add))
        wait(DVE, rsqrt(ost, w3))
        done["o", qb] = dve(DVE.tensor_tensor(o_sb, o_sb, ost.unsqueeze(2).to_broadcast([P, DH, P]), ALU.mult))
        if qb == 0:
            diff_mix(0)

    def diff_mix(qb):
        wait(PE, done["o", qb])
        b = next_bank()
        for h in range(DH):
            last = PE.transpose(banks[b][:, h * P:(h + 1) * P], o_sb[:, h, :], ident[:, :])
        o_turned[0] = pe(last)
        wait(SC, o_turned[0], subln_ready, neg_lam_ready)
        done["diff", qb] = act(SC.activation(mixedT[:, 4:8, qb * P:(qb + 1) * P],
                                             banks[b][:, :].rearrange("p (h t) -> p h t", t=P), ACT.Copy,
                                             scale=small[:, 1:2]))
        bank_free[b] = done["diff", qb]

    vg = v.rearrange("p h (g c) -> p (h g) c", g=GROUPS)
    sq = XT.rearrange("p c t -> p (c t)")[:, 0:1024].rearrange("p (g c) -> p g c", c=P)
    mean = small[:, 24:32]
    var = small[:, 32:40]
    G8 = NH * GROUPS

    def each(t):
        return t.unsqueeze(2).to_broadcast([P, G8, P])

    def per_half(row):
        return row.unsqueeze(1).to_broadcast([P, NH, SGU])

    def sgu_norm():
        wait(DVE, done["v", 0], done["v", 1])
        n = dve(DVE.tensor_reduce(mean, vg, AX, ALU.add))
        wait(DVE, n)
        n = dve(DVE.tensor_scalar(mean, mean, 1.0 / P, None, ALU.mult))
        wait(DVE, n)
        n = dve(DVE.tensor_tensor(vg, vg, each(mean), ALU.subtract))
        wait(DVE, n, done["u"])
        n = dve(DVE.tensor_tensor(sq, vg, vg, ALU.mult))
        wait(DVE, n)
        n = dve(DVE.tensor_reduce(var, sq, AX, ALU.add))
        wait(DVE, n)
        n = dve(DVE.tensor_scalar(var, var, 1.0 / P, LN_EPS, ALU.mult, ALU.add))
        wait(DVE, rsqrt(var, n), sgu_in)
        n = dve(DVE.tensor_tensor(vg, vg, each(var), ALU.mult))
        wait(DVE, n)
        n = dve(DVE.tensor_tensor(v, v, per_half(bc[:, 0:512]), ALU.mult))
        wait(DVE, n)
        done["vn"] = dve(DVE.tensor_tensor(v, v, per_half(bc[:, 512:1024]), ALU.add))

    def last_u():
        fill_u(1)
        sgu_norm()

    rotating[0] = 7
    attention(NH * DH, diff_scores, diff_soften, diff_turn, diff_apply,
              [lambda: fill_values(0), lambda: fill_values(1), lambda: fill_v(0), lambda: fill_v(1),
               lambda: fill_u(0), last_u, fill_sgu_weights])

    mixed_sgu = []
    sp_banks = []
    wait(PE, done["vn"], done["sgu_w"], sgu_in, done["u"])
    for n in range(NH):
        b = next_bank()
        for g in range(GROUPS):
            o = banks[b][:, g * P:(g + 1) * P]
            PE.matmul(o, v[:, n, g * P:(g + 1) * P], sgu_wT[:, g, :], start=True, stop=False)
            last = PE.matmul(o, ones[0:1, :], sgu_bias[0:1, g * P:(g + 1) * P], start=False, stop=True)
        sp_banks.append((b, pe(last)))
    diff_mix(1)
    for n, (b, s) in enumerate(sp_banks):
        wait(DVE, sp_banks[-1][1], done["sgu_raw_read"])
        bank_free[b] = dve(DVE.tensor_tensor(mixedT[:, 0:4, n * P:(n + 1) * P],
                                             banks[b][:, :].rearrange("p (g t) -> p g t", g=GROUPS),
                                             uT[:, :, n * P:(n + 1) * P], ALU.mult))
        mixed_sgu.append(bank_free[b])

    rotating[0] = 8

    memX = tok(arena[3])
    wait(SC, *mixed_sgu)
    mem_in = [load(f"mem{h}", memX[:, h, :], a["mem"][0, h * P:(h + 1) * P, :]) for h in range(NH)]

    def project_out(lhs, first_piece, *ready):
        wrote = []
        for h in range(NH):
            steps = []
            for half in range(2):
                b, s = token_major(lhs, first_piece + half, h, *ready)
                wait(DVE, s)
                xs = X[:, h, 512 * half:512 * (half + 1)]
                bank_free[b] = dve(DVE.tensor_tensor(xs, banks[b][:, :], xs, ALU.add))
                steps.append(bank_free[b])
                if h == NH - 1:
                    release(s)
            wrote.append(steps)
        return wrote, s

    x1, mixed_read = project_out(mixedT, P_OUT, done["diff", 0], done["diff", 1], *mixed_sgu)

    memT = chunks(arena[4])
    scaled_m = normalise(memX, memX, 84, [(mem_in[h], *set_free) for h in range(NH)])
    memT_done = both(transpose_gained(memT, memX, G_MEM, set_free, scaled_m))
    kmT = chunks(arena[5])
    vm = tok(arena[3])

    scaled = normalise(XN, X, 16, [(*x1[h], *both(scaled_m)) for h in range(NH)])
    for j in range(2):
        for pair in range(2):
            b, s = transposed(memT, P_KM + j, pair, *memT_done)
            c = 4 * j + 2 * pair
            km_done = evacuate(kmT[:, c:c + 2, :].rearrange("p c t -> p (c t)"), b, s, *set_free, o_turned[0])
        release(s)
    xT = both(transpose_gained(XT, XN, G_XQ, (), scaled))
    qmT = chunks(arena[6])
    for j in range(2):
        for pair in range(2):
            b, s = transposed(XT, P_QM + j, pair, *xT)
            c = 4 * j + 2 * pair
            qm_done = evacuate(qmT[:, c:c + 2, :].rearrange("p c t -> p (c t)"), b, s, mixed_read)
        release(s)

    def fill_vm(j, h):
        b, s = token_major(memT, P_VM + j, h)
        done["vm", j] = evacuate(vm[:, h, 512 * j:512 * (j + 1)], b, s, *memT_done)
        if h == NH - 1:
            release(s)
        done["memT"] = s

    omT = XT
    MSCALE = float(MHD) ** -0.5
    xn_turned = xT

    def mem_scores(h):
        wait(PE, qm_done, km_done)
        b = score_banks[h] = next_bank()
        for qb in range(NH):
            for c in range(2):
                last = PE.matmul(banks[b][:, qb * M:(qb + 1) * M], qmT[:, 2 * h + c, qb * P:(qb + 1) * P],
                                 kmT[:, 2 * h + c, :], start=c == 0, stop=c == 1)
        score_step[h] = pe(last)

    def mem_soften(h):
        b = score_banks[h]
        sc = scratch(h).rearrange("p (q k) -> p q k", q=NH)
        s_ps = banks[b][:, :].rearrange("p (q k) -> p q k", q=NH)
        st = stats(h)
        wait(DVE, score_step[h])
        t = dve(DVE.tensor_reduce(st[:, 0:2], s_ps, AX, ALU.max))
        wait(DVE, t)
        t = dve(DVE.tensor_scalar(st[:, 2:4], st[:, 0:2], -MSCALE, None, ALU.mult))
        wait(SC, t, set_free[h % NSETS], *xn_turned)
        for qb in range(NH):
            t = act(SC.activation(sc[:, qb, :], s_ps[:, qb, :], ACT.Exp, bias=st[:, 2 + qb:3 + qb], scale=MSCALE,
                                  accum_out=st[:, 4 + qb:5 + qb]))
        bank_free[b] = t
        wait(DVE, t)
        t = dve(DVE.reciprocal(st[:, 6:8], st[:, 4:6]))
        wait(DVE, t)
        soft_step[h] = dve(DVE.tensor_tensor(sc, sc, st[:, 6:8].unsqueeze(2).to_broadcast([P, NH, M]), ALU.mult))

    def mem_turn(h):
        wait(PE, soft_step[h])
        b = next_bank()
        for kb in range(M // P):
            for qb in range(NH):
                o = kb * S + qb * P
                last = PE.transpose(banks[b][:, o:o + P], scratch(h)[:, qb * M + kb * P:qb * M + (kb + 1) * P],
                                    ident[:, :])
        turn_step[h] = evacuate(scratch(h), b, pe(last))

    def mem_apply(h):
        pT = scratch(h).rearrange("p (k q) -> p k q", q=S)
        wait(PE, turn_step[h], done["vm", h // 2])
        b = next_bank()
        for c in range(2):
            for kb in range(M // P):
                o = h * MHD + c * P
                last = PE.matmul(banks[b][:, c * S:(c + 1) * S], vm[:, kb, o:o + P], pT[:, kb, :],
                                 start=kb == 0, stop=kb == M // P - 1)
        set_free[h % NSETS] = pe(last)
        done["om"] = evacuate(omT[:, 2 * h:2 * h + 2, :].rearrange("p c t -> p (c t)"), b, set_free[h % NSETS],
                              qm_done, on_act=False)

    attention(MH, mem_scores, mem_soften, mem_turn, mem_apply,
              [lambda: fill_vm(0, 0), lambda: fill_vm(0, 1), lambda: fill_vm(1, 0), lambda: fill_vm(1, 1)])
    x2, om_read = project_out(omT, P_OM, done["om"])

    NR = NG + NE
    wr = arena[3][:, 0:KC * NR].rearrange("p (c n) -> p c n", c=KC)
    rb = arena[3][:, 320:320 + NR]
    wait(SC, *set_free)
    load("router", wr[:, :, 0:NG], a["w_router_group"][0].rearrange("(p c) n -> p c n", c=KC))
    load("router", wr[:, :, NG:NR], a["w_router_expert"][0].rearrange("(p c) n -> p c n", c=KC))
    load("router", rb[:, 0:NG], a["b_router_group"].partition_broadcast(P).rearrange("q l n -> q (l n)"))
    router_in = load("router", rb[:, NG:NR], a["b_router_expert"].partition_broadcast(P).rearrange("q l n -> q (l n)"))
    wait(POOL, *set_free)
    tri = arena[3][:, 384:512]
    tri0 = pool(POOL.memset(tri, 1.0))
    wait(POOL, tri0)
    tri_ready = pool(POOL.affine_select(out=tri, in_=tri, compare_op=ALU.is_gt, fill=0.0, base=0, pattern=[[1, P]],
                                        channel_multiplier=-1))
    rank = arena[3][:, 512:544]
    rank_ready = pool(POOL.iota(rank, pattern=[[-1, NE]], base=NE, channel_multiplier=0,
                                allow_small_or_imprecise_dtypes=True))

    scaled = normalise(XN, X, 16, [(*x2[h], *set_free) for h in range(NH)])
    xT = both(transpose_gained(XT, XN, G_FFN, (om_read,), scaled))
    wait(PE, router_in, *xT)
    b = next_bank()
    for h in range(NH):
        for k in range(KC):
            last = PE.matmul(banks[b][:, h * 64:h * 64 + NR], XT[:, k, h * P:(h + 1) * P], wr[:, k, :],
                             start=k == 0, stop=k == KC - 1)
    s = pe(last)
    R = arena[3]

    def tile3(at, n):
        return R[:, at:at + NH * n].rearrange("p (h n) -> p h n", h=NH)

    logits = tile3(560, NR)
    top, gate_g = tile3(640, 1), tile3(642, 1)
    eg, hot_g, pick = tile3(656, NG), tile3(664, NG), tile3(672, NG)
    el = tile3(688, EPG)
    tmp = tile3(704, NE)
    m1, m2, e2, den = tile3(768, 1), tile3(770, 1), tile3(772, 1), tile3(774, 1)
    hot1, hot2, el2 = tile3(784, EPG), tile3(800, EPG), tile3(816, EPG)
    wsel, asel = tile3(832, EPG), tile3(848, EPG)
    assigned, weight = tile3(864, NE), tile3(928, NE)

    def V(ins, *ready):
        s = dve(ins)
        wait(DVE, s)
        return s

    def wide(ap, n):
        return ap.to_broadcast([P, NH, n])

    wait(DVE, s, router_in, rank_ready)
    V(DVE.tensor_tensor(logits, banks[b][:, 0:128].rearrange("p (h n) -> p h n", h=NH)[:, :, 0:NR],
                        rb.unsqueeze(1).to_broadcast([P, NH, NR]), ALU.add))
    bank_free[b] = (dve.sem, dve.count)

    def first_max(hot, top_, src, n):
        V(DVE.tensor_reduce(top_, src, AX, ALU.max))
        V(DVE.tensor_tensor(hot, src, wide(top_, n), ALU.is_equal))
        V(DVE.tensor_tensor(hot, hot, rank[:, 0:n].unsqueeze(1).to_broadcast([P, NH, n]), ALU.mult))
        V(DVE.tensor_reduce(den, hot, AX, ALU.max))
        V(DVE.tensor_tensor(hot, hot, wide(den, n), ALU.is_equal))

    lg = logits[:, :, 0:NG]
    first_max(hot_g, top, lg, NG)
    g1 = V(DVE.tensor_tensor(eg, lg, wide(top, NG), ALU.subtract))
    wait(SC, g1)
    g2 = act(SC.activation(eg, eg, ACT.Exp))
    wait(DVE, g2)
    V(DVE.tensor_reduce(gate_g, eg, AX, ALU.add))
    V(DVE.reciprocal(gate_g, gate_g))
    for h in range(NH):
        V(DVE.tensor_tensor(tmp[:, h, :].rearrange("p (g e) -> p g e", g=NG),
                            logits[:, h, NG:NR].rearrange("p (g e) -> p g e", g=NG),
                            hot_g[:, h, :].unsqueeze(2).to_broadcast([P, NG, EPG]), ALU.mult))
        V(DVE.tensor_reduce(el[:, h, :], tmp[:, h, :].rearrange("p (g e) -> p e g", g=NG), AX, ALU.add))
    first_max(hot1, m1, el, EPG)
    V(DVE.scalar_tensor_tensor(out=el2, in0=hot1, scalar=-3.0e38, in1=el, op0=ALU.mult, op1=ALU.add))
    first_max(hot2, m2, el2, EPG)
    g3 = V(DVE.tensor_tensor(e2, m2, m1, ALU.subtract))
    wait(SC, g3)
    g4 = act(SC.activation(e2, e2, ACT.Exp))
    wait(DVE, g4)
    V(DVE.tensor_scalar(den, e2, 1.0, None, ALU.add))
    V(DVE.reciprocal(den, den))
    V(DVE.tensor_tensor(den, den, gate_g, ALU.mult))
    V(DVE.tensor_tensor(e2, e2, den, ALU.mult))
    V(DVE.tensor_tensor(wsel, hot1, wide(den, EPG), ALU.mult))
    V(DVE.tensor_tensor(el2, hot2, wide(e2, EPG), ALU.mult))
    V(DVE.tensor_tensor(wsel, wsel, el2, ALU.add))
    V(DVE.tensor_tensor(asel, hot1, hot2, ALU.add))
    for h in range(NH):
        for dst, sel in ((assigned, asel), (weight, wsel)):
            V(DVE.tensor_tensor(dst[:, h, :].rearrange("p (g e) -> p g e", g=NG),
                                sel[:, h, :].unsqueeze(1).to_broadcast([P, NG, EPG]),
                                hot_g[:, h, :].unsqueeze(2).to_broadcast([P, NG, EPG]), ALU.mult))
    V(DVE.memset(pos[:, :, NE:NE + 1], -1.0))
    V(DVE.memset(wts[:, :, NE:NE + 1], 0.0))
    weights_ready = V(DVE.tensor_copy(wts[:, :, 0:NE], weight))
    wait(PE, weights_ready, tri_ready)
    b = next_bank()
    PE.matmul(banks[b][:, 0:NE], tri, assigned[:, 0, :], start=True, stop=True)
    PE.matmul(banks[b][:, NE:2 * NE], tri, assigned[:, 1, :], start=True, stop=False)
    PE.matmul(banks[b][:, NE:2 * NE], ones[:, :], assigned[:, 0, :], start=False, stop=True)
    PE.matmul(banks[b][:, 2 * NE:3 * NE], ones[:, :], assigned[:, 0, :], start=True, stop=False)
    s = pe(PE.matmul(banks[b][:, 2 * NE:3 * NE], ones[:, :], assigned[:, 1, :], start=False, stop=True))
    wait(DVE, s)
    place = pos[:, :, 0:NE]
    V(DVE.tensor_scalar(place, banks[b][:, 0:2 * NE].rearrange("p (h n) -> p h n", h=NH), 1.0, None, ALU.add))
    V(DVE.tensor_tensor(place, place, assigned, ALU.mult))
    V(DVE.tensor_scalar(place, place, -1.0, None, ALU.add))
    V(DVE.tensor_reduce(den[:, 0, :], banks[b][:, 2 * NE:3 * NE], AX, ALU.max))
    routed = V(DVE.tensor_scalar(spill_flag[:, :], den[0:1, 0, :], float(SLOTS), None, ALU.is_gt))
    bank_free[b] = routed

    ACC = banks[0:4]
    GATH, GU, DN, MISC = banks[4:8]
    NGU = 2 * DE // JT
    NY = D // JT
    E3 = arena[3]
    ROWS = arena[4][:, 0:512]
    XTE = arena[4][:, 512:1024]
    SILU = arena[4][:, 1024:1024 + DE // JT]
    HID = arena[4][:, 1280:1280 + DE // JT]
    HT = arena[4][:, 1536:2048]
    YS = arena[5][:, 0:NY]
    ONEHOT = arena[5][:, 512:512 + 3 * NH * SLOTS].rearrange("p (j h s) -> p j h s", j=3, h=NH)
    ROUTE = arena[5][:, 1024:1024 + 3 * NH * P].rearrange("p (j h s) -> p j h s", j=3, h=NH)
    ROUTET = arena[6][:, 0:3 * NH * P].rearrange("p (j h t) -> p j h t", j=3, h=NH)
    SP_IOTA = arena[6][:, 1024:1024 + P]
    hn = XN.rearrange("t h (p c) -> t h c p", c=KC)
    gain_ffn = gains[:, G_FFN, :]
    HCH = DE // JT // P
    CPT = KC // JT

    wait(DVE, om_read)
    wait(SC, om_read)
    for b in range(8):
        wait(PE, bank_free[b])
    wait(PE, *both(x2))
    for h in range(NH):
        for j in range(2):
            last = PE.matmul(ACC[2 * h + j][:, :], ident[:, :], X[:, h, 512 * j:512 * (j + 1)], start=True, stop=True,
                             skip_group_check=True)
    residual_in = pe(last)
    wait(DVE, iota_ready)

    def build(q, e, j, places, turned):
        q.wait(DVE, "turned", turned)
        for h in range(NH):
            DVE.tensor_scalar(ONEHOT[:, j, h, :], places[:, 0:SLOTS], pos[:, h, bass.ds(e, 1)], None, ALU.is_equal)
        for h in range(NH):
            last = DVE.tensor_scalar(ROUTE[:, j, h, :], places[:, :], pos[:, h, bass.ds(e, 1)], wts[:, h, bass.ds(e, 1)],
                                     ALU.is_equal, ALU.mult)
        q.passed("built", last)

    def gather(q, n, j):
        q.wait(PE, "built", n + 1)
        q.wait(PE, "xT", n)
        for h in range(NH):
            for t in range(JT):
                last = PE.matmul(GATH[t * SLOTS:(t + 1) * SLOTS, 0:CPT * P], ONEHOT[:, j, h, :],
                                 hn[:, h, t * CPT:(t + 1) * CPT, :], start=h == 0, stop=h == NH - 1,
                                 tile_position=(0, t * SLOTS), skip_group_check=True)
        q.passed("gathered", last)

    def rows_out(q, n):
        q.wait(SC, "gathered", n + 1)
        q.wait(SC, "turned", n)
        q.passed("rows", SC.activation(ROWS[:, 0:CPT * P], GATH[:, 0:CPT * P], ACT.Copy))

    def turn_rows(q, n, j, hidden_read):
        q.wait(PE, "rows", n + 1)
        for c in range(CPT):
            PE.transpose(GATH[:, c * P:(c + 1) * P], ROWS[:, c * P:(c + 1) * P], ident[:, :])
        q.wait(PE, "routeT", n)
        q.wait(PE, "hiddenT", hidden_read)
        for h in range(NH):
            last = PE.transpose(MISC[:, h * P:(h + 1) * P], ROUTE[:, j, h, :], ident[:, :])
        q.passed("turned", last)

    def xT_out(q, n):
        q.wait(DVE, "turned", n + 1)
        for c in range(CPT):
            g = gain_ffn[:, c::CPT].unsqueeze(2).to_broadcast([P, JT, SLOTS])
            last = DVE.tensor_tensor(XTE[:, c * P:(c + 1) * P].rearrange("p (t s) -> p t s", t=JT),
                                     GATH[:, c * P:(c + 1) * P].rearrange("p (t s) -> p t s", t=JT), g, ALU.mult)
        q.passed("xT", last)

    def routeT_out(q, n, j, scattered):
        q.wait(SC, "turned", n + 1)
        q.wait(SC, "scattered", scattered)
        q.passed("routeT", SC.activation(ROUTET[:, j, :, :].rearrange("p h t -> p (h t)"), MISC[:, 0:NH * P],
                                         ACT.Copy))

    def gate_up(q, n, w):
        q.wait(PE, "xT", n + 1)
        q.wait(PE, "hidden", n)
        wgu = ring[:, w * PIECE:(w + 2) * PIECE].rearrange("p (m c n) -> p m c n", m=2, c=KC)
        for k in range(KC):
            o = (k % CPT) * P + (k // CPT) * SLOTS
            for t in range(JT):
                last = PE.matmul(GU[t * SLOTS:(t + 1) * SLOTS, 0:NGU], XTE[:, o:o + SLOTS],
                                 wgu[:, :, k, t * (DE // JT):(t + 1) * (DE // JT)], start=k == 0, stop=k == KC - 1,
                                 tile_position=(0, t * SLOTS), skip_group_check=True)
        q.passed("gate_up", last)

    def silu_out(q, n):
        q.wait(SC, "gate_up", n + 1)
        q.wait(SC, "hidden", n)
        q.passed("silu", SC.activation(SILU, GU[:, 0:DE // JT], ACT.Silu))

    def hidden_out(q, n):
        q.wait(DVE, "silu", n + 1)
        q.wait(DVE, "hidden_turned", n)
        q.passed("hidden", DVE.tensor_tensor(HID, GU[:, DE // JT:NGU], SILU, ALU.mult))

    def turn_hidden(q, n, route_read):
        q.wait(PE, "hidden", n + 1)
        q.wait(PE, "hiddenT", n)
        q.wait(PE, "routeT", route_read)
        for i in range(HCH):
            last = PE.transpose(MISC[:, 256 + i * P:256 + (i + 1) * P], HID[:, i * P:(i + 1) * P], ident[:, :])
        q.passed("hidden_turned", last)

    def hiddenT_out(q, n):
        q.wait(SC, "hidden_turned", n + 1)
        q.wait(SC, "down", n)
        q.passed("hiddenT", SC.activation(HT[:, 0:HCH * P], MISC[:, 256:256 + HCH * P], ACT.Copy))

    def down(q, n, w):
        q.wait(PE, "hiddenT", n + 1)
        q.wait(PE, "y", n)
        wd = ring[:, (w + 2) * PIECE:(w + 3) * PIECE].rearrange("p (c n) -> p c n", n=D)
        K4 = DE // P
        for k in range(K4):
            o = (k % HCH) * P + (k // HCH) * SLOTS
            for t in range(JT):
                last = PE.matmul(DN[t * SLOTS:(t + 1) * SLOTS, 0:NY], HT[:, o:o + SLOTS],
                                 wd[:, k, t * NY:(t + 1) * NY], start=k == 0, stop=k == K4 - 1,
                                 tile_position=(0, t * SLOTS), skip_group_check=True)
        q.passed("down", last)

    def y_out(q, n):
        q.wait(DVE, "down", n + 1)
        q.wait(DVE, "scattered", n)
        q.passed("y", DVE.tensor_copy(YS, DN[:, 0:NY]))

    def scatter(q, n, j, halves, signal=True):
        q.wait(PE, "y", n + 1)
        q.wait(PE, "routeT", n + 1)
        for h in halves:
            for t in range(JT):
                o = (t * NY) % 512
                last = PE.matmul(ACC[2 * h + t * NY // 512][:, o:o + NY],
                                 ROUTET[t * SLOTS:(t + 1) * SLOTS, j, h, :], YS[t * SLOTS:(t + 1) * SLOTS, :],
                                 start=False, stop=True, tile_position=(t * SLOTS, 0), skip_group_check=True)
        if signal:
            q.passed("scattered", last)

    w_gate = a["w_gate"][0].rearrange("e (p c) n -> e p (c n)", c=KC)
    w_up = a["w_up"][0].rearrange("e (p c) n -> e p (c n)", c=KC)
    w_down = a["w_down"][0].rearrange("e (c p) n -> e p c n", p=P)

    def expert_loads(e, w, sems):
        for i, src in enumerate((w_gate, w_up)):
            SP.dma_start(ring[:, (w + i) * PIECE:(w + i + 1) * PIECE],
                         src[bass.ds(e, 1), :, :].rearrange("o p n -> (o p) n")).then_inc(sems[i], 16)
        SP.dma_start(ring[:, (w + 2) * PIECE:(w + 3) * PIECE].rearrange("p (c n) -> p c n", n=D),
                     w_down[bass.ds(e, 1), :, :, :].rearrange("o p c n -> (o p) c n")).then_inc(sems[2], 16)

    def weights_of(n0, i, part):
        p = NFIRST + 3 * n0 + part
        return slot_sem[p % RING], 16 * (p // RING + 1) + 16 * i

    q = Handoffs(nc, "moe_")

    def step(n, n0, i, route_next=True, scatter_prev=True, build_next=True):
        w = (NFIRST + 3 * n0) % RING
        j = n0 % 3
        if build_next:
            build(q, n + 2, (j + 2) % 3, iota, n)
        if route_next:
            gather(q, n + 1, (j + 1) % 3)
            rows_out(q, n + 1)
        for part in (0, 1):
            PE.wait_ge(*weights_of(n0, i, part))
        gate_up(q, n, w)
        silu_out(q, n)
        hidden_out(q, n)
        if route_next:
            turn_rows(q, n + 1, (j + 1) % 3, n)
            xT_out(q, n + 1)
            routeT_out(q, n + 1, (j + 1) % 3, n - 1)
        if scatter_prev:
            scatter(q, n - 1, (j + 2) % 3, (0,), signal=False)
        turn_hidden(q, n, n + 2 if route_next else n + 1)
        hiddenT_out(q, n)
        if scatter_prev:
            scatter(q, n - 1, (j + 2) % 3, (1,))
        PE.wait_ge(*weights_of(n0, i, 2))
        down(q, n, w)
        y_out(q, n)

    def expert_stream(n, n0, *read):
        w = (NFIRST + 3 * n0) % RING
        if read:
            wait(SP, *read)
        else:
            q.wait(SP, "gate_up", n - 2)
            q.wait(SP, "down", n - 2)
        expert_loads(n, w, [slot_sem[w], slot_sem[w + 1], slot_sem[w + 2]])

    expert_stream(0, 0, *released[NFIRST - RING:NFIRST - RING + 3])
    expert_stream(1, 1, *released[NFIRST - RING + 3:NFIRST - RING + 6])
    wait(SP, *released[NFIRST - RING + 6:NFIRST - RING + 9])

    build(q, 0, 0, iota, 0)
    build(q, 1, 1, iota, 0)
    gather(q, 0, 0)
    rows_out(q, 0)
    turn_rows(q, 0, 0, 0)
    xT_out(q, 0)
    routeT_out(q, 0, 0, 0)
    step(0, 0, 0, scatter_prev=False)
    ROUNDS = (NE - 2) // 3
    assert NE == 2 + 3 * ROUNDS
    with nc.Fori(0, ROUNDS) as i:
        for j in range(3):
            expert_stream(i * 3 + (2 + j), 2 + j)
            step(i * 3 + (1 + j), 1 + j, i)
    step(NE - 1, NE - 1, 0, route_next=False, build_next=False)
    scatter(q, NE - 1, (NE - 1) % 3, (0, 1))

    engines = (PE, DVE, SC, POOL, SP)
    for engine in engines:
        wait(engine, routed)
    spill = nc.values_load(spill_flag[0:1, 0:1], min_val=0, max_val=1)
    sq = Handoffs(nc, "spill_")
    spill_sem = [nc.alloc_semaphore(f"spill_weights{i}") for i in range(3)]
    spill_iota_sem = nc.alloc_semaphore("spill_iota")
    SPILL_W = 3
    passes = S // SLOTS - 1
    with nc.If(spill > 0):
        for engine in engines:
            q.wait(engine, "scattered", NE)
        for m in range(passes):
            if m:
                sq.wait(DVE, "built", m * NE)
            DVE.tensor_scalar(SP_IOTA, iota[:, :], float(SLOTS * (m + 1)), None, ALU.add).then_inc(spill_iota_sem, 1)
            DVE.wait_ge(spill_iota_sem, m + 1)
            with nc.Fori(0, NE) as e:
                n = e + m * NE
                sq.wait(SP, "down", n)
                expert_loads(e, SPILL_W, spill_sem)
                build(sq, e, 0, SP_IOTA, n)
                gather(sq, n, 0)
                rows_out(sq, n)
                turn_rows(sq, n, 0, n)
                xT_out(sq, n)
                routeT_out(sq, n, 0, n)
                for i in (0, 1):
                    PE.wait_ge(spill_sem[i], (n + 1) * 16)
                gate_up(sq, n, SPILL_W)
                silu_out(sq, n)
                hidden_out(sq, n)
                turn_hidden(sq, n, n + 1)
                hiddenT_out(sq, n)
                PE.wait_ge(spill_sem[2], (n + 1) * 16)
                down(sq, n, SPILL_W)
                y_out(sq, n)
                scatter(sq, n, 0, (0, 1))
        for engine in engines:
            sq.wait(engine, "scattered", passes * NE)

    released2 = []

    def release2(step=None):
        released2.append(step)
        k = len(released2) - 1 + RING
        if k < len(second):
            wait(SP, step)
            load_piece(P_SECOND + k, second[k])

    for k in range(RING):
        if k % 3 == 0:
            q.wait(SP, "gate_up", NE - 2 + k // 3)
            q.wait(SP, "down", NE - 2 + k // 3)
        load_piece(P_SECOND + k, second[k])

    def gain_row(name, src, *free):
        wait(SC, *free)
        return load(name, bc[:, :], src.partition_broadcast(P).rearrange("q l n -> q (l n)"))

    final_in = gain_row("norm_final", a["norm_final"].rearrange("(l n) -> l n", l=1), done["vn"])

    def gained_rms(h, bank_of, into, gain_in, *ready):
        stat = small[:, 16 + 2 * h:18 + 2 * h]
        r = inverse_rms([banks[bank_of(h, j)][:, :] for j in range(2)], XN[:, h, :], stat, "psum", *ready)
        wait(DVE, r, gain_in)
        steps = []
        for j in range(2):
            b = bank_of(h, j)
            steps.append(dve(into(b, h, j, stat[:, 0:1])))
            bank_free[b] = steps[-1]
        return steps

    moe_out = (q.sems["scattered"], NE + q.AHEAD)

    def final_row(b, h, j, r):
        o = slice(512 * j, 512 * (j + 1))
        return DVE.scalar_tensor_tensor(out=X[:, h, o], in0=banks[b][:, :], scalar=r, in1=bc[:, o], op0=ALU.mult,
                                        op1=ALU.mult)

    x3 = [gained_rms(h, lambda h, j: 2 * h + j, final_row, final_in, moe_out) for h in range(NH)]
    for b in range(4, 8):
        bank_free[b] = x3[0][0]
    mix_post_in = gain_row("mix_post", a["norm_mix_post_2"], *both(x3))

    scaled = normalise(XN, X, 20, x3)
    xT = both(transpose_gained(XT, XN, G_PRE2, (x3[0][0],), scaled))

    q2T, k2T, v2, o2T = chunks(arena[3]), chunks(arena[4]), tok(arena[5]), chunks(arena[6])
    DH2 = D // H2
    piece = P_QKV
    for dst, scale in ((q2T, float(DH2) ** -0.5), (k2T, 1.0)):
        for j in range(2):
            for pair in range(2):
                b, s = transposed(XT, piece, pair, *xT)
                c = 4 * j + 2 * pair
                qk_done = evacuate(dst[:, c:c + 2, :].rearrange("p c t -> p (c t)"), b, s, x3[0][0], scale=scale)
            release2(s)
            piece += 1
    P_V2 = piece

    def fill_v2(j, h):
        b, s = token_major(XT, P_V2 + j, h)
        done["v2", j] = evacuate(v2[:, h, 512 * j:512 * (j + 1)], b, s, on_act=False)
        if h == NH - 1:
            release2(s)

    slopes2 = [2.0 ** (-8.0 * (i + 1) / H2) for i in range(H2)]
    xn_turned = xT

    def own_scores(h):
        wait(PE, qk_done)
        b = score_banks[h] = next_bank()
        for qb in range(NH):
            nk = (qb + 1) * P
            last = PE.matmul(banks[b][:, qb * S:qb * S + nk], q2T[:, h, qb * P:(qb + 1) * P], k2T[:, h, 0:nk],
                             start=True, stop=True)
        score_step[h] = pe(last)

    def own_soften(h):
        b = score_banks[h]
        sc = scratch(h).rearrange("p (q k) -> p q k", q=NH)
        s_ps = banks[b][:, :].rearrange("p (q k) -> p q k", q=NH)
        st = stats(h)
        wait(DVE, score_step[h], set_free[h % NSETS], *xn_turned)
        for qb in range(NH):
            nk = (qb + 1) * P
            t = dve(DVE.scalar_tensor_tensor(out=sc[:, qb, 0:nk], in0=alibi[:, S - nk:S], scalar=slopes2[h],
                                             in1=s_ps[:, qb, 0:nk], op0=ALU.mult, op1=ALU.add))
        bank_free[b] = t
        wait(DVE, t)
        for qb in range(NH):
            t = dve(DVE.tensor_reduce(st[:, qb:qb + 1], sc[:, qb, 0:(qb + 1) * P], AX, ALU.max))
        wait(DVE, t)
        t = dve(DVE.tensor_scalar(st[:, 2:4], st[:, 0:2], -1.0, None, ALU.mult))
        wait(SC, t)
        for qb in range(NH):
            nk = (qb + 1) * P
            t = act(SC.activation(sc[:, qb, 0:nk], sc[:, qb, 0:nk], ACT.Exp, bias=st[:, 2 + qb:3 + qb],
                                  accum_out=st[:, 4 + qb:5 + qb]))
        wait(DVE, t)
        t = dve(DVE.reciprocal(st[:, 6:8], st[:, 4:6]))
        wait(DVE, t)
        for qb in range(NH):
            nk = (qb + 1) * P
            soft_step[h] = dve(DVE.tensor_scalar(sc[:, qb, 0:nk], sc[:, qb, 0:nk], st[:, 6 + qb:7 + qb], None,
                                                 ALU.mult))

    def own_turn(h):
        sc = scratch(h)
        wait(PE, soft_step[h])
        b = next_bank()
        PE.transpose(banks[b][:, 0:P], sc[:, 0:P], ident[:, :])
        PE.transpose(banks[b][:, P:2 * P], sc[:, S:S + P], ident[:, :])
        t = pe(PE.transpose(banks[b][:, 2 * P:3 * P], sc[:, S + P:S + 2 * P], ident[:, :]))
        wait(SC, t)
        turn_step[h] = bank_free[b] = act(SC.activation(sc[:, 0:3 * P], banks[b][:, 0:3 * P], ACT.Copy))

    def own_apply(h):
        pT = scratch(h)
        wait(PE, turn_step[h], done["v2", h // 4])
        b = next_bank()
        hd = slice(h * DH2, (h + 1) * DH2)
        PE.matmul(banks[b][:, 0:S], v2[:, 0, hd], pT[:, 0:S], start=True, stop=False)
        set_free[h % NSETS] = pe(PE.matmul(banks[b][:, P:S], v2[:, 1, hd], pT[:, S:S + P], start=False, stop=True))
        wait(SC, set_free[h % NSETS])
        done["o2"] = bank_free[b] = act(SC.activation(o2T[:, h, :], banks[b][:, 0:S], ACT.Copy))

    attention(H2, own_scores, own_soften, own_turn, own_apply,
              [lambda: fill_v2(0, 0), lambda: fill_v2(0, 1), lambda: fill_v2(1, 0), lambda: fill_v2(1, 1)])

    def post_row(b, h, j, r):
        o = slice(512 * j, 512 * (j + 1))
        return DVE.scalar_tensor_tensor(out=XN[:, h, o], in0=banks[b][:, :], scalar=r, in1=bc[:, o], op0=ALU.mult,
                                        op1=ALU.mult)

    def post_norm(h, bank_of, gain_in, *ready):
        normed = gained_rms(h, bank_of, post_row, gain_in, *ready)
        steps = []
        for j in range(2):
            o = slice(512 * j, 512 * (j + 1))
            wait(DVE, normed[j])
            steps.append(dve(DVE.tensor_tensor(X[:, h, o], X[:, h, o], XN[:, h, o], ALU.add)))
        return steps

    used, x4 = {}, []
    for h in range(NH):
        for j in range(2):
            used[h, j], s = token_major(o2T, P_O2 + j, h, done["o2"])
            if h == NH - 1:
                release2(s)
        x4.append(post_norm(h, lambda h, j: used[h, j], mix_post_in, s, *set_free))
    o2_read = s
    ffn_post_in = gain_row("ffn_post", a["norm_ffn_post_2"], *both(x4))

    scaled = normalise(XN, X, 20, x4)
    xT = both(transpose_gained(XT, XN, G_FFN2, (), scaled))

    def hidden2(f, n=1):
        return arena[3 + f // 8][:, (f % 8) * S:(f % 8 + n) * S]

    for j in range(DFF // 512):
        for pair in range(2):
            b, s = transposed(XT, P_UP + j, pair, *xT)
            f = 4 * j + 2 * pair
            wait(SC, o2_read)
            t = evacuate(hidden2(f, 2), b, s, func=ACT.Relu)
            wait(DVE, t)
            squared = dve(DVE.tensor_tensor(hidden2(f, 2), hidden2(f, 2), hidden2(f, 2), ALU.mult))
        release2(s)
    out_banks = [next_bank() for _ in range(4)]
    wait(PE, squared)
    NDOWN = DFF // 512
    down_done = {}
    for j in range(NDOWN):
        wait(PE, landed(P_DOWN + j))
        w = slot(P_DOWN + j).rearrange("p (c n) -> p c n", n=D)
        for h in range(NH):
            for half in range(2):
                for k in range(4):
                    last = PE.matmul(banks[out_banks[2 * h + half]][:, :], hidden2(4 * j + k)[:, h * P:(h + 1) * P],
                                     w[:, k, 512 * half:512 * (half + 1)], start=j == 0 and k == 0,
                                     stop=j == NDOWN - 1 and k == 3, skip_group_check=True)
            half_done = pe(last)
            if j == NDOWN - 1:
                down_done[h] = half_done
        release2(half_done)
    x_ready = [post_norm(h, lambda h, j: out_banks[2 * h + j], ffn_post_in, down_done[h])
               for h in range(NH)]
    stored = nc.alloc_semaphore("stored")
    for h in range(NH):
        for j in range(2):
            o = slice(512 * j, 512 * (j + 1))
            wait(SP, x_ready[h][j])
            SP.dma_start(out[0, h * P:(h + 1) * P, o], X[:, h, o]).then_inc(stored, 16)
    SP.wait_ge(stored, 16 * NH * 2)


INPUTS = ("x", "mem", "norm_mix", "w_in", "sgu_ln_g", "sgu_ln_b", "sgu_w", "sgu_b", "lambda_q1", "lambda_k1",
          "lambda_q2", "lambda_k2", "diff_subln", "w_out", "norm_xq", "norm_mem", "w_q_mem", "w_kv_mem", "w_o_mem",
          "norm_ffn", "w_router_group", "b_router_group", "w_router_expert", "b_router_expert", "w_gate", "w_up",
          "w_down", "norm_final", "norm_mix_pre_2", "norm_mix_post_2", "norm_ffn_pre_2", "norm_ffn_post_2", "w_up_2",
          "w_down_2", "attn_w_qkv_2", "attn_w_o_2")


def kernel(**inputs):
    import numpy as np
    import concourse.bacc as bacc
    from concourse.bass_utils import run_bass_kernel_spmd

    nc = bacc.Bacc("TRN2", target_bir_lowering=False, num_devices=1)
    arrays, aps = {}, {}
    for name in INPUTS:
        arrays["in_" + name] = np.ascontiguousarray(inputs[name])
        aps[name] = nc.dram_tensor("in_" + name, arrays["in_" + name].shape, F32, kind="ExternalInput").ap()
    out = nc.dram_tensor("out_0", arrays["in_x"].shape, F32, kind="ExternalOutput").ap()
    build_program(nc, aps, out)
    return run_bass_kernel_spmd(nc, [arrays], core_ids=[0]).results[0]["out_0"]
```

```python
import math

import concourse.bass as bass
from concourse import mybir

F32 = mybir.dt.float32
I32 = mybir.dt.int32
F32R = mybir.dt.float32r
ALU = mybir.AluOpType
ACT = mybir.ActivationFunctionType
AX = mybir.AxisListType.X

P = 128
PIECE = 4096
RING = 9
SLOTS = 64
NEG = -1.0e30
RMS_EPS = 1e-6
LN_EPS = 1e-5


class Steps:

    def __init__(self, nc, name):
        self.sem = nc.alloc_semaphore(name)
        self.count = 0

    def __call__(self, instruction):
        self.count += 1
        instruction.then_inc(self.sem, 1)
        return (self.sem, self.count)


class Handoffs:

    AHEAD = 3

    def __init__(self, nc, prefix):
        names = ("built", "gathered", "rows", "turned", "xT", "routeT", "gate_up", "silu", "hidden",
                 "hidden_turned", "hiddenT", "down", "slot_weight", "y_high", "y", "scattered")
        self.sems = {name: nc.alloc_semaphore(prefix + name) for name in names}
        for name in names:
            nc.gpsimd.sem_inc(self.sems[name], self.AHEAD)

    def wait(self, engine, name, experts):
        engine.wait_ge(self.sems[name], experts + self.AHEAD)

    def passed(self, name, instruction):
        instruction.then_inc(self.sems[name], 1)


class LastReads(list):

    def __init__(self, n):
        super().__init__([None] * n)
        self.order = list(range(n))

    def __setitem__(self, b, step):
        super().__setitem__(b, step)
        if b in self.order:
            self.order.remove(b)
        self.order.append(b)

    def take(self, held):
        b = next(b for b in self.order if b not in held)
        self.order.remove(b)
        return b


class WeightStream:

    SIZE = PIECE // 2

    def __init__(self, nc, name, units, slots, parts, wait, act, dve):
        self.nc, self.units, self.slots, self.parts = nc, units, slots, parts
        self.wait, self.act, self.dve = wait, act, dve
        self.sems = [nc.alloc_semaphore(f"{name}_slot{i}") for i in range(len(slots))]
        self.deferred = False
        self.split, self.read = [], []

    def load(self, n):
        lanes = len(self.slots)
        if n >= len(self.units):
            return
        if n >= lanes:
            self.wait(self.nc.sync, self.split[n - lanes])
        c = self.units[n].shape[1]
        self.nc.sync.dma_start(self.slots[n % lanes].rearrange("p (c n) -> p c n", c=c),
                               self.units[n]).then_inc(self.sems[n % lanes], 16)

    def split_unit(self):
        n, lanes = len(self.split), len(self.slots)
        src = self.slots[n % lanes]
        high, low = [t[:, :] for t in self.parts[n % 2]]
        self.wait(self.nc.scalar, (self.sems[n % lanes], 16 * (n // lanes + 1)))
        if n >= 2:
            self.wait(self.nc.scalar, self.read[n - 2])
        rounded = self.act(self.nc.scalar.activation(high, src, ACT.Copy))
        self.wait(self.nc.vector, rounded)
        self.split.append(self.dve(self.nc.vector.tensor_tensor(low, src, high.bitcast(F32), ALU.subtract)))
        self.load(n + lanes)

    def split_ahead(self, now=False):
        while (now or not self.deferred) and len(self.split) < min(len(self.read) + 2, len(self.units)):
            self.split_unit()

    def next_unit(self):
        self.split_ahead(now=True)
        n = len(self.read)
        self.wait(self.nc.tensor, self.split[n])
        return self.parts[n % 2]


def build_program(nc, a, out):
    _, S, D = a["x"].shape
    NH = S // P
    KC = D // P
    M = a["mem"].shape[1]
    GROUPS, CHUNK = a["sgu_b"].shape[1:]
    SGU = GROUPS * P
    DQK = a["lambda_q1"].shape[1]
    DH = 4
    MH = 4
    MHD = D // MH
    NG = a["w_router_group"].shape[2]
    NE = a["w_router_expert"].shape[2]
    EPG = NE // NG
    DE = a["w_gate"].shape[3]
    H2 = 8
    DFF = a["w_up_2"].shape[2]
    LAMBDA_INIT = 0.8 - 0.6 * math.exp(-0.3 * 0)
    assert (S, D, M, CHUNK, DE, KC, NH) == (256, 1024, 256, 128, 512, 8, 2)
    HALF = KC // 2
    JT = P // SLOTS
    assert JT in (2, 4)

    PE, DVE, SC, POOL, SP = nc.tensor, nc.vector, nc.scalar, nc.gpsimd, nc.sync
    pe, dve, act, pool = Steps(nc, "pe_steps"), Steps(nc, "dve_steps"), Steps(nc, "act_steps"), Steps(nc, "pool_steps")
    waited = {}

    def wait(engine, *steps):
        for s in steps:
            if s is None:
                continue
            sem, value = s
            key = (id(engine), id(sem))
            if waited.get(key, 0) < value:
                engine.wait_ge(sem, value)
                waited[key] = value

    at = -(-nc.sbuf_base // 32) * 32
    ring = nc.alloc_sbuf_tensor("ring", [P, RING * PIECE], F32)
    arena = [nc.alloc_sbuf_tensor(f"arena{i}", [P, 2048], F32) for i in range(7)]
    arena_at = at + RING * PIECE * 4

    def rounded(name, n, offset):
        return nc.alloc_sbuf_tensor_at(name, [P, n], F32R, offset=offset)

    bc = nc.alloc_sbuf_tensor("gain_rows", [P, 1024], F32)
    ident = nc.alloc_sbuf_tensor("ident", [P, P], F32)
    ones = nc.alloc_sbuf_tensor("ones", [P, P], F32)
    alibi = nc.alloc_sbuf_tensor("alibi", [P, S], F32)
    iota = nc.alloc_sbuf_tensor("iota", [P, P], F32)
    gains = nc.alloc_sbuf_tensor("gains", [P, 6, KC], F32)
    small = nc.alloc_sbuf_tensor("small", [P, 128], F32)
    pos = nc.alloc_sbuf_tensor("pos", [P, NH, NE + 1], F32)
    wts = nc.alloc_sbuf_tensor("wts", [P, NH, NE + 1], F32)
    spill_flag = nc.alloc_sbuf_tensor("spill_flag", [1, 1], I32)
    banks = [nc.alloc_psum_tensor(f"bank{i}", [P, 512], F32) for i in range(8)]
    bank_free = LastReads(8)

    def tok(t):
        return t[:, :].rearrange("p (h n) -> p h n", h=NH)

    def chunks(t):
        return t[:, :].rearrange("p (c t) -> p c t", t=S)

    X, XN, XT = tok(arena[0]), tok(arena[1]), chunks(arena[2])

    slot_sem = [nc.alloc_semaphore(f"expert_slot{i}") for i in range(RING)]
    TILE = 8192

    def slot(s):
        return ring[:, s * PIECE:(s + 1) * PIECE]

    def slot_at(s):
        return at + s * PIECE * 4

    def weight_parts(name, offset):
        return [[rounded(f"{name}_{part}{i}", PIECE // 2, offset + (2 * i + k) * TILE)
                 for k, part in enumerate(("high", "low"))] for i in range(2)]

    def columns(w, i):
        return w.rearrange("(p c) n -> p c n", c=KC)[:, :, 256 * i:256 * (i + 1)]

    def half_rows(w, j):
        return [w.rearrange("(p c) n -> p c n", c=KC)[:, HALF * i:HALF * (i + 1), 512 * j:512 * (j + 1)]
                for i in range(2)]

    def row_pairs(w):
        return [w.rearrange("(c p) n -> p c n", p=P)[:, i:i + 2, :] for i in range(0, w.shape[0] // P, 2)]

    w_z, w_kv = a["w_in"][0], a["w_kv_mem"][0]
    first = [*half_rows(w_z, 1), *[columns(w_z, i) for i in (0, 1, 4, 6)], *half_rows(w_z, 4),
             *[columns(w_z, i) for i in (5, 7)], *[columns(w_kv, i) for i in range(4)], *row_pairs(a["w_out"][0]),
             *half_rows(w_kv, 2), half_rows(w_kv, 3)[0], *[columns(a["w_q_mem"][0], i) for i in range(4)],
             half_rows(w_kv, 3)[1], *row_pairs(a["w_o_mem"][0])]
    w_qkv, w_up2 = a["attn_w_qkv_2"][0], a["w_up_2"][0]
    second = [*half_rows(w_qkv, 4), *[columns(w_qkv, i) for i in (0, 4, 1, 5, 2, 6, 3, 7)], *half_rows(w_qkv, 5),
              *row_pairs(a["attn_w_o_2"][0]), *[columns(w_up2, i) for i in range(DFF // 256)],
              *row_pairs(a["w_down_2"][0])]

    def half_slots(*slots):
        return [ring[:, o:o + WeightStream.SIZE] for s_ in slots for o in (s_ * PIECE, s_ * PIECE + WeightStream.SIZE)]

    weights = WeightStream(nc, "first", first, half_slots(0, 1, 2, 6, 7, 8), weight_parts("w1", slot_at(3)), wait, act,
                           dve)
    FIRST_LANES = len(weights.slots)
    assert len(first) % FIRST_LANES == FIRST_LANES // 2
    LOW0, LOW1 = slot_at(5), slot_at(5) + TILE

    loads = {}

    def load(name, dst, src, engine=SC):
        if name not in loads:
            loads[name] = [nc.alloc_semaphore("load_" + name), 0]
        loads[name][1] += 16
        engine.dma_start(dst, src).then_inc(loads[name][0], 16)
        return (loads[name][0], loads[name][1])

    G_MIX, G_XQ, G_MEM, G_FFN, G_PRE2, G_FFN2 = range(6)

    def load_gain(load_name, i, name, engine=SC):
        return load(load_name, gains[:, i, :], a[name][0].rearrange("(p c) -> p c", c=KC), engine)

    gain_mix_in = load_gain("gain_mix", G_MIX, "norm_mix")
    x_in = [load(f"x{h}", X[:, h, :], a["x"][0, h * P:(h + 1) * P, :], SP) for h in range(NH)]
    for n in range(4):
        weights.load(n)
    vv = arena[5][:, 0:1024].rearrange("p (h n) -> p h n", h=NH)
    sgu_raw = arena[6][:, 0:512].rearrange("p (g s) -> p g s", g=GROUPS)
    sgu_wT = arena[5][:, 1024:1536].rearrange("p (g t) -> p g t", g=GROUPS)
    sgu_bias = arena[6][0:1, 512:1024]
    lam_rows = arena[6][:, 1024:1024 + 4 * DQK].rearrange("p (i n) -> p i n", i=4)
    subln = small[:, 0:1]
    load("sgu", sgu_raw, a["sgu_w"][0].rearrange("g t s -> t g s"), SP)
    for half, name in enumerate(("sgu_ln_g", "sgu_ln_b")):
        load("sgu", bc[:, 512 * half:512 * (half + 1)], a[name].rearrange("l g c -> l (g c)").partition_broadcast(P)
             .rearrange("q l n -> q (l n)"), SP)
    sgu_in = load("sgu", sgu_bias, a["sgu_b"].rearrange("l g c -> l (g c)"), SP)
    for i, name in enumerate(("lambda_q1", "lambda_k1", "lambda_q2", "lambda_k2")):
        load("lambda", lam_rows[:, i, :], a[name].partition_broadcast(P).rearrange("q l n -> q (l n)"), SP)
    lam_in = load("lambda", subln, a["diff_subln"].rearrange("l (p o) -> p (l o)", o=1), SP)
    for n in range(4, 8):
        weights.load(n)
    for i, name in ((G_XQ, "norm_xq"), (G_MEM, "norm_mem"), (G_FFN, "norm_ffn"), (G_PRE2, "norm_mix_pre_2"),
                    (G_FFN2, "norm_ffn_pre_2")):
        gains_in = load_gain("gains", i, name, SP)
    for n in range(8, FIRST_LANES):
        weights.load(n)

    minus_half = small[:, 8:16]
    pool_const = pool(POOL.memset(ident[:, :], 0.0))
    ones_ready = pool(POOL.memset(ones[:, :], 1.0))
    pool(POOL.memset(minus_half, -0.5))
    wait(POOL, pool_const)
    ident_ready = pool(POOL.affine_select(out=ident[:, :], in_=ident[:, :], compare_op=ALU.not_equal, fill=1.0,
                                          base=0, pattern=[[-1, P]], channel_multiplier=1))
    al0 = pool(POOL.iota(alibi[:, :], pattern=[[1, S]], base=-P, channel_multiplier=-1,
                         allow_small_or_imprecise_dtypes=True))
    wait(POOL, al0)
    alibi_ready = pool(POOL.affine_select(out=alibi[:, :], in_=alibi[:, :], compare_op=ALU.is_ge, fill=NEG,
                                          base=P, pattern=[[-1, S]], channel_multiplier=1))
    iota_ready = pool(POOL.iota(iota[:, :].rearrange("p (j s) -> p j s", j=JT), pattern=[[0, JT], [1, SLOTS]], base=0,
                                channel_multiplier=0, allow_small_or_imprecise_dtypes=True))

    held = set()

    def next_bank():
        b = bank_free.take(held)
        wait(PE, bank_free[b])
        return b

    def hold(*those):
        held.update(those)
        for b in those:
            assert b in bank_free.order
            wait(PE, bank_free[b])

    def give_back(*those):
        held.difference_update(those)

    ROOT_D = float(D) ** -0.5
    assert ROOT_D == 2.0 ** -5

    def rsqrt(v, *ready):
        wait(POOL, *ready)
        return pool(POOL.tensor_tensor(v, v, minus_half[:, 0:v.shape[1]], ALU.pow))

    def sum_squares(src, stat, squares, *ready):
        wait(SC, *ready)
        s = act(SC.activation(squares, src, ACT.Square, scale=ROOT_D, accum_out=stat))
        wait(DVE, *ready, s)
        return rsqrt(stat, dve(DVE.tensor_scalar(stat, stat, RMS_EPS, None, ALU.add)))

    def scale_rows(h, dst, src, stat, ready):
        wait(DVE, ready)
        wait(SC, ready)
        return [dve(DVE.tensor_scalar(dst[:, h, 0:512], src[:, h, 0:512], stat, None, ALU.mult)),
                act(SC.activation(dst[:, h, 512:1024], src[:, h, 512:1024], ACT.Copy, scale=stat))]

    def normalise(dst, src, col, ready, squares=None):
        stats_of = [small[:, col + 2 * h:col + 2 * h + 1] for h in range(NH)]
        squares = squares or [dst[:, h, :] for h in range(NH)]
        summed = []
        for h in range(NH):
            wait(SC, *ready[h])
            summed.append(act(SC.activation(squares[h], src[:, h, :], ACT.Square, scale=ROOT_D,
                                            accum_out=stats_of[h])))
        done = []
        for h in range(NH):
            r = stats_of[h]
            wait(DVE, *ready[h], summed[h])
            done.append(scale_rows(h, dst, src, r, rsqrt(r, dve(DVE.tensor_scalar(r, r, RMS_EPS, None, ALU.add)))))
        return done

    def transpose_gained(dst, src, gain, free, ready, low=None, gain_in=None, behind_first=None):
        gain_in = gain_in or gains_in
        s = src.rearrange("t h (p c) -> t h c p", c=KC)
        wait(PE, ident_ready)
        done = []
        for h in range(NH):
            wait(PE, *ready[h])
            steps = []
            for c4 in range(2):
                b = next_bank()
                for c in range(4):
                    last = PE.transpose(banks[b][:, c * P:(c + 1) * P], s[:, h, 4 * c4 + c, :], ident[:, :])
                t = pe(last)
                if low is not None:
                    wait(SC, t, gain_in, *free)
                    for c in range(4):
                        k = 4 * c4 + c
                        e = act(SC.activation(dst[:, k, h * P:(h + 1) * P], banks[b][:, c * P:(c + 1) * P], ACT.Copy,
                                              scale=gains[:, gain, k:k + 1]))
                    wait(DVE, e)
                    for c in range(4):
                        k = 4 * c4 + c
                        o = slice(h * P, (h + 1) * P)
                        e = dve(DVE.scalar_tensor_tensor(out=low[:, k, o], in0=banks[b][:, c * P:(c + 1) * P],
                                                         scalar=gains[:, gain, k:k + 1], in1=dst[:, k, o].bitcast(F32),
                                                         op0=ALU.mult, op1=ALU.subtract))
                elif c4:
                    wait(SC, t, gain_in, *free)
                    for c in range(4):
                        k = 4 * c4 + c
                        e = act(SC.activation(dst[:, k, h * P:(h + 1) * P], banks[b][:, c * P:(c + 1) * P], ACT.Copy,
                                              scale=gains[:, gain, k:k + 1]))
                else:
                    wait(DVE, t, gain_in, *free)
                    e = dve(DVE.tensor_tensor(dst[:, 0:4, h * P:(h + 1) * P],
                                              banks[b][:, :].rearrange("p (c t) -> p c t", c=4),
                                              gains[:, gain, 0:4].unsqueeze(2).to_broadcast([P, 4, P]), ALU.mult))
                steps.append(e)
                bank_free[b] = e
            done.append(steps)
            if h == 0 and behind_first:
                behind_first()
        return done

    def both(steps):
        return [t for half in steps for t in half]

    def evacuate(dst, b, step, *free, scale=1.0, func=None, on_act=True):
        if on_act:
            wait(SC, step, *free)
            bank_free[b] = act(SC.activation(dst, banks[b][:, :], func or ACT.Copy, scale=scale))
        else:
            wait(DVE, step, *free)
            bank_free[b] = dve(DVE.tensor_scalar(dst, banks[b][:, :], scale, None, ALU.mult))
        return bank_free[b]

    def split_from(bank, high, low, step, *free, scale=None):
        wait(SC, step, *free)
        wait(DVE, act(SC.activation(high, bank, ACT.Copy, scale=1.0 if scale is None else scale)))
        if scale is None:
            return dve(DVE.tensor_tensor(low, bank, high.bitcast(F32), ALU.subtract))
        return dve(DVE.scalar_tensor_tensor(out=low, in0=bank, scalar=scale, in1=high.bitcast(F32), op0=ALU.mult,
                                            op1=ALU.subtract))

    def three(out, lhs, rhs, first, last):
        (lh, ll), (rh, rl) = lhs, rhs
        PE.matmul(out, lh, rh, start=first, stop=False, skip_group_check=True)
        PE.matmul(out, lh, rl, start=False, stop=False, skip_group_check=True)
        return PE.matmul(out, ll, rh, start=False, stop=last, skip_group_check=True)

    def transposed(stream, x, ready=None):
        w = [t[:, :].rearrange("p (c n) -> p c n", c=KC) for t in stream.next_unit()]
        b = next_bank()
        for n in range(2):
            for k in range(KC):
                if ready:
                    wait(PE, ready[NH - 1][k // HALF])
                last = three(banks[b][:, n * S:(n + 1) * S], [t[:, k, n * P:(n + 1) * P] for t in w],
                             [t[:, k, :] for t in x], k == 0, k == KC - 1)
        stream.read.append(pe(last))
        return b, stream.read[-1]

    def by_rows(stream, x, out_banks, closing, n_rows, first_row, ready=None):
        w = [t[:, :].rearrange("p (c n) -> p c n", c=n_rows) for t in stream.next_unit()]
        steps = []
        for h in range(NH):
            if ready:
                wait(PE, ready[h][first_row // HALF])
            for j in range(WeightStream.SIZE // n_rows // 512):
                for c in range(n_rows):
                    f = first_row + c
                    last = three(banks[out_banks[h][j]][:, :], [t[:, f, h * P:(h + 1) * P] for t in x],
                                 [t[:, c, 512 * j:512 * (j + 1)] for t in w], f == 0,
                                 closing and c == n_rows - 1)
            steps.append(pe(last))
        stream.read.append(steps[-1])
        return steps

    open_banks = {}

    def token_major(stream, x, key, half, ready=None):
        if half == 0:
            open_banks[key] = [[next_bank()] for _ in range(NH)]
        steps = by_rows(stream, x, open_banks[key], half == 1, 4, 4 * half, ready)
        if half == 0:
            stream.split_ahead()
        return [t[0] for t in open_banks[key]], steps

    def attention(stream, units, scores, soften, turn, apply, fillers):
        stream.deferred = True
        for u in range(units + 3):
            if u < units:
                scores(u)
            if 0 <= u - 2 < units:
                turn(u - 2)
            if 0 <= u - 3 < units:
                apply(u - 3)
            if u < units:
                soften(u)
            stream.split_ahead(now=True)
            for f in fillers.get(u, ()):
                f()
        stream.deferred = False

    NSETS = 4
    set_free = [None] * NSETS

    def scratch(u):
        i = u % NSETS
        return arena[1][:, 512 * i:512 * (i + 1)]

    def stats(u):
        i = u % NSETS
        return small[:, 48 + 8 * i:56 + 8 * i]

    wait(SC, ones_ready)
    act(SC.activation(small[:, 120:121], ones[:, 0:1], ACT.Square))
    scaled = normalise(XN, X, 16, [(t,) for t in x_in])
    XTp = [chunks(rounded("hT_high", 2048, arena_at + 2 * TILE)), chunks(rounded("hT_low", 2048, LOW0))]
    h_parts = transpose_gained(XTp[0], XN, G_MIX, (), scaled, low=XTp[1], gain_in=gain_mix_in,
                               behind_first=weights.split_unit)
    xT = both(h_parts)

    uT = arena[3][:, 0:1024].rearrange("p (g t) -> p g t", t=S)
    v = arena[3][:, 1024:2048].rearrange("p (h n) -> p h n", h=NH)
    qT = arena[4][:, 0:1024].rearrange("p (g t) -> p g t", t=S)
    kT = arena[4][:, 1024:2048].rearrange("p (g t) -> p g t", t=S)
    done = {}

    def fill_qk(dst, pair, scale):
        b, s = transposed(weights, XTp)
        done["qk", pair] = evacuate(dst[:, 2 * pair:2 * pair + 2, :].rearrange("p g t -> p (g t)"), b, s, scale=scale)
        weights.split_ahead()

    def fill_values(half):
        bs, steps = token_major(weights, XTp, "values", half)
        if half:
            for h in range(NH):
                done["values"] = evacuate(vv[:, h, :], bs[h], steps[h], on_act=False)
            weights.split_ahead()

    def fill_v(half):
        bs, steps = token_major(weights, XTp, "v", half, h_parts)
        if half:
            for h in range(NH):
                done["v", h] = evacuate(v[:, h, :], bs[h], steps[h], func=ACT.Gelu)
            weights.split_ahead()

    def fill_u(pair):
        b, s = transposed(weights, XTp)
        done["u"] = evacuate(uT[:, 2 * pair:2 * pair + 2, :].rearrange("p g t -> p (g t)"), b, s, func=ACT.Gelu)
        weights.split_ahead()

    def fill_sgu_weights():
        wait(PE, sgu_in)
        b = next_bank()
        for g in range(GROUPS):
            last = PE.transpose(banks[b][:, g * P:(g + 1) * P], sgu_raw[:, g, :], ident[:, :])
        copied = evacuate(sgu_wT.rearrange("p g t -> p (g t)"), b, pe(last))
        wait(POOL, copied)
        done["sgu_w"] = pool(POOL.affine_select(out=sgu_wT, in_=sgu_wT, compare_op=ALU.is_ge, fill=0.0, base=0,
                                                pattern=[[0, GROUPS], [1, P]], channel_multiplier=-1))
        done["sgu_raw_read"] = copied

    slopes = [2.0 ** (-8.0 * (i + 1) / DH) for i in range(DH)]
    xn_turned = xT
    score_step, soft_step, turn_step = {}, {}, {}
    o_sb = [arena[5][:, o:o + 512].rearrange("p (h n) -> p h n", n=P) for o in (1536, 0)]
    O_BANKS = (6, 7)
    mixedT = [chunks(rounded("mixed_high", 2048, arena_at + 6 * TILE)), chunks(rounded("mixed_low", 2048, LOW1))]
    score_banks = {}

    def diff_scores(u):
        h, qb = divmod(u, NH)
        nk = (qb + 1) * P
        wait(PE, done["qk", h // 2])
        score_banks[u] = [next_bank() for _ in range(2)]
        for i in range(2):
            rows = slice(i * DQK, (i + 1) * DQK)
            last = PE.matmul(banks[score_banks[u][i]][:, 0:nk], qT[rows, h, qb * P:(qb + 1) * P], kT[rows, h, 0:nk],
                             start=True, stop=True)
        score_step[u] = pe(last)

    def diff_soften(u):
        h, qb = divmod(u, NH)
        nk = (qb + 1) * P
        sc = scratch(u).rearrange("p (i k) -> p i k", i=2)[:, :, 0:nk]
        st = stats(u)
        wait(DVE, score_step[u], alibi_ready, set_free[u % NSETS], *xn_turned)
        for i in range(2):
            b = score_banks[u][i]
            t = bank_free[b] = dve(DVE.scalar_tensor_tensor(out=sc[:, i, :], in0=alibi[:, S - nk:S], scalar=slopes[h],
                                                            in1=banks[b][:, 0:nk], op0=ALU.mult, op1=ALU.add))
        wait(DVE, t)
        t = dve(DVE.tensor_reduce(st[:, 0:2], sc, AX, ALU.max))
        wait(DVE, t)
        t = dve(DVE.tensor_scalar(st[:, 2:4], st[:, 0:2], -1.0, None, ALU.mult))
        wait(SC, t)
        for i in range(2):
            t = act(SC.activation(sc[:, i, :], sc[:, i, :], ACT.Exp, bias=st[:, 2 + i:3 + i],
                                  accum_out=st[:, 4 + i:5 + i]))
        wait(DVE, t)
        t = dve(DVE.reciprocal(st[:, 6:8], st[:, 4:6]))
        wait(DVE, t, neg_lam_ready)
        t = dve(DVE.tensor_scalar(sc[:, 1, :], sc[:, 1, :], st[:, 7:8], neg_lam, ALU.mult, ALU.mult))
        wait(DVE, t)
        soft_step[u] = dve(DVE.scalar_tensor_tensor(out=sc[:, 0, :], in0=sc[:, 0, :], scalar=st[:, 6:7],
                                                    in1=sc[:, 1, :], op0=ALU.mult, op1=ALU.add))

    def diff_turn(u):
        h, qb = divmod(u, NH)
        wait(PE, soft_step[u])
        b = next_bank()
        for kb in range(qb + 1):
            last = PE.transpose(banks[b][:, kb * P:(kb + 1) * P], scratch(u)[:, kb * P:(kb + 1) * P], ident[:, :])
        t = pe(last)
        wait(SC, t)
        bank_free[b] = turn_step[u] = act(SC.activation(scratch(u)[:, 256:256 + (qb + 1) * P],
                                                        banks[b][:, 0:(qb + 1) * P], ACT.Copy))

    def diff_apply(u):
        h, qb = divmod(u, NH)
        aT = scratch(u)[:, 256:512].rearrange("p (k q) -> p k q", q=P)
        wait(PE, turn_step[u], done["values"])
        for kb in range(qb + 1):
            last = PE.matmul(banks[O_BANKS[qb]][:, h * P:(h + 1) * P], aT[:, kb, :], vv[:, kb, h * P:(h + 1) * P],
                             start=kb == 0, stop=kb == qb)
        set_free[u % NSETS] = pe(last)
        if h < DH - 1:
            return
        o, bank = o_sb[qb], banks[O_BANKS[qb]]
        wait(SC, set_free[u % NSETS])
        w1 = act(SC.activation(o.rearrange("p h n -> p (h n)"), bank[:, :], ACT.Copy))
        osq = bank[:, :].rearrange("p (h n) -> p h n", n=P)
        ost = small[:, 80 + 4 * qb:84 + 4 * qb]
        wait(DVE, w1)
        w2 = dve(DVE.tensor_tensor(osq, o, o, ALU.mult))
        wait(DVE, w2)
        w3 = dve(DVE.tensor_reduce(ost, osq, AX, ALU.add))
        bank_free[O_BANKS[qb]] = w3
        wait(DVE, w3)
        w3 = dve(DVE.tensor_scalar(ost, ost, 1.0 / P, RMS_EPS, ALU.mult, ALU.add))
        wait(DVE, rsqrt(ost, w3))
        done["o", qb] = dve(DVE.tensor_tensor(o, o, ost.unsqueeze(2).to_broadcast([P, DH, P]), ALU.mult))

    def diff_mix(qb):
        wait(PE, done["o", qb])
        b = next_bank()
        for h in range(DH):
            last = PE.transpose(banks[b][:, h * P:(h + 1) * P], o_sb[qb][:, h, :], ident[:, :])
        done["o turned"] = pe(last)
        high, low = [t[:, 4:8, qb * P:(qb + 1) * P] for t in mixedT]
        done["diff", qb] = split_from(banks[b][:, :].rearrange("p (h t) -> p h t", t=P), high, low, done["o turned"],
                                      subln_ready, neg_lam_ready, done["v_read"], scale=small[:, 1:2])
        bank_free[b] = done["diff", qb]

    vg = v.rearrange("p h (g c) -> p (h g) c", g=GROUPS)
    BN, BA = DVE.BN_STATS_DIM, DVE.BN_AGGR_DIM
    G8 = NH * GROUPS
    moments = arena[6][:, 1536:1536 + G8 * BN].rearrange("p (g s) -> p g s", s=BN)
    mean_var = arena[6][:, 1664:1664 + G8 * BA].rearrange("p (g s) -> p g s", s=BA)
    var = small[:, 32:40]

    def sgu_moments():
        wait(DVE, *[done["v", h] for h in range(NH)])
        for g in range(G8):
            t = dve(DVE.bn_stats(moments[:, g, :], vg[:, g, :]))
        wait(DVE, t)
        for g in range(G8):
            t = dve(DVE.bn_aggr(mean_var[:, g, :], moments[:, g, :]))
        wait(DVE, t)
        t = dve(DVE.tensor_scalar(var, mean_var[:, :, 1], LN_EPS, None, ALU.add))
        done["var"] = rsqrt(var, t)

    def sgu_norm():
        wait(DVE, done["var"])
        for n in range(NH):
            for g in range(n * GROUPS, (n + 1) * GROUPS):
                t = dve(DVE.tensor_scalar(vg[:, g, :], vg[:, g, :], mean_var[:, g, 0:1], var[:, g:g + 1],
                                          ALU.subtract, ALU.mult))
            wait(POOL, t, sgu_in)
            t = pool(POOL.tensor_tensor(v[:, n, :], v[:, n, :], bc[:, 0:512], ALU.mult))
            wait(POOL, t)
            done["vn"] = pool(POOL.tensor_tensor(v[:, n, :], v[:, n, :], bc[:, 512:1024], ALU.add))
        done["v_read"] = (dve.sem, dve.count)

    mixed_sgu = []

    def fill_gating():
        sp_banks = []
        wait(PE, done["vn"], done["sgu_w"], sgu_in)
        for n in range(NH):
            b = next_bank()
            for g in range(GROUPS):
                o = banks[b][:, g * P:(g + 1) * P]
                PE.matmul(o, v[:, n, g * P:(g + 1) * P], sgu_wT[:, g, :], start=True, stop=False)
                last = PE.matmul(o, ones[0:1, :], sgu_bias[0:1, g * P:(g + 1) * P], start=False, stop=True)
            sp_banks.append((b, pe(last)))
        gated_at = (arena[5][:, 1536:2048], arena[6][:, 1024:1536])
        for n, (b, s) in enumerate(sp_banks):
            wait(DVE, sp_banks[-1][1], done["sgu_raw_read"], done["u"], l2)
            gated = gated_at[n].rearrange("p (g t) -> p g t", g=GROUPS)
            t = dve(DVE.tensor_tensor(gated, banks[b][:, :].rearrange("p (g t) -> p g t", g=GROUPS),
                                      uT[:, :, n * P:(n + 1) * P], ALU.mult))
            bank_free[b] = t
            mixed_sgu.append(split_from(gated, *[m[:, 0:4, n * P:(n + 1) * P] for m in mixedT], t))

    fill_v(0)
    fill_v(1)
    sgu_moments()
    fill_u(0)
    sgu_norm()
    fill_u(1)
    fill_qk(qT, 0, float(DQK) ** -0.5)
    lam = small[:, 40:44]
    lam_tmp = arena[6][:, 1024 + 4 * DQK:1024 + 6 * DQK].rearrange("p (i n) -> p i n", i=2)
    wait(DVE, lam_in)
    l1 = dve(DVE.tensor_tensor(lam_tmp, lam_rows[:, 0::2, :], lam_rows[:, 1::2, :], ALU.mult))
    wait(DVE, l1)
    l2 = dve(DVE.tensor_reduce(lam[:, 0:2], lam_tmp, AX, ALU.add))
    wait(SC, l2)
    l3 = act(SC.activation(lam[:, 2:4], lam[:, 0:2], ACT.Exp))
    wait(DVE, l3)
    l4 = dve(DVE.tensor_tensor(lam[:, 0:1], lam[:, 3:4], lam[:, 2:3], ALU.subtract))
    wait(DVE, l4)
    neg_lam_ready = dve(DVE.tensor_scalar(lam[:, 0:1], lam[:, 0:1], -LAMBDA_INIT, None, ALU.add))
    neg_lam = lam[:, 0:1]
    subln_ready = dve(DVE.tensor_scalar(small[:, 1:2], subln, 1.0 - LAMBDA_INIT, None, ALU.mult))

    fill_sgu_weights()
    fill_qk(kT, 0, 1.0)

    memX = tok(arena[3])
    memT = [chunks(rounded("memT_high", 2048, arena_at + 2 * TILE)), chunks(rounded("memT_low", 2048, LOW0))]
    kmT = chunks(arena[3])

    def load_memory():
        wait(SC, *mixed_sgu)
        for h in range(NH):
            done["mem", h] = load(f"mem{h}", memX[:, h, :], a["mem"][0, h * P:(h + 1) * P, :])

    def norm_memory():
        done["mem scaled"] = normalise(memX, memX, 88, [(done["mem", h], *mixed_sgu, done["vn"]) for h in range(NH)],
                                       squares=[arena[6][:, 1024:2048], bc[:, :]])

    def turn_memory():
        h_read = weights.read[-1]
        done["memT"] = both(transpose_gained(memT[0], memX, G_MEM, (h_read,), done["mem scaled"], low=memT[1]))

    def fill_km(pair):
        wait(PE, *done["memT"])
        b, s = transposed(weights, memT)
        done["km"] = evacuate(kmT[:, 2 * pair:2 * pair + 2, :].rearrange("p c t -> p (c t)"), b, s)
        weights.split_ahead()

    OUT = ((0, 1), (2, 3))

    def project_rows(stream, x, unit, of=4, ahead=True, ready=None):
        if unit == 0:
            hold(*OUT[0], *OUT[1])
        steps = by_rows(stream, x, OUT, unit == of - 1, 2, 2 * unit, ready)
        if ahead and unit < of - 1:
            stream.split_ahead()
        return steps

    def fill_out(unit, ahead=True):
        wait(PE, *mixed_sgu)
        project_rows(weights, mixedT, unit, ahead=ahead)

    hold(*O_BANKS)
    attention(weights, NH * DH, diff_scores, diff_soften, diff_turn, diff_apply,
              {0: [lambda: fill_values(0)], 1: [fill_gating, load_memory, lambda: fill_values(1)],
               2: [lambda: fill_qk(qT, 1, float(DQK) ** -0.5), norm_memory],
               3: [lambda: fill_qk(kT, 1, 1.0), turn_memory], 4: [lambda: fill_km(0)], 5: [lambda: fill_km(1)], 6: [lambda: fill_km(2)],
               7: [lambda: fill_km(3)], 8: [lambda: fill_out(0)]})

    def gain_row(name, src, *free):
        wait(SP, *free)
        return load(name, bc[:, :], src.partition_broadcast(P).rearrange("q l n -> q (l n)"), SP)

    final_in = gain_row("norm_final", a["norm_final"].rearrange("(l n) -> l n", l=1), done["vn"],
                        *both(done["mem scaled"]))

    def add_to_x(steps):
        wrote = []
        for h in range(NH):
            wait(DVE, steps[h])
            wrote.append([])
            for j in range(2):
                xs = X[:, h, 512 * j:512 * (j + 1)]
                bank_free[OUT[h][j]] = dve(DVE.tensor_tensor(xs, banks[OUT[h][j]][:, :], xs, ALU.add))
                wrote[h].append(bank_free[OUT[h][j]])
        give_back(*OUT[0], *OUT[1])
        return wrote

    fill_out(1, ahead=False)
    give_back(*O_BANKS)
    for qb in range(NH):
        diff_mix(qb)
    weights.split_ahead()
    for unit in (2, 3):
        out_steps = project_rows(weights, mixedT, unit, ready=[(None, done["diff", qb]) for qb in range(NH)])
    mixed_read = out_steps[-1]
    weights.split_ahead()
    x1 = add_to_x(out_steps)

    vm = tok(arena[5])
    scaled = normalise(XN, X, 16, [(*x1[h], *set_free) for h in range(NH)])
    XQ = [chunks(rounded("xqT_high", 2048, arena_at + 4 * TILE)), chunks(rounded("xqT_low", 2048, LOW1))]

    def fill_vm(j, half):
        bs, steps = token_major(weights, memT, ("vm", j), half)
        if half:
            done["vm read"] = steps[-1]
            for h in range(NH):
                done["vm", j] = evacuate(vm[:, h, 512 * j:512 * (j + 1)], bs[h], steps[h], *set_free,
                                         done["o turned"])
            weights.split_ahead()

    qmT = chunks(arena[6])

    def fill_qm(head):
        b, s = transposed(weights, XQ, xq_parts)
        done["qm", head] = evacuate(qmT[:, 2 * head:2 * head + 2, :].rearrange("p c t -> p (c t)"), b, s, mixed_read)
        weights.split_ahead()

    for half in range(2):
        fill_vm(0, half)
    xq_parts = transpose_gained(XQ[0], XN, G_XQ, (mixed_read,), scaled, low=XQ[1])
    xT = both(xq_parts)
    fill_vm(1, 0)
    fill_qm(0)
    fill_qm(1)

    omT = [chunks(rounded("omT_high", 2048, arena_at + 2 * TILE)), chunks(rounded("omT_low", 2048, LOW0))]
    MSCALE = float(MHD) ** -0.5
    xn_turned = xT

    def mem_scores(h):
        wait(PE, done["qm", h], done["km"])
        b = score_banks[h] = next_bank()
        for qb in range(NH):
            for c in range(2):
                last = PE.matmul(banks[b][:, qb * M:(qb + 1) * M], qmT[:, 2 * h + c, qb * P:(qb + 1) * P],
                                 kmT[:, 2 * h + c, :], start=c == 0, stop=c == 1)
        score_step[h] = pe(last)

    def mem_soften(h):
        b = score_banks[h]
        sc = scratch(h).rearrange("p (q k) -> p q k", q=NH)
        s_ps = banks[b][:, :].rearrange("p (q k) -> p q k", q=NH)
        st = stats(h)
        wait(DVE, score_step[h])
        t = dve(DVE.tensor_reduce(st[:, 0:2], s_ps, AX, ALU.max))
        wait(DVE, t)
        t = dve(DVE.tensor_scalar(st[:, 2:4], st[:, 0:2], -MSCALE, None, ALU.mult))
        wait(SC, t, set_free[h % NSETS], *xn_turned)
        for qb in range(NH):
            t = act(SC.activation(sc[:, qb, :], s_ps[:, qb, :], ACT.Exp, bias=st[:, 2 + qb:3 + qb], scale=MSCALE,
                                  accum_out=st[:, 4 + qb:5 + qb]))
        bank_free[b] = t
        wait(DVE, t)
        t = dve(DVE.reciprocal(st[:, 6:8], st[:, 4:6]))
        wait(DVE, t)
        soft_step[h] = dve(DVE.tensor_tensor(sc, sc, st[:, 6:8].unsqueeze(2).to_broadcast([P, NH, M]), ALU.mult))

    def mem_turn(h):
        wait(PE, soft_step[h])
        b = next_bank()
        for kb in range(M // P):
            for qb in range(NH):
                o = kb * S + qb * P
                last = PE.transpose(banks[b][:, o:o + P], scratch(h)[:, qb * M + kb * P:qb * M + (kb + 1) * P],
                                    ident[:, :])
        turn_step[h] = evacuate(scratch(h), b, pe(last))

    def mem_apply(h):
        pT = scratch(h).rearrange("p (k q) -> p k q", q=S)
        wait(PE, turn_step[h], done["vm", h // 2])
        b = next_bank()
        for c in range(2):
            for kb in range(M // P):
                o = h * MHD + c * P
                last = PE.matmul(banks[b][:, c * S:(c + 1) * S], vm[:, kb, o:o + P], pT[:, kb, :],
                                 start=kb == 0, stop=kb == M // P - 1)
        set_free[h % NSETS] = pe(last)
        done["om", h] = split_from(banks[b][:, :], *[t[:, 2 * h:2 * h + 2, :].rearrange("p c t -> p (c t)") for t in omT],
                                set_free[h % NSETS], done["vm read"])
        bank_free[b] = done["om", h]

    def fill_o_mem(unit):
        wait(PE, done["om", 1])
        project_rows(weights, omT, unit)

    attention(weights, MH, mem_scores, mem_soften, mem_turn, mem_apply,
              {0: [lambda: fill_qm(2)], 1: [lambda: fill_qm(3)], 2: [lambda: fill_vm(1, 1)],
               4: [lambda: fill_o_mem(0)], 6: [lambda: fill_o_mem(1)]})
    wait(PE, done["om", MH - 1])
    for unit in (2, 3):
        out_steps = project_rows(weights, omT, unit)
    om_read = out_steps[-1]
    x2 = add_to_x(out_steps)

    NR = NG + NE
    wr = arena[3][:, 0:KC * NR].rearrange("p (c n) -> p c n", c=KC)
    rb = arena[3][:, 320:320 + NR]
    wait(SC, *set_free)
    load("router", wr[:, :, 0:NG], a["w_router_group"][0].rearrange("(p c) n -> p c n", c=KC))
    load("router", wr[:, :, NG:NR], a["w_router_expert"][0].rearrange("(p c) n -> p c n", c=KC))
    load("router", rb[:, 0:NG], a["b_router_group"].partition_broadcast(P).rearrange("q l n -> q (l n)"))
    router_in = load("router", rb[:, NG:NR], a["b_router_expert"].partition_broadcast(P).rearrange("q l n -> q (l n)"))
    wait(POOL, *set_free)
    tri = arena[3][:, 384:512]
    tri0 = pool(POOL.memset(tri, 1.0))
    wait(POOL, tri0)
    tri_ready = pool(POOL.affine_select(out=tri, in_=tri, compare_op=ALU.is_gt, fill=0.0, base=0, pattern=[[1, P]],
                                        channel_multiplier=-1))
    rank = arena[3][:, 512:544]
    rank_ready = pool(POOL.iota(rank, pattern=[[-1, NE]], base=NE, channel_multiplier=0,
                                allow_small_or_imprecise_dtypes=True))

    scaled = normalise(XN, X, 16, [(*x2[h], *set_free) for h in range(NH)])
    t_parts = transpose_gained(XT, XN, G_FFN, (om_read,), scaled)
    wait(PE, router_in)
    held.update(range(4))
    b = next_bank()
    for h in range(NH):
        wait(PE, *t_parts[h])
        for k in range(KC):
            last = PE.matmul(banks[b][:, h * 64:h * 64 + NR], XT[:, k, h * P:(h + 1) * P], wr[:, k, :],
                             start=k == 0, stop=k == KC - 1)
    s = pe(last)
    R = arena[3]

    def tile3(at, n):
        return R[:, at:at + NH * n].rearrange("p (h n) -> p h n", h=NH)

    ACC = banks[0:4]
    wait(PE, *both(x2), *[bank_free[i] for i in range(8) if i != b])
    for h in range(NH):
        for j in range(2):
            last = PE.matmul(ACC[2 * h + j][:, :], ident[:, :], X[:, h, 512 * j:512 * (j + 1)], start=True, stop=True,
                             skip_group_check=True)
    pe(last)

    logits = tile3(560, NR)
    top, gate_g = tile3(640, 1), tile3(642, 1)
    eg, hot_g = tile3(656, NG), tile3(664, NG)
    el = tile3(688, EPG)
    tmp = tile3(704, NE)
    m1, m2, e2, den, best = [tile3(768 + 2 * i, 1) for i in range(5)]
    hot1, hot2, el2 = tile3(784, EPG), tile3(800, EPG), tile3(816, EPG)
    wsel, asel = tile3(832, EPG), tile3(848, EPG)
    assigned = tile3(864, NE)

    beside = []
    chain = {"choice": None, "weights": None}

    def V(ins):
        chain["choice"] = dve(ins)
        if beside:
            beside.pop(0)()
        wait(DVE, chain["choice"])
        return chain["choice"]

    def then(engine, steps, make):
        def emit():
            wait(engine, chain["weights"])
            chain["weights"] = steps(make())
        beside.append(emit)

    def wide(ap, n):
        return ap.to_broadcast([P, NH, n])

    wait(DVE, s, router_in, rank_ready)
    pos_fill = dve(DVE.memset(pos[:, :, NE:NE + 1], -1.0))
    wts_fill = dve(DVE.memset(wts[:, :, NE:NE + 1], 0.0))
    V(DVE.tensor_tensor(logits, banks[b][:, 0:128].rearrange("p (h n) -> p h n", h=NH)[:, :, 0:NR],
                        rb.unsqueeze(1).to_broadcast([P, NH, NR]), ALU.add))
    bank_free[b] = chain["choice"]

    def first_max(hot, top_, src, n, beside_top=None):
        V(DVE.tensor_reduce(top_, src, AX, ALU.max))
        if beside_top:
            beside_top()
        V(DVE.tensor_tensor(hot, src, wide(top_, n), ALU.is_equal))
        V(DVE.tensor_tensor(hot, hot, rank[:, 0:n].unsqueeze(1).to_broadcast([P, NH, n]), ALU.mult))
        V(DVE.tensor_reduce(best, hot, AX, ALU.max))
        V(DVE.tensor_tensor(hot, hot, wide(best, n), ALU.is_equal))

    lg = logits[:, :, 0:NG]

    def group_weight():
        then(DVE, dve, lambda: DVE.tensor_tensor(eg, lg, wide(top, NG), ALU.subtract))
        then(SC, act, lambda: SC.activation(eg, eg, ACT.Exp))
        then(DVE, dve, lambda: DVE.tensor_reduce(gate_g, eg, AX, ALU.add))
        then(DVE, dve, lambda: DVE.reciprocal(gate_g, gate_g))

    def expert_weights():
        then(DVE, dve, lambda: DVE.tensor_tensor(e2, m2, m1, ALU.subtract))
        then(SC, act, lambda: SC.activation(e2, e2, ACT.Exp))
        then(DVE, dve, lambda: DVE.tensor_scalar(den, e2, 1.0, None, ALU.add))
        then(DVE, dve, lambda: DVE.reciprocal(den, den))
        then(DVE, dve, lambda: DVE.tensor_tensor(den, den, gate_g, ALU.mult))
        then(DVE, dve, lambda: DVE.tensor_tensor(e2, e2, den, ALU.mult))

    def over_groups(dst, sel, h):
        return DVE.tensor_tensor(dst.rearrange("p (g e) -> p g e", g=NG),
                                 sel[:, h, :].unsqueeze(1).to_broadcast([P, NG, EPG]),
                                 hot_g[:, h, :].unsqueeze(2).to_broadcast([P, NG, EPG]), ALU.mult)

    first_max(hot_g, top, lg, NG, group_weight)
    for h in range(NH):
        t = dve(DVE.tensor_tensor(tmp[:, h, :].rearrange("p (g e) -> p g e", g=NG),
                                  logits[:, h, NG:NR].rearrange("p (g e) -> p g e", g=NG),
                                  hot_g[:, h, :].unsqueeze(2).to_broadcast([P, NG, EPG]), ALU.mult))
    wait(DVE, t)
    for h in range(NH):
        t = dve(DVE.tensor_reduce(el[:, h, :], tmp[:, h, :].rearrange("p (g e) -> p e g", g=NG), AX, ALU.add))
    wait(DVE, t)
    first_max(hot1, m1, el, EPG)
    V(DVE.scalar_tensor_tensor(out=el2, in0=hot1, scalar=-3.0e38, in1=el, op0=ALU.mult, op1=ALU.add))
    first_max(hot2, m2, el2, EPG, expert_weights)
    V(DVE.tensor_tensor(asel, hot1, hot2, ALU.add))
    for h in range(NH):
        chosen = dve(over_groups(assigned[:, h, :], asel, h))
    then(DVE, dve, lambda: DVE.tensor_tensor(wsel, hot1, wide(den, EPG), ALU.mult))
    then(DVE, dve, lambda: DVE.tensor_tensor(el2, hot2, wide(e2, EPG), ALU.mult))
    then(DVE, dve, lambda: DVE.tensor_tensor(wsel, wsel, el2, ALU.add))
    then(DVE, dve, lambda: over_groups(wts[:, 0, 0:NE], wsel, 0))
    then(DVE, dve, lambda: over_groups(wts[:, 1, 0:NE], wsel, 1))
    for emit in beside:
        emit()
    beside.clear()
    wait(DVE, chain["weights"], pos_fill, wts_fill)
    wait(PE, chosen, tri_ready)
    b = 5
    PE.matmul(banks[b][:, 0:NE], tri, assigned[:, 0, :], start=True, stop=True)
    PE.matmul(banks[b][:, NE:2 * NE], tri, assigned[:, 1, :], start=True, stop=False)
    PE.matmul(banks[b][:, NE:2 * NE], ones[:, :], assigned[:, 0, :], start=False, stop=True)
    PE.matmul(banks[b][:, 2 * NE:3 * NE], ones[:, :], assigned[:, 0, :], start=True, stop=False)
    s = pe(PE.matmul(banks[b][:, 2 * NE:3 * NE], ones[:, :], assigned[:, 1, :], start=False, stop=True))
    wait(DVE, s)
    place = pos[:, :, 0:NE]
    V(DVE.tensor_scalar(place, banks[b][:, 0:2 * NE].rearrange("p (h n) -> p h n", h=NH), 1.0, None, ALU.add))
    V(DVE.tensor_tensor(place, place, assigned, ALU.mult))
    V(DVE.tensor_scalar(place, place, -1.0, None, ALU.add))
    V(DVE.tensor_reduce(den[:, 0, :], banks[b][:, 2 * NE:3 * NE], AX, ALU.max))
    routed = V(DVE.tensor_scalar(spill_flag[:, :], den[0:1, 0, :], float(SLOTS), None, ALU.is_gt))
    bank_free[b] = routed

    for engine in (PE, DVE, SC):
        wait(engine, routed)
    GATH, GU, DN, MISC = banks[4:8]
    NGU = 2 * DE // JT
    NY = D // JT
    ROWS = arena[4][:, 0:512]
    XTE = arena[4][:, 512:1024]
    SILU = arena[4][:, 1024:1024 + DE // JT]
    HID = arena[4][:, 1280:1280 + DE // JT]
    HT = arena[4][:, 1536:2048]
    YS = [rounded("y_high", 512, arena_at + 5 * TILE), rounded("y_low", 512, arena_at + 3 * TILE)]
    SLOT_WEIGHT = arena[3][:, 1024:1027]
    ONEHOT = arena[5][:, 512:512 + 3 * NH * SLOTS].rearrange("p (j h s) -> p j h s", j=3, h=NH)
    ROUTE = arena[5][:, 1024:1024 + 3 * NH * P].rearrange("p (j h s) -> p j h s", j=3, h=NH)
    ROUTET = rounded("routeT", 3 * NH * P, arena_at + 6 * TILE)[:, :].rearrange("p (j h t) -> p j h t", j=3, h=NH)
    SP_IOTA = arena[6][:, 1024:1024 + P]
    hn = XN.rearrange("t h (p c) -> t h c p", c=KC)
    gain_ffn = gains[:, G_FFN, :]
    HCH = DE // JT // P
    CPT = KC // JT

    wait(DVE, om_read)
    wait(SC, om_read)
    wait(DVE, iota_ready)

    def build(q, e, j, places, turned):
        q.wait(DVE, "turned", turned)
        for h in range(NH):
            DVE.tensor_scalar(ONEHOT[:, j, h, :], places[:, 0:SLOTS], pos[:, h, bass.ds(e, 1)], None, ALU.is_equal)
        for h in range(NH):
            last = DVE.tensor_scalar(ROUTE[:, j, h, :], places[:, :], pos[:, h, bass.ds(e, 1)], wts[:, h, bass.ds(e, 1)],
                                     ALU.is_equal, ALU.mult)
        q.passed("built", last)

    def gather(q, n, j):
        q.wait(PE, "built", n + 1)
        q.wait(PE, "xT", n)
        for h in range(NH):
            for t in range(JT):
                last = PE.matmul(GATH[t * SLOTS:(t + 1) * SLOTS, 0:CPT * P], ONEHOT[:, j, h, :],
                                 hn[:, h, t * CPT:(t + 1) * CPT, :], start=h == 0, stop=h == NH - 1,
                                 tile_position=(0, t * SLOTS), skip_group_check=True)
        q.passed("gathered", last)

    def rows_out(q, n):
        q.wait(SC, "gathered", n + 1)
        q.wait(SC, "turned", n)
        q.passed("rows", SC.activation(ROWS[:, 0:CPT * P], GATH[:, 0:CPT * P], ACT.Copy))

    def turn_rows(q, n, j, hidden_read):
        q.wait(PE, "rows", n + 1)
        for c in range(CPT):
            PE.transpose(GATH[:, c * P:(c + 1) * P], ROWS[:, c * P:(c + 1) * P], ident[:, :])
        q.wait(PE, "routeT", n)
        q.wait(PE, "hiddenT", hidden_read)
        for h in range(NH):
            last = PE.transpose(MISC[:, h * P:(h + 1) * P], ROUTE[:, j, h, :], ident[:, :])
        q.passed("turned", last)

    def xT_out(q, n):
        q.wait(DVE, "turned", n + 1)
        for c in range(CPT):
            g = gain_ffn[:, c::CPT].unsqueeze(2).to_broadcast([P, JT, SLOTS])
            last = DVE.tensor_tensor(XTE[:, c * P:(c + 1) * P].rearrange("p (t s) -> p t s", t=JT),
                                     GATH[:, c * P:(c + 1) * P].rearrange("p (t s) -> p t s", t=JT), g, ALU.mult)
        q.passed("xT", last)

    def routeT_out(q, n, j, scattered):
        q.wait(DVE, "turned", n + 1)
        q.wait(DVE, "scattered", scattered)
        DVE.tensor_reduce(SLOT_WEIGHT[:, j:j + 1], MISC[:, 0:NH * P], AX, ALU.add).then_inc(q.sems["slot_weight"], 1)
        q.passed("routeT", DVE.tensor_scalar(ROUTET[:, j, :, :].rearrange("p h t -> p (h t)"), MISC[:, 0:NH * P], 0.0,
                                             None, ALU.is_gt))

    def gate_up(q, n, w):
        q.wait(PE, "xT", n + 1)
        q.wait(PE, "hidden", n)
        wgu = ring[:, w * PIECE:(w + 2) * PIECE].rearrange("p (m c n) -> p m c n", m=2, c=KC)
        for k in range(KC):
            o = (k % CPT) * P + (k // CPT) * SLOTS
            for t in range(JT):
                last = PE.matmul(GU[t * SLOTS:(t + 1) * SLOTS, 0:NGU], XTE[:, o:o + SLOTS],
                                 wgu[:, :, k, t * (DE // JT):(t + 1) * (DE // JT)], start=k == 0, stop=k == KC - 1,
                                 tile_position=(0, t * SLOTS), skip_group_check=True)
        q.passed("gate_up", last)

    def silu_out(q, n):
        q.wait(SC, "gate_up", n + 1)
        q.wait(SC, "hidden", n)
        q.passed("silu", SC.activation(SILU, GU[:, 0:DE // JT], ACT.Silu))

    def hidden_out(q, n):
        q.wait(DVE, "silu", n + 1)
        q.wait(DVE, "hidden_turned", n)
        q.passed("hidden", DVE.tensor_tensor(HID, GU[:, DE // JT:NGU], SILU, ALU.mult))

    def turn_hidden(q, n, route_read):
        q.wait(PE, "hidden", n + 1)
        q.wait(PE, "hiddenT", n)
        q.wait(PE, "routeT", route_read)
        for i in range(HCH):
            last = PE.transpose(MISC[:, 256 + i * P:256 + (i + 1) * P], HID[:, i * P:(i + 1) * P], ident[:, :])
        q.passed("hidden_turned", last)

    def hiddenT_out(q, n):
        q.wait(SC, "hidden_turned", n + 1)
        q.wait(SC, "down", n)
        q.passed("hiddenT", SC.activation(HT[:, 0:HCH * P], MISC[:, 256:256 + HCH * P], ACT.Copy))

    def down(q, n, w):
        q.wait(PE, "hiddenT", n + 1)
        q.wait(PE, "y", n)
        wd = ring[:, (w + 2) * PIECE:(w + 3) * PIECE].rearrange("p (c n) -> p c n", n=D)
        K4 = DE // P
        for k in range(K4):
            o = (k % HCH) * P + (k // HCH) * SLOTS
            for t in range(JT):
                last = PE.matmul(DN[t * SLOTS:(t + 1) * SLOTS, 0:NY], HT[:, o:o + SLOTS],
                                 wd[:, k, t * NY:(t + 1) * NY], start=k == 0, stop=k == K4 - 1,
                                 tile_position=(0, t * SLOTS), skip_group_check=True)
        q.passed("down", last)

    def y_out(q, n, j):
        q.wait(SC, "down", n + 1)
        q.wait(SC, "scattered", n)
        q.wait(SC, "slot_weight", n + 1)
        q.passed("y_high", SC.activation(YS[0][:, :], DN[:, 0:NY], ACT.Copy, scale=SLOT_WEIGHT[:, j:j + 1]))
        q.wait(DVE, "y_high", n + 1)
        q.passed("y", DVE.scalar_tensor_tensor(out=YS[1][:, :], in0=DN[:, 0:NY], scalar=SLOT_WEIGHT[:, j:j + 1],
                                               in1=YS[0][:, :].bitcast(F32), op0=ALU.mult, op1=ALU.subtract))

    def scatter(q, n, j, halves, signal=True):
        q.wait(PE, "y", n + 1)
        q.wait(PE, "routeT", n + 1)
        for h in halves:
            for t in range(JT):
                o = (t * NY) % 512
                for y in YS:
                    last = PE.matmul(ACC[2 * h + t * NY // 512][:, o:o + NY],
                                     ROUTET[t * SLOTS:(t + 1) * SLOTS, j, h, :], y[t * SLOTS:(t + 1) * SLOTS, :],
                                     start=False, stop=True, tile_position=(t * SLOTS, 0), skip_group_check=True)
        if signal:
            q.passed("scattered", last)

    w_gate = a["w_gate"][0].rearrange("e (p c) n -> e p (c n)", c=KC)
    w_up = a["w_up"][0].rearrange("e (p c) n -> e p (c n)", c=KC)
    w_down = a["w_down"][0].rearrange("e (c p) n -> e p c n", p=P)

    def expert_loads(e, w, sems, before_down=None):
        for i, src in enumerate((w_gate, w_up)):
            SP.dma_start(ring[:, (w + i) * PIECE:(w + i + 1) * PIECE],
                         src[bass.ds(e, 1), :, :].rearrange("o p n -> (o p) n")).then_inc(sems[i], 16)
        if before_down:
            before_down()
        SP.dma_start(ring[:, (w + 2) * PIECE:(w + 3) * PIECE].rearrange("p (c n) -> p c n", n=D),
                     w_down[bass.ds(e, 1), :, :, :].rearrange("o p c n -> (o p) c n")).then_inc(sems[2], 16)

    def slots_of(n):
        return (6 + 3 * n) % RING

    def weights_of(n0, i, part):
        return slot_sem[slots_of(n0) + part], 16 * (n0 // 3 + 1) + 16 * i

    q = Handoffs(nc, "moe_")

    def step(n, n0, i, route_next=True, scatter_prev=True, build_next=True):
        w = slots_of(n0)
        j = n0 % 3
        if build_next:
            build(q, n + 2, (j + 2) % 3, iota, n)
        if route_next:
            gather(q, n + 1, (j + 1) % 3)
            rows_out(q, n + 1)
        for part in (0, 1):
            PE.wait_ge(*weights_of(n0, i, part))
        gate_up(q, n, w)
        silu_out(q, n)
        hidden_out(q, n)
        if route_next:
            turn_rows(q, n + 1, (j + 1) % 3, n)
            routeT_out(q, n + 1, (j + 1) % 3, n - 1)
            xT_out(q, n + 1)
        if scatter_prev:
            scatter(q, n - 1, (j + 2) % 3, (0,), signal=False)
        turn_hidden(q, n, n + 2 if route_next else n + 1)
        hiddenT_out(q, n)
        if scatter_prev:
            scatter(q, n - 1, (j + 2) % 3, (1,))
        PE.wait_ge(*weights_of(n0, i, 2))
        down(q, n, w)
        y_out(q, n, j)

    def expert_stream(n, n0):
        w = slots_of(n0)
        q.wait(SP, "gate_up", n - 2)
        expert_loads(n, w, [slot_sem[w + i] for i in range(3)], lambda: q.wait(SP, "down", n - 2))

    for n in range(2):
        w = slots_of(n)
        for i, src in enumerate((w_gate, w_up, w_down)):
            wait(SP, weights.split[len(first) - FIRST_LANES + 2 * (3 * n + i) + 1])
            dst = ring[:, (w + i) * PIECE:(w + i + 1) * PIECE]
            SP.dma_start(dst.rearrange("p (c n) -> p c n", n=D) if src is w_down else dst,
                         src[n]).then_inc(slot_sem[w + i], 16)
    wait(SP, weights.read[-1])

    build(q, 0, 0, iota, 0)
    build(q, 1, 1, iota, 0)
    gather(q, 0, 0)
    rows_out(q, 0)
    turn_rows(q, 0, 0, 0)
    xT_out(q, 0)
    routeT_out(q, 0, 0, 0)
    step(0, 0, 0, scatter_prev=False)
    ROUNDS = (NE - 2) // 3
    assert NE == 2 + 3 * ROUNDS
    with nc.Fori(0, ROUNDS) as i:
        for j in range(3):
            expert_stream(i * 3 + (2 + j), 2 + j)
            step(i * 3 + (1 + j), 1 + j, i)
    step(NE - 1, NE - 1, 0, route_next=False, build_next=False)
    engines = (PE, DVE, SC, POOL, SP)
    for engine in engines:
        wait(engine, routed)
    spill = nc.values_load(spill_flag[0:1, 0:1], min_val=0, max_val=1)
    scatter(q, NE - 1, (NE - 1) % 3, (0, 1))

    sq = Handoffs(nc, "spill_")
    spill_sem = [nc.alloc_semaphore(f"spill_weights{i}") for i in range(3)]
    spill_iota_sem = nc.alloc_semaphore("spill_iota")
    SPILL_W = 3
    passes = S // SLOTS - 1
    with nc.If(spill > 0):
        for engine in engines:
            q.wait(engine, "scattered", NE)
        for m in range(passes):
            if m:
                sq.wait(DVE, "built", m * NE)
            DVE.tensor_scalar(SP_IOTA, iota[:, :], float(SLOTS * (m + 1)), None, ALU.add).then_inc(spill_iota_sem, 1)
            DVE.wait_ge(spill_iota_sem, m + 1)
            with nc.Fori(0, NE) as e:
                n = e + m * NE
                sq.wait(SP, "down", n)
                expert_loads(e, SPILL_W, spill_sem)
                build(sq, e, 0, SP_IOTA, n)
                gather(sq, n, 0)
                rows_out(sq, n)
                turn_rows(sq, n, 0, n)
                xT_out(sq, n)
                routeT_out(sq, n, 0, n)
                for i in (0, 1):
                    PE.wait_ge(spill_sem[i], (n + 1) * 16)
                gate_up(sq, n, SPILL_W)
                silu_out(sq, n)
                hidden_out(sq, n)
                turn_hidden(sq, n, n + 1)
                hiddenT_out(sq, n)
                PE.wait_ge(spill_sem[2], (n + 1) * 16)
                down(sq, n, SPILL_W)
                y_out(sq, n, 0)
                scatter(sq, n, 0, (0, 1))
        for engine in engines:
            sq.wait(engine, "scattered", passes * NE)

    weights = WeightStream(nc, "second", second, half_slots(3, 4, 5, 6), weight_parts("w2", slot_at(0)), wait, act, dve)
    xT_parts = [chunks(rounded("xT_high", 2048, arena_at + 2 * TILE)), chunks(rounded("xT_low", 2048, slot_at(2)))]
    o_parts = [chunks(rounded("o_high", 2048, arena_at + 6 * TILE)), chunks(rounded("o_low", 2048, slot_at(2) + TILE))]
    hidden_parts = [rounded("hidden_high", 8192, arena_at + 3 * TILE), rounded("hidden_low", 8192, slot_at(7))]
    for n in range(8):
        q.wait(SP, "gate_up", NE - 2 + n // 6)
        q.wait(SP, "down", NE - 2)
        weights.load(n)
    q.wait(SC, "gate_up", NE)
    weights.split_unit()

    def gained(into, h, bank_of, gain_in, *ready):
        stat = small[:, 16 + 2 * h:18 + 2 * h]
        wait(SC, *ready)
        wait(DVE, gain_in)
        for j in range(2):
            b = bank_of(h, j)
            o = slice(512 * j, 512 * (j + 1))
            wait(DVE, act(SC.activation(tok(arena[2])[:, h, o], banks[b][:, :], ACT.Square, scale=ROOT_D,
                                        accum_out=stat[:, j:j + 1])))
            bank_free[b] = gained_rows = dve(DVE.tensor_tensor(into[:, h, o], banks[b][:, :], bc[:, o], ALU.mult))
        return gained_rows, rsqrt(stat[:, 0:1], dve(DVE.tensor_scalar(stat[:, 0:1], stat[:, 0:1], stat[:, 1:2], RMS_EPS,
                                                                      ALU.add, ALU.add)))

    moe_out = (q.sems["scattered"], NE + q.AHEAD)
    scaled, x3 = [], []
    for h in range(NH):
        z, r, r2 = X[:, h, :], small[:, 16 + 2 * h:17 + 2 * h], small[:, 20 + h:21 + h]
        gained_rows, r_ready = gained(X, h, lambda h, j: 2 * h + j, final_in, moe_out)
        wait(SC, gained_rows)
        t = act(SC.activation(XN[:, h, :], z, ACT.Square, scale=ROOT_D, accum_out=r2))
        wait(DVE, r_ready, t)
        t = dve(DVE.tensor_scalar(r2, r2, r, r, ALU.mult, ALU.mult))
        wait(DVE, t)
        wait(DVE, rsqrt(r2, dve(DVE.tensor_scalar(r2, r2, RMS_EPS, None, ALU.add))))
        scaled.append([dve(DVE.tensor_scalar(XN[:, h, :], z, r, r2, ALU.mult, ALU.mult))])
    for h in range(NH):
        wait(SC, *scaled[h])
        x3.append([act(SC.activation(X[:, h, :], X[:, h, :], ACT.Copy, scale=small[:, 16 + 2 * h:17 + 2 * h]))])
    for b in range(4, 8):
        bank_free[b] = scaled[0][0]
    give_back(*range(4))
    mix_post_in = gain_row("mix_post", a["norm_mix_post_2"], *both(scaled))

    q.wait(SC, "scattered", NE)
    u_parts = transpose_gained(xT_parts[0], XN, G_PRE2, (moe_out,), scaled, low=xT_parts[1])
    xT = both(u_parts)

    q2T, k2T, v2 = chunks(arena[3]), chunks(arena[4]), tok(arena[5])
    DH2 = D // H2

    def fill_q2(pair):
        b, s = transposed(weights, xT_parts)
        evacuate(q2T[:, 2 * pair:2 * pair + 2, :].rearrange("p c t -> p (c t)"), b, s, scale=float(DH2) ** -0.5)
        weights.split_ahead()

    def fill_k2(pair):
        b, s = transposed(weights, xT_parts)
        done["qk2", pair] = evacuate(k2T[:, 2 * pair:2 * pair + 2, :].rearrange("p c t -> p (c t)"), b, s)
        weights.split_ahead()


    def fill_v2(j, half):
        bs, steps = token_major(weights, xT_parts, ("v2", j), half, u_parts)
        if half:
            for h in range(NH):
                done["v2", j] = evacuate(v2[:, h, 512 * j:512 * (j + 1)], bs[h], steps[h], on_act=False)
            weights.split_ahead()

    fill_v2(0, 0)
    fill_v2(0, 1)
    fill_q2(0)
    fill_k2(0)
    fill_q2(1)
    fill_k2(1)

    slopes2 = [2.0 ** (-8.0 * (i + 1) / H2) for i in range(H2)]
    xn_turned = xT

    def own_scores(h):
        wait(PE, done["qk2", h // 2])
        b = score_banks[h] = next_bank()
        for qb in range(NH):
            nk = (qb + 1) * P
            last = PE.matmul(banks[b][:, qb * S:qb * S + nk], q2T[:, h, qb * P:(qb + 1) * P], k2T[:, h, 0:nk],
                             start=True, stop=True)
        score_step[h] = pe(last)

    def own_soften(h):
        b = score_banks[h]
        sc = scratch(h).rearrange("p (q k) -> p q k", q=NH)
        s_ps = banks[b][:, :].rearrange("p (q k) -> p q k", q=NH)
        st = stats(h)
        wait(DVE, score_step[h], set_free[h % NSETS], *xn_turned)
        for qb in range(NH):
            nk = (qb + 1) * P
            t = dve(DVE.scalar_tensor_tensor(out=sc[:, qb, 0:nk], in0=alibi[:, S - nk:S], scalar=slopes2[h],
                                             in1=s_ps[:, qb, 0:nk], op0=ALU.mult, op1=ALU.add))
        bank_free[b] = t
        wait(DVE, t)
        for qb in range(NH):
            t = dve(DVE.tensor_reduce(st[:, qb:qb + 1], sc[:, qb, 0:(qb + 1) * P], AX, ALU.max))
        wait(DVE, t)
        t = dve(DVE.tensor_scalar(st[:, 2:4], st[:, 0:2], -1.0, None, ALU.mult))
        wait(SC, t)
        for qb in range(NH):
            nk = (qb + 1) * P
            t = act(SC.activation(sc[:, qb, 0:nk], sc[:, qb, 0:nk], ACT.Exp, bias=st[:, 2 + qb:3 + qb],
                                  accum_out=st[:, 4 + qb:5 + qb]))
        wait(DVE, t)
        t = dve(DVE.reciprocal(st[:, 6:8], st[:, 4:6]))
        wait(DVE, t)
        for qb in range(NH):
            nk = (qb + 1) * P
            soft_step[h] = dve(DVE.tensor_scalar(sc[:, qb, 0:nk], sc[:, qb, 0:nk], st[:, 6 + qb:7 + qb], None,
                                                 ALU.mult))

    def own_turn(h):
        sc = scratch(h)
        wait(PE, soft_step[h])
        b = next_bank()
        PE.transpose(banks[b][:, 0:P], sc[:, 0:P], ident[:, :])
        PE.transpose(banks[b][:, P:2 * P], sc[:, S:S + P], ident[:, :])
        t = pe(PE.transpose(banks[b][:, 2 * P:3 * P], sc[:, S + P:S + 2 * P], ident[:, :]))
        wait(SC, t)
        turn_step[h] = bank_free[b] = act(SC.activation(sc[:, 0:3 * P], banks[b][:, 0:3 * P], ACT.Copy))

    def own_apply(h):
        pT = scratch(h)
        wait(PE, turn_step[h], done["v2", h // 4])
        b = next_bank()
        hd = slice(h * DH2, (h + 1) * DH2)
        PE.matmul(banks[b][:, 0:S], v2[:, 0, hd], pT[:, 0:S], start=True, stop=False)
        set_free[h % NSETS] = pe(PE.matmul(banks[b][:, P:S], v2[:, 1, hd], pT[:, S:S + P], start=False, stop=True))
        done["o2", h] = bank_free[b] = split_from(banks[b][:, 0:S], *[t[:, h, :] for t in o_parts],
                                               set_free[h % NSETS])

    def fill_o2(unit):
        wait(PE, done["o2", H2 // 2 - 1])
        project_rows(weights, o_parts, unit)

    attention(weights, H2, own_scores, own_soften, own_turn, own_apply,
              {0: [lambda: fill_q2(2)], 1: [lambda: fill_k2(2)], 2: [lambda: fill_q2(3)], 3: [lambda: fill_k2(3)],
               4: [lambda: fill_v2(1, 0)], 5: [lambda: fill_v2(1, 1)], 7: [lambda: fill_o2(0)],
               10: [lambda: fill_o2(1)]})

    def add_post(h, r_ready):
        wait(DVE, r_ready)
        return [dve(DVE.scalar_tensor_tensor(out=X[:, h, o:o + 512], in0=XN[:, h, o:o + 512],
                                             scalar=small[:, 16 + 2 * h:17 + 2 * h], in1=X[:, h, o:o + 512],
                                             op0=ALU.mult, op1=ALU.add)) for o in (0, 512)]

    wait(PE, done["o2", H2 - 1])
    for unit in (2, 3):
        steps = project_rows(weights, o_parts, unit)
    pre_stat = [small[:, 20 + h:21 + h] for h in range(NH)]
    _, r_ready = gained(XN, 0, lambda h, j: OUT[h][j], mix_post_in, steps[0], *both(x3), *set_free)
    x4 = [add_post(0, r_ready)]
    _, r_ready = gained(XN, 1, lambda h, j: OUT[h][j], mix_post_in, steps[1])
    pre_ready = [sum_squares(X[:, 0, :], pre_stat[0], XN[:, 0, :], *x4[0])]
    x4.append(add_post(1, r_ready))
    scaled = [scale_rows(0, XN, X, pre_stat[0], pre_ready[0])]
    pre_ready.append(sum_squares(X[:, 1, :], pre_stat[1], XN[:, 1, :], *x4[1]))
    scaled.append(scale_rows(1, XN, X, pre_stat[1], pre_ready[1]))
    o2_read = steps[-1]
    ffn_post_in = gain_row("ffn_post", a["norm_ffn_post_2"], *both(x4))

    ffn_parts = transpose_gained(xT_parts[0], XN, G_FFN2, (), scaled, low=xT_parts[1])
    xT = both(ffn_parts)
    squared, hidden_done = [], []

    def square(b, s):
        u = len(squared) % 2
        relu, sqr = scratch(2 * u), scratch(2 * u + 1)
        wait(SC, s, o2_read, *xT, hidden_done[-1] if hidden_done else None)
        wait(DVE, act(SC.activation(relu, banks[b][:, :], ACT.Relu)))
        bank_free[b] = dve(DVE.tensor_tensor(sqr, banks[b][:, :], relu, ALU.mult))
        squared.append((sqr, bank_free[b]))

    def split_squares():
        n = len(hidden_done)
        sqr, s = squared[n]
        hidden_done.append(split_from(sqr, *[t[:, 512 * n:512 * (n + 1)] for t in hidden_parts], s))

    for f in range(DFF // 256):
        b, s = transposed(weights, xT_parts, ffn_parts)
        if f:
            split_squares()
        weights.split_ahead()
        square(b, s)
    split_squares()

    hid = [t[:, :].rearrange("p (f t) -> p f t", t=S) for t in hidden_parts]
    NF = DFF // P
    for unit in range(NF // 2):
        wait(PE, hidden_done[unit])
        steps = project_rows(weights, hid, unit, NF // 2)
    x_ready = [add_post(h, gained(XN, h, lambda h, j: OUT[h][j], ffn_post_in, steps[h])[1]) for h in range(NH)]
    stored = nc.alloc_semaphore("stored")
    for h in range(NH):
        for j in range(2):
            o = slice(512 * j, 512 * (j + 1))
            wait(SP, x_ready[h][j])
            SP.dma_start(out[0, h * P:(h + 1) * P, o], X[:, h, o]).then_inc(stored, 16)
    SP.wait_ge(stored, 16 * NH * 2)


INPUTS = ("x", "mem", "norm_mix", "w_in", "sgu_ln_g", "sgu_ln_b", "sgu_w", "sgu_b", "lambda_q1", "lambda_k1",
          "lambda_q2", "lambda_k2", "diff_subln", "w_out", "norm_xq", "norm_mem", "w_q_mem", "w_kv_mem", "w_o_mem",
          "norm_ffn", "w_router_group", "b_router_group", "w_router_expert", "b_router_expert", "w_gate", "w_up",
          "w_down", "norm_final", "norm_mix_pre_2", "norm_mix_post_2", "norm_ffn_pre_2", "norm_ffn_post_2", "w_up_2",
          "w_down_2", "attn_w_qkv_2", "attn_w_o_2")


def kernel(**inputs):
    import numpy as np
    import concourse.bacc as bacc
    from concourse.bass_utils import run_bass_kernel_spmd

    nc = bacc.Bacc("TRN2", target_bir_lowering=False, num_devices=1)
    arrays, aps = {}, {}
    for name in INPUTS:
        arrays["in_" + name] = np.ascontiguousarray(inputs[name])
        aps[name] = nc.dram_tensor("in_" + name, arrays["in_" + name].shape, F32, kind="ExternalInput").ap()
    out = nc.dram_tensor("out_0", arrays["in_x"].shape, F32, kind="ExternalOutput").ap()
    build_program(nc, aps, out)
    return run_bass_kernel_spmd(nc, [arrays], core_ids=[0]).results[0]["out_0"]
```
